# Optimizing a Trainium2 kernel written in Bass

```python
import jax, jax.numpy as jnp
from jax import lax
import numpy as np

D_MODEL = 1024
BATCH = 1
SEQ = 128
DEPTH = 2
DEC_BATCH = 1
DEC_SEQ = 512
PAST_LEN = 128

GRID_W = 64
N_EVEN = (DEPTH + 1) // 2
N_ODD = DEPTH // 2
HEAD_DIM = 64
NA_WIDTH = D_MODEL // 2
NA_HEADS = NA_WIDTH // HEAD_DIM
WIN_ROWS = 8
WIN_COLS = 16
FN_WIDTH = D_MODEL // 2
FN_GROUP_DIM = 64
FN_GROUPS = FN_WIDTH // FN_GROUP_DIM
SG_WIDTH = D_MODEL
SG_GROUPS = 4
SG_GROUP_DIM = SG_WIDTH // SG_GROUPS
CHUNK = 128
N_EXPERTS = 16
N_EXPERT_GROUPS = 4
EXPERTS_PER_GROUP = N_EXPERTS // N_EXPERT_GROUPS
TOP_K = 2
EXPERT_FF = D_MODEL // 4
EPS = 1e-6
NEG_INF = -1e30

kernel_name = "hybrid_natten_fnet_gmlp_moe_diffusion_step"

def rmsnorm(x, g):
    xf = x.astype(jnp.float32)
    y = xf * lax.rsqrt(jnp.mean(xf * xf, axis=-1, keepdims=True) + EPS)
    return (y * g.astype(jnp.float32)).astype(x.dtype)

def modulate(x, g, shift, scale):
    return rmsnorm(x, g) * (1 + scale) + shift

def ada_chunks(cond, w, b):
    m = jax.nn.silu(cond) @ w + b
    return jnp.split(m, 6, axis=-1)

def context_attention(q, k, v):
    s = jnp.einsum('bqhd,bkhd->bhqk', q, k).astype(jnp.float32) * (HEAD_DIM ** -0.5)
    p = jax.nn.softmax(s, axis=-1).astype(v.dtype)
    out = jnp.einsum('bhqk,bkhd->bqhd', p, v)
    return out.reshape(q.shape[0], q.shape[1], NA_WIDTH)

def neighbourhood_attention(q, k, v, k_ctx, v_ctx, rpb):
    B, L, H, Dh = q.shape
    rows = L // GRID_W
    wr = min(WIN_ROWS, rows)
    r = jnp.arange(rows)
    row_start = jnp.clip(r - wr // 2, 0, rows - wr)
    row_idx = row_start[:, None] + jnp.arange(wr)[None, :]
    col = jnp.arange(GRID_W)
    col_start = jnp.clip(col - WIN_COLS // 2, 0, GRID_W - WIN_COLS)
    col_valid = (col[None, :] >= col_start[:, None]) & (col[None, :] < col_start[:, None] + WIN_COLS)
    qg = q.reshape(B, rows, GRID_W, H, Dh)
    kg = k.reshape(B, rows, GRID_W, H, Dh)[:, row_idx]
    vg = v.reshape(B, rows, GRID_W, H, Dh)[:, row_idx]
    scale = HEAD_DIM ** -0.5
    s_lat = jnp.einsum('brqhd,brikhd->brhqik', qg, kg).astype(jnp.float32) * scale
    dr = row_idx - r[:, None] + (WIN_ROWS - 1)
    dc = jnp.clip(col[None, :] - col[:, None] + (WIN_COLS - 1), 0, 2 * WIN_COLS - 2)
    bias = rpb[:, dr[:, None, :, None], dc[None, :, None, :]]
    s_lat = s_lat + jnp.transpose(bias, (1, 0, 2, 3, 4)).astype(jnp.float32)[None]
    s_lat = jnp.where(col_valid[:, None, :], s_lat, NEG_INF).reshape(B, rows, H, GRID_W, wr * GRID_W)
    s_ctx = jnp.einsum('brqhd,bkhd->brhqk', qg, k_ctx).astype(jnp.float32) * scale
    p = jax.nn.softmax(jnp.concatenate([s_lat, s_ctx], axis=-1), axis=-1).astype(v.dtype)
    p_lat = p[..., :wr * GRID_W].reshape(B, rows, H, GRID_W, wr, GRID_W)
    p_ctx = p[..., wr * GRID_W:]
    out = (jnp.einsum('brhqik,brikhd->brqhd', p_lat, vg)
           + jnp.einsum('brhqk,bkhd->brqhd', p_ctx, v_ctx))
    return out.reshape(B, L, NA_WIDTH)

def fourier_mix(u):
    B, L, _ = u.shape
    uf = u.astype(jnp.float32).reshape(B, L, FN_GROUPS, FN_GROUP_DIM)
    y = jnp.fft.fft2(uf, axes=(1, 3), norm='ortho').real
    return y.reshape(B, L, FN_WIDTH).astype(u.dtype)

def spatial_gating(z, v_gain, w_s, b_s):
    B, L, _ = z.shape
    z = jax.nn.gelu(z)
    u, v = jnp.split(z, 2, axis=-1)
    v = rmsnorm(v.reshape(B, L, SG_GROUPS, SG_GROUP_DIM), v_gain.reshape(SG_GROUPS, SG_GROUP_DIM))
    vc = v.reshape(B, L // CHUNK, CHUNK, SG_GROUPS, SG_GROUP_DIM)
    s = jnp.einsum('gpq,bnqgd->bnpgd', w_s, vc) + b_s.T[:, :, None]
    return u * s.reshape(B, L, SG_WIDTH)

def moe(h, router_w, router_b, w_gate, w_up, w_down):
    B, L, D = h.shape
    t = h.reshape(B * L, D)
    scores = jax.nn.sigmoid((t @ router_w).astype(jnp.float32))
    sel = (scores + router_b.astype(jnp.float32)).reshape(-1, N_EXPERT_GROUPS, EXPERTS_PER_GROUP)
    group_score = lax.top_k(sel, TOP_K)[0].sum(-1)
    g_best = jnp.argmax(group_score, axis=-1)
    sel_in = jnp.take_along_axis(sel, g_best[:, None, None], axis=1)[:, 0]
    _, local = lax.top_k(sel_in, TOP_K)
    ids = g_best[:, None] * EXPERTS_PER_GROUP + local
    w = jnp.take_along_axis(scores, ids, axis=1)
    w = w / jnp.sum(w, axis=-1, keepdims=True)
    gates = jnp.sum(jax.nn.one_hot(ids, N_EXPERTS, dtype=jnp.float32) * w[..., None], axis=1).astype(h.dtype)
    hid = jax.nn.silu(jnp.einsum('nd,edf->nef', t, w_gate)) * jnp.einsum('nd,edf->nef', t, w_up)
    y = jnp.einsum('nef,efd->nd', hid * gates[:, :, None], w_down)
    return y.reshape(B, L, D)

def _trunk(x, cond, cache_k, cache_v, w):
    (ada_w, ada_b, norm1_g, norm2_g, na_w_in, na_w_out, q_gain, k_gain, rpb,
     sg_w_in, sg_w_out, sg_v_gain, sg_w_s, sg_b_s, router_w, router_b,
     moe_w_gate, moe_w_up, moe_w_down) = w
    is_context = cache_k is None
    ks, vs = [], []
    B, L, _ = x.shape
    for layer in range(DEPTH):
        sh1, sc1, g1, sh2, sc2, g2 = ada_chunks(cond, ada_w[layer], ada_b[layer])
        h = modulate(x, norm1_g[layer], sh1, sc1)
        if layer % 2 == 0:
            i = layer // 2
            proj = h @ na_w_in[i]
            q, k, v, u = jnp.split(proj, [NA_WIDTH, 2 * NA_WIDTH, 3 * NA_WIDTH], axis=-1)
            q = rmsnorm(q.reshape(B, L, NA_HEADS, HEAD_DIM), q_gain[i])
            k = rmsnorm(k.reshape(B, L, NA_HEADS, HEAD_DIM), k_gain[i])
            v = v.reshape(B, L, NA_HEADS, HEAD_DIM)
            if is_context:
                a = context_attention(q, k, v)
                ks.append(k)
                vs.append(v)
            else:
                a = neighbourhood_attention(q, k, v, cache_k[:, i], cache_v[:, i], rpb[i])
            mix = jnp.concatenate([a, fourier_mix(u)], axis=-1) @ na_w_out[i]
        else:
            j = layer // 2
            mix = spatial_gating(h @ sg_w_in[j], sg_v_gain[j], sg_w_s[j], sg_b_s[j]) @ sg_w_out[j]
        x = x + g1 * mix
        h = modulate(x, norm2_g[layer], sh2, sc2)
        x = x + g2 * moe(h, router_w, router_b, moe_w_gate[layer], moe_w_up[layer], moe_w_down[layer])
    return x, ks, vs

def setup_inputs(seed: int = 0) -> dict:
    key = jax.random.key(seed)
    ks = jax.random.split(key, 32)

    def nrm(k, shape, scale):
        return jax.random.normal(k, shape, jnp.float32) * scale

    D = D_MODEL
    return {
        "x_prompt": nrm(ks[0], (BATCH, SEQ, D), 1.0),
        "x_sample": nrm(ks[1], (DEC_BATCH, DEC_SEQ, D), 1.0),
        "cache_k": nrm(ks[2], (DEC_BATCH, N_EVEN, PAST_LEN, NA_HEADS, HEAD_DIM), 1.0),
        "cache_v": nrm(ks[3], (DEC_BATCH, N_EVEN, PAST_LEN, NA_HEADS, HEAD_DIM), 1.0),
        "c": nrm(ks[4], (DEC_BATCH, D), 1.0),
        "c_ctx": nrm(ks[5], (D,), 1.0),
        "ada_w": nrm(ks[6], (DEPTH, D, 6 * D), 0.5 * D ** -0.5),
        "ada_b": nrm(ks[7], (DEPTH, 6 * D), 0.02),
        "norm1_g": 1.0 + nrm(ks[8], (DEPTH, D), 0.1),
        "norm2_g": 1.0 + nrm(ks[9], (DEPTH, D), 0.1),
        "na_w_in": nrm(ks[10], (N_EVEN, D, 3 * NA_WIDTH + FN_WIDTH), D ** -0.5),
        "na_w_out": nrm(ks[11], (N_EVEN, NA_WIDTH + FN_WIDTH, D), (NA_WIDTH + FN_WIDTH) ** -0.5),
        "q_gain": 1.0 + nrm(ks[12], (N_EVEN, HEAD_DIM), 0.1),
        "k_gain": 1.0 + nrm(ks[13], (N_EVEN, HEAD_DIM), 0.1),
        "rpb": nrm(ks[14], (N_EVEN, NA_HEADS, 2 * WIN_ROWS - 1, 2 * WIN_COLS - 1), 0.1),
        "sg_w_in": nrm(ks[15], (N_ODD, D, 2 * SG_WIDTH), D ** -0.5),
        "sg_w_out": nrm(ks[16], (N_ODD, SG_WIDTH, D), SG_WIDTH ** -0.5),
        "sg_v_gain": 1.0 + nrm(ks[17], (N_ODD, SG_WIDTH), 0.1),
        "sg_w_s": nrm(ks[18], (N_ODD, SG_GROUPS, CHUNK, CHUNK), CHUNK ** -0.5),
        "sg_b_s": 1.0 + nrm(ks[19], (N_ODD, SG_GROUPS, CHUNK), 0.1),
        "router_w": nrm(ks[20], (D, N_EXPERTS), D ** -0.5),
        "router_b": nrm(ks[21], (N_EXPERTS,), 0.01),
        "moe_w_gate": nrm(ks[22], (DEPTH, N_EXPERTS, D, EXPERT_FF), D ** -0.5),
        "moe_w_up": nrm(ks[23], (DEPTH, N_EXPERTS, D, EXPERT_FF), D ** -0.5),
        "moe_w_down": nrm(ks[24], (DEPTH, N_EXPERTS, EXPERT_FF, D), EXPERT_FF ** -0.5),
    }

def reference(x_prompt, x_sample, cache_k, cache_v, c, c_ctx, ada_w, ada_b, norm1_g, norm2_g,
              na_w_in, na_w_out, q_gain, k_gain, rpb, sg_w_in, sg_w_out, sg_v_gain, sg_w_s, sg_b_s,
              router_w, router_b, moe_w_gate, moe_w_up, moe_w_down):
    w = (ada_w, ada_b, norm1_g, norm2_g, na_w_in, na_w_out, q_gain, k_gain, rpb,
         sg_w_in, sg_w_out, sg_v_gain, sg_w_s, sg_b_s, router_w, router_b,
         moe_w_gate, moe_w_up, moe_w_down)
    y_prompt, k_list, v_list = _trunk(x_prompt, c_ctx[None, None, :], None, None, w)
    k_ctx = jnp.stack(k_list, axis=1)
    v_ctx = jnp.stack(v_list, axis=1)
    y_sample, _, _ = _trunk(x_sample, c[:, None, :], cache_k, cache_v, w)
    return (y_prompt, y_sample, k_ctx, v_ctx)


_drawn_inputs = setup_inputs


def setup_inputs(seed=0):
    import zlib

    import numpy as np

    out = dict(_drawn_inputs(seed))
    spreads = {}
    factors = {'q_gain': 2.947, 'rpb': 7.827}
    for name, (base, spread) in spreads.items():
        noise = np.random.default_rng([zlib.crc32(name.encode()), seed]).standard_normal(out[name].shape)
        drawn = base * np.exp(spread * noise) if base else spread * noise
        out[name] = __import__('jax').numpy.asarray(drawn.astype(out[name].dtype))
    for name, factor in factors.items():
        out[name] = (out[name] * factor).astype(out[name].dtype)
    return out
```

```python
from contextlib import ExitStack

import numpy as np

import concourse.bass as bass
from concourse import mybir

F32 = mybir.dt.float32
I32 = mybir.dt.int32
ALU = mybir.AluOpType
ACT = mybir.ActivationFunctionType
AX = mybir.AxisListType.X

P = 128
D = 1024
DC = D // P
GRID_W, GRID_R = 64, 8
TT = 5
TOK = TT * P
HEADS, HD = 8, 64
NAW = HEADS * HD
E, EG, FF = 16, 4, 256
SG = 4
EPS = 1e-6
NEG = -1e30
MAXOV = (2 * TOK - 3) // P
NTILE = E + MAXOV
RING_BANKS = 5
ADA_N = 6 * D // 512
COLS_T = P // GRID_R
KEY_START = [0, 64, 192, 256]
BIAS_TYPE = [0, 1, 1, 2]
BAND = 256
W0 = [16, 8, 0]

UNITS = [(hp, 0, par) for hp in range(4) for par in range(2)]
UNITS += [(hp, qt, par) for hp in range(4) for qt in range(1, TT) for par in range(2)]
NCTX = HEADS


def plan_jobs():
    jobs = []

    def add(key, reader):
        jobs.append((key, reader))

    def norm_transposes(layer):
        for h in range(2):
            add(("tc", layer, h), "dve" if h else "act")
        for c in range(DC):
            add(("t", layer, c), "act" if c % 2 else "dve")

    def out_and_router(layer):
        for t in range(TT):
            for b in range(2):
                add(("o", layer, t, b), "dve")
            if t >= 1:
                for h in range(2):
                    add(("r", layer, t - 1, h), "act")
        for h in range(2):
            add(("r", layer, TT - 1, h), "act")

    norm_transposes(0)
    for blk in range(4):
        for t in range(TT):
            add(("p", 0, blk, t), "dve" if blk == 3 else "act")
    add(("fca",), "act")
    add(("fcb",), "dve")
    for m in range(4):
        add(("fa", m), "act")
        add(("fb", m), "dve")
        add(("fy", m - 1) if m else ("fcy",), "act")
    add(("fy", 3), "act")
    add(("kct",), "act")
    add(("qtc",), "dve")
    add(("ktc",), "act")
    for hp in range(4):
        add(("qt", hp), "dve")
        add(("kt", hp), "act")
    for u in range(len(UNITS)):
        add(("s", u), "act")
        if u >= 2:
            add(("pt", u - 2), "act")
    for u in range(len(UNITS) - 2, len(UNITS)):
        add(("pt", u), "act")
    out_and_router(0)
    norm_transposes(1)
    add(("ws",), "act")
    for blk in (2, 3, 0, 1):
        for t in range(TT):
            add(("p", 1, blk, t), "act")
    for t in range(TT):
        for b in range(2):
            add(("sp", t, b), "dve")
        if t >= 1:
            for h in range(2):
                add(("ut", t - 1, h), "act")
    for h in range(2):
        add(("ut", TT - 1, h), "act")
    out_and_router(1)
    return jobs


JOBS = plan_jobs()
JOB = {key: k for k, (key, _) in enumerate(JOBS)}


def build(nc, x_prompt, x_sample, cache_k, cache_v, c, c_ctx, ada_w, ada_b, norm1_g, norm2_g, na_w_in, na_w_out,
          q_gain, k_gain, rpb, sg_w_in, sg_w_out, sg_v_gain, sg_w_s, sg_b_s, router_w, router_b, moe_w_gate,
          moe_w_up, moe_w_down, dft, tables, mask, route_consts, scale_rows, y_prompt, y_sample, k_ctx, v_ctx):
    with ExitStack() as ctx:
        def sb(name, n):
            return ctx.enter_context(nc.sbuf_tensor(name, [P, n], F32))

        def sem(name):
            return ctx.enter_context(nc.semaphore(name))

        def dram(name, shape):
            return nc.dram_tensor(name, shape, F32, kind="Internal").ap()

        Xr, Hr, HTr = sb("x_res", TT * D), sb("h_tok", TT * D), sb("h_feat", DC * TOK)
        UV, RING, BZ, PS, SM = sb("uv", 10240), sb("ring", 9 * 2048), sb("bz", 6144), sb("ps", 2560), sb("small", 472)

        X = Xr[:, :].rearrange("p (t d) -> p t d", t=TT)
        H = Hr[:, :].rearrange("p (t d) -> p t d", t=TT)
        HT = HTr[:, :].rearrange("p (c n) -> p c n", c=DC)

        def block(s):
            return RING[:, 4096 * s:4096 * (s + 1)].rearrange("p (c n) -> p c n", c=DC)

        def xslot(s):
            return RING[:, 6144 * s:6144 * (s + 1)]

        at = [0]

        def small(n):
            at[0] += n
            assert at[0] <= 472
            return SM[:, at[0] - n:at[0]]

        ident = small(P)
        rw = small(DC * E).rearrange("p (c e) -> p c e", c=DC)
        mod1 = small(64).rearrange("p (l q k c) -> p l q k c", l=2, q=2, k=2)
        kgain_b = UV[:, 7500:7564]
        ss, ms, rs = small(TT), small(TT), small(TT)
        nhalf = small(1)
        gcol = small(2)
        rb = small(E)
        slot_i = small(2 * TT).bitcast(I32).rearrange("p (t s) -> p t s", t=TT)
        w12 = small(2 * TT).rearrange("p (s t) -> p s t", s=2)
        idx_i = small(NTILE).bitcast(I32)
        over_i = small(1 + MAXOV).bitcast(I32)
        bs = small(SG)

        rows = UV[0:2, 0:6 * D]
        fin = [UV[0:96, 6144 + 384 * l:6528 + 384 * l].rearrange("p (k n) -> p k n", k=3) for l in range(2)]
        cond = UV[:, 7000:7016].rearrange("p (q c) -> p q c", q=2)
        scond = UV[:, 7016:7032].rearrange("p (q c) -> p q c", q=2)
        zeros = UV[:, 8192:9216]
        srow = UV[0:96, 7170:7171]
        Z = HTr[:, 0:4096].rearrange("p (h w) -> p h w", h=HEADS)
        mk = HTr[:, 4096:4864].rearrange("p (y k r) -> p y k r", y=3, r=GRID_R)
        ZM = BZ[:, :].rearrange("p (h y k r) -> p h y k r", h=HEADS, y=3, r=GRID_R)
        junk = UV[:, 9216:10240]
        V = UV[:, 0:2560].rearrange("p (t n) -> p t n", t=TT)
        U = UV[:, 2560:5120].rearrange("p (t n) -> p t n", t=TT)
        QT = UV[:, 5120:7680].rearrange("p (g n) -> p g n", g=4)
        KT = UV[:, 7680:10240].rearrange("p (g n) -> p g n", g=4)
        sq = [UV[:, 5120:5632], UV[:, 5632:6144]]
        ssq = UV[:, 6144:6224].rearrange("p (t h) -> p t h", t=TT)
        msq, rsq = UV[:, 6224:6304], UV[:, 6304:6384]
        kout = UV[:, 6464:6976]
        kraw = UV[:, 6976:7488]
        kcT, vc = PS[:, 0:512].rearrange("p (g n) -> p g n", g=4), PS[:, 512:1024]
        vs = PS[:, 1024:2560].rearrange("p (i n) -> p i n", i=3)
        pb = Hr[:, 0:1152].rearrange("p (b n) -> p b n", b=3)
        ptb = Hr[:, 1152:1920].rearrange("p (b n) -> p b n", b=2)
        nm, rsum, rinv = Hr[:, 4992:4996], Hr[:, 4996:5000], Hr[:, 5000:5004]
        fab = [KT[:, :, :].rearrange("p g n -> p (g n)")[:, 1024 * b:1024 * (b + 1)].rearrange("p (s n) -> p s n", s=2)
               for b in range(2)]
        V1 = UV[:, 0:5120].rearrange("p (t n) -> p t n", t=TT)
        U1 = UV[:, 5120:10240].rearrange("p (t n) -> p t n", t=TT)
        ws = PS[:, 0:512].rearrange("p (g n) -> p g n", g=SG)
        wst = PS[:, 512:1024].rearrange("p (g n) -> p g n", g=SG)
        vgain = PS[:, 1024:2048]
        sqv = Hr[:, 0:1024]
        ssv = Hr[:, 1024:1044]
        msv, rsv = Hr[:, 1044:1064], Hr[:, 1064:1084]
        g_b = BZ[:, 0:2048].rearrange("p (q n) -> p q n", q=2)
        sc_b = BZ[:, 2048:4096].rearrange("p (q n) -> p q n", q=2)
        sh_b = BZ[:, 4096:6144].rearrange("p (q n) -> p q n", q=2)
        tmp = [UV[:, 0:512], UV[:, 512:1024]]
        XG = UV[:, 0:3072].rearrange("p (b n) -> p b n", b=3)
        XT = UV[:, 3072:6144].rearrange("p (b c n) -> p b c n", b=3, c=DC)
        YO = UV[:, 6144:9216].rearrange("p (b n) -> p b n", b=3)
        silu_g, hid, hidT = UV[:, 9216:9472], UV[:, 9472:9728], UV[:, 9728:9984].rearrange("p (c n) -> p c n", c=2)
        G = Hr[:, 0:4096].rearrange("p (b s n) -> p b s n", b=2, s=2)
        rc = UV[:, 6144:6144 + 306]
        triu, ones, tokid = rc[:, 0:128], rc[:, 128:256], rc[:, 256:261]
        rank4, rank16, e128, oi = rc[:, 261:265], rc[:, 265:281], rc[:, 281:297], rc[:, 297:306]
        lists = UV[0:NTILE, 6500:6628]

        bank = [ctx.enter_context(nc.psum_tensor(f"bank{i}", [P, 512], F32)) for i in range(8)]

        raw_mod = [dram(f"raw_mod{l}", (2, 6 * D)) for l in range(2)]
        mod = [dram(f"mod{l}", (2, 6, D)) for l in range(2)]
        h2_rows = [dram(f"h2_rows{l}", (TOK, D)) for l in range(2)]
        slot_token = [dram(f"slot_token{l}", (NTILE * P, 1)) for l in range(2)]
        y_rows = dram("y_rows", (NTILE * P, D))

        x_in = sem("x_in")
        small_in = sem("small_in")
        cond_in = sem("cond_in")
        cond_silu = sem("cond_silu")
        block_in = [sem(f"block_in{s}") for s in range(4)]
        ada_mm, ada_read = sem("ada_mm"), sem("ada_read")
        rows_out, fin_in, fin_done, mod_out = sem("rows_out"), sem("fin_in"), sem("fin_done"), sem("mod_out")
        fin_side, fin_memset = sem("fin_side"), sem("fin_memset")
        mod1_in = sem("mod1_in")
        z_in, zm_done = sem("z_in"), sem("zm_done")
        y_zeroed = sem("y_zeroed")
        zero_set, list_zeroed = sem("zero_set"), sem("list_zeroed")
        job_done, job_read_act, job_read_dve = sem("job_done"), sem("job_read_act"), sem("job_read_dve")
        sumsq, meansq, rstd, normed = sem("sumsq"), sem("meansq"), sem("rstd"), sem("normed")
        x_mid, x_out = sem("x_mid"), sem("x_out")
        dve_step = sem("dve_step")
        qk_ss, qk_ms, qk_rs, qk_normed = sem("qk_ss"), sem("qk_ms"), sem("qk_rs"), sem("qk_normed")
        cache_in, v_shifted = sem("cache_in"), sem("v_shifted")
        kout_done, kv_out = sem("kout_done"), sem("kv_out")
        maxed, p_normed, pv_done, o_read = sem("maxed"), sem("p_normed"), sem("pv_done"), sem("o_read")
        bcast_in, bcast_g_in = sem("bcast_in"), sem("bcast_g_in")
        h2_scaled, h2_ready, h2_stored = sem("h2_scaled"), sem("h2_ready"), sem("h2_stored")
        logits_done, scored, picked, pos_done, routed = (sem("logits_done"), sem("scored"), sem("picked"),
                                                         sem("pos_done"), sem("routed"))
        rc_in, scattered, list_in, listT_done, idx_ready = (sem("rc_in"), sem("scattered"), sem("list_in"),
                                                           sem("listT_done"), sem("idx_ready"))
        sg_in, v_done, v_ms, v_rs = sem("sg_in"), sem("v_done"), sem("v_ms"), sem("v_rs")
        qk_summed = sem("qk_summed")
        v_normed = sem("v_normed")
        expert_in = [sem(f"expert_in{s}") for s in range(3)]
        gathered = [sem(f"gathered{s}") for s in range(3)]
        y_stored = [sem(f"y_stored{s}") for s in range(3)]
        xt_mm, xt_act, xt_dve = sem("xt_mm"), sem("xt_act"), sem("xt_dve")
        gu_mm, silu_done, hid_done = sem("gu_mm"), sem("silu_done"), sem("hid_done")
        hidT_mm, hidT_read, down_mm, y_act, y_dve = (sem("hidT_mm"), sem("hidT_read"), sem("down_mm"), sem("y_act"),
                                                    sem("y_dve"))
        OVN = ["gathered0", "gathered1", "gathered2", "in0", "in1", "in2", "xt_mm", "xt_act", "xt_dve", "gu_mm",
               "silu", "hid", "hidT_mm", "hidT_read", "down_mm", "y_act", "y_dve", "stored", "landed", "over"]
        ov = [{n: sem(f"ov{l}_{n}") for n in OVN} for l in range(2)]
        got = [sem(f"got{b}") for b in range(2)]
        g_scaled = sem("g_scaled")
        out_done = sem("out_done")

        reads = {"act": 0, "dve": 0}
        read_after = []
        for _, reader in JOBS:
            reads[reader] += 1
            read_after.append((reader, reads[reader]))

        def wait_read(eng, key):
            reader, n = read_after[JOB[key]]
            eng.wait_ge(job_read_act if reader == "act" else job_read_dve, n)

        def jbank(key):
            return bank[JOB[key] % RING_BANKS]

        def job_free(pe, key):
            k = JOB[key]
            if k >= RING_BANKS:
                wait_read(pe, JOBS[k - RING_BANKS][0])

        def wait_job(eng, key):
            eng.wait_ge(job_done, JOB[key] + 1)

        def cnd(t):
            return 0 if t == 0 else 1

        NB = 2 * ADA_N
        AFTER = [("in", 0, 0), ("in", 0, 1), ("in", 0, 2), ("in", 0, 3), ("dft",), ("tab",), ("out", 0, 0), ("out", 0, 1),
                 ("in", 1, 2), ("in", 1, 3), ("in", 1, 0), ("in", 1, 1), ("out", 1, 0), ("out", 1, 1)]
        SLOT = [0, 1, 2, 3, 0, 1, 2, 3, 0, 1, 2, 3, 2, 3]
        place = {}
        loads = [NB // 4] * 4
        for key, s in zip(AFTER, SLOT):
            loads[s] += 1
            place[key] = (s, loads[s])

        def wait_block(eng, key):
            s, n = place[key]
            eng.wait_ge(block_in[s], 16 * n)

        def blk_ap(key):
            return block(place[key][0])

        ada_v = ada_w.rearrange("l (p c) (g u n) -> l g u p c n", c=DC, u=4, n=512)
        win_v = na_w_in[0].rearrange("(p c) (b n) -> b p c n", c=DC, n=512)
        wout_v = na_w_out[0].rearrange("(c p) (b n) -> b p c n", p=P, n=512)
        sgin_v = sg_w_in[0].rearrange("(p c) (b n) -> b p c n", c=DC, n=512)
        sgout_v = sg_w_out[0].rearrange("(c p) (b n) -> b p c n", p=P, n=512)

        def latent_out(layer, cc):
            out = HT[:, cc, P:TOK]
            if layer == 0:
                return out.rearrange("p (c r) -> p r c", r=GRID_R)
            return out.rearrange("p (r c) -> p r c", r=GRID_R)

        def by_row(a):
            return a.rearrange("p (r c) -> p r c", r=GRID_R)

        def xsrc(t):
            return x_prompt[0] if t == 0 else x_sample[0, P * (t - 1):P * t, :]

        def ydst(t):
            return y_prompt[0] if t == 0 else y_sample[0, P * (t - 1):P * t, :]

        blk = ctx.enter_context(nc.Block())

        @blk.sync
        def _(sp):
            def load_block(key, src):
                s, n = place[key]
                sp.dma_start(block(s), src).then_inc(block_in[s], 16)

            for layer in range(2):
                if layer == 0:
                    for u in range(4):
                        sp.dma_start(block(u), ada_v[0, 0, u]).then_inc(block_in[u], 16)
                with sp.Fori(1 - layer, ADA_N // 4) as g:
                    for u in range(4):
                        sp.wait_ge(ada_mm, ADA_N * layer + 4 * g + u - 3)
                        sp.dma_start(block(u), ada_v[layer, g, u]).then_inc(block_in[u], 16)

            for b in range(4):
                sp.wait_ge(ada_mm, NB - 3 + b)
                load_block(("in", 0, b), win_v[b])
            wait_job(sp, ("p", 0, 0, TT - 1))
            load_block(("dft",), dft)
            wait_job(sp, ("p", 0, 1, TT - 1))
            s, _ = place[("tab",)]
            sp.dma_start(block(s)[:, 0, :], tables).then_inc(block_in[s], 16)
            for b in range(2):
                wait_job(sp, ("p", 0, 2 + b, TT - 1))
                load_block(("out", 0, b), wout_v[b])

            def load_expert(layer, e, s):
                w = xslot(s)
                sp.dma_start(w[:, 0:2048], moe_w_gate[layer].rearrange("e (p c) f -> e p (c f)", c=DC)[e])\
                    .then_inc(expert_in[s], 16)
                sp.dma_start(w[:, 2048:4096], moe_w_up[layer].rearrange("e (p c) f -> e p (c f)", c=DC)[e])\
                    .then_inc(expert_in[s], 16)
                sp.dma_start(w[:, 4096:6144], moe_w_down[layer].rearrange("e (p c) n -> e p (c n)", c=2)[e])\
                    .then_inc(expert_in[s], 16)

            for layer in range(2):
                if layer == 0:
                    wait_job(sp, ("fy", 3))
                else:
                    wait_job(sp, ("p", 1, 1, TT - 1))
                load_expert(layer, 0, 0)
                if layer == 0:
                    wait_job(sp, ("s", len(UNITS) - 1))
                else:
                    sp.wait_ge(h2_ready, TT)
                    sp.wait_ge(x_out, TT)
                if layer == 1:
                    wait_job(sp, ("ut", TT - 1, 1))
                sp.dma_start(rc, route_consts[:, 0:306]).then_inc(rc_in, 16)
                for q in range(2):
                    sp.dma_start(g_b[:, q, :], mod[layer][q, 2:3, :].to_broadcast([P, D])).then_inc(bcast_in, 16)
                    sp.dma_start(sc_b[:, q, :], mod[layer][q, 4:5, :].to_broadcast([P, D])).then_inc(bcast_in, 16)
                    sp.dma_start(sh_b[:, q, :], mod[layer][q, 3:4, :].to_broadcast([P, D])).then_inc(bcast_in, 16)
                wait_job(sp, ("o", layer, TT - 1, 1))
                load_expert(layer, 1, 1)
                load_expert(layer, 2, 2)
                sp.wait_ge(x_mid, 2 * TT * (layer + 1))
                for q in range(2):
                    sp.dma_start(g_b[:, q, :], mod[layer][q, 5:6, :].to_broadcast([P, D])).then_inc(bcast_g_in, 16)

                def store_y(e, s):
                    base = E * layer
                    sp.wait_ge(y_act, base + e + 1)
                    sp.wait_ge(y_dve, base + e + 1)
                    sp.dma_start(y_rows.rearrange("(e p) n -> e p n", p=P)[e], YO[:, s, :])\
                        .then_inc(y_stored[s], 16)

                with sp.Fori(0, 4) as g:
                    for u in range(3):
                        sp.wait_ge(down_mm, E * layer + 3 * g + u + 1)
                        load_expert(layer, 3 * g + u + 3, u)
                        store_y(3 * g + u, u)
                sp.wait_ge(down_mm, E * layer + 13)
                load_expert(layer, 15, 0)
                store_y(12, 0)
                sp.wait_ge(routed, layer + 1)
                n_over = sp.value_load(over_i[0:1, 0:1], min_val=0, max_val=MAXOV)
                for o in range(MAXOV):
                    s = (o + 1) % 3
                    if o == 0:
                        store_y(13, 1)
                    elif o == 1:
                        store_y(14, 2)
                    elif o == 2:
                        sp.wait_ge(down_mm, E * layer + 16)
                        store_y(15, 0)
                    with sp.If(n_over > o):
                        ex = sp.value_load(over_i[0:1, o + 1:o + 2], min_val=0, max_val=E - 1)
                        if o >= 3:
                            sp.wait_ge(ov[layer]["down_mm"], o - 2)
                        w, arrived = xslot(s), ov[layer][f"in{s}"]
                        sp.dma_start(w[:, 0:2048], moe_w_gate[layer].rearrange("e (p c) f -> e p (c f)", c=DC)[ex])\
                            .then_inc(arrived, 16)
                        sp.dma_start(w[:, 2048:4096], moe_w_up[layer].rearrange("e (p c) f -> e p (c f)", c=DC)[ex])\
                            .then_inc(arrived, 16)
                        sp.dma_start(w[:, 4096:6144], moe_w_down[layer].rearrange("e (p c) n -> e p (c n)", c=2)[ex])\
                            .then_inc(arrived, 16)
                sp.wait_ge(ov[layer]["over"], 1)
                if layer == 0:
                    for b in (2, 3, 0, 1):
                        load_block(("in", 1, b), sgin_v[b])
                    for b in range(2):
                        wait_job(sp, ("p", 1, b, TT - 1))
                        load_block(("out", 1, b), sgout_v[b])
            for t in range(TT):
                sp.wait_ge(x_out, TT + t + 1)
                sp.dma_start(ydst(t), X[:, t, :]).then_inc(out_done, 16)
            sp.wait_ge(out_done, 16 * TT)
            sp.wait_ge(kv_out, 32)

        @blk.gpsimd
        def _(pool):
            def rstd_of(k):
                t = k % TT
                pool.wait_ge(meansq, k + 1)
                nc.gpsimd.tensor_tensor(rs[:, t:t + 1], ms[:, t:t + 1], nhalf[:, :], ALU.pow).then_inc(rstd, 1)

            for k in range(TT):
                rstd_of(k)
            pool.wait_ge(qk_ms, 1)
            nc.gpsimd.tensor_tensor(rsq, msq, nhalf.to_broadcast([P, 80]), ALU.pow).then_inc(qk_rs, 1)

            for layer in range(2):
                if layer == 1:
                    for t in range(TT):
                        rstd_of(2 * TT + t)
                    pool.wait_ge(v_ms, 1)
                    nc.gpsimd.tensor_tensor(rsv, msv, nhalf.to_broadcast([P, 20]), ALU.pow).then_inc(v_rs, 1)
                for t in range(TT):
                    rstd_of((2 * layer + 1) * TT + t)
                    n = TT * layer + t
                    pool.wait_ge(h2_scaled, n + 1)
                    nc.gpsimd.tensor_tensor(H[:, t, :], H[:, t, :], sh_b[:, cnd(t), :], ALU.add).then_inc(h2_ready, 1)
                    pool.wait_ge(h2_ready, n + 1)
                    pool.dma_start(h2_rows[layer][P * t:P * (t + 1), :], H[:, t, :]).then_inc(h2_stored, 16)
                pool.wait_ge(list_zeroed, 32)
                pool.wait_ge(rc_in, 16 * (layer + 1))
                pool.wait_ge(routed, layer + 1)
                for t in range(TT):
                    for k in range(2):
                        nc.gpsimd.indirect_dma_start(
                            out=slot_token[layer][:, :],
                            out_offset=bass.IndirectOffsetOnAxis(ap=slot_i[:, t, k:k + 1], axis=0),
                            in_=tokid[:, t:t + 1], in_offset=None).then_inc(scattered, 16)
                pool.wait_ge(scattered, 160 * (layer + 1))
                pool.dma_start(lists, slot_token[layer].rearrange("(e p) o -> e (p o)", p=P)).then_inc(list_in, 16)
                pool.wait_ge(idx_ready, layer + 1)
                pool.wait_ge(h2_stored, 16 * TT * (layer + 1))

                def gather(e, s, signal):
                    nc.gpsimd.indirect_dma_start(
                        out=XG[:, s, :], out_offset=None, in_=h2_rows[layer][:, :],
                        in_offset=bass.IndirectOffsetOnAxis(ap=idx_i[:, e:e + 1], axis=0)).then_inc(signal, 16)

                for e in range(E):
                    if e >= 3:
                        pool.wait_ge(xt_mm, E * layer + e - 2)
                    gather(e, e % 3, gathered[e % 3])
                n_over = pool.value_load(over_i[0:1, 0:1], min_val=0, max_val=MAXOV)
                pool.wait_ge(xt_mm, E * (layer + 1))
                for o in range(MAXOV):
                    s = (o + 1) % 3
                    with pool.If(n_over > o):
                        if o >= 3:
                            pool.wait_ge(ov[layer]["xt_mm"], o - 2)
                        gather(E + o, s, ov[layer][f"gathered{s}"])
                for s in range(3):
                    pool.wait_ge(y_stored[s], 16 * (6 if s == 0 else 5) * (layer + 1))
                pool.wait_ge(ov[layer]["over"], 1)
                for t in range(TT):
                    n = TT * layer + t
                    if t >= 2:
                        pool.wait_ge(x_out, n - 1)
                    for k in range(2):
                        nc.gpsimd.indirect_dma_start(
                            out=G[:, t % 2, k, :], out_offset=None, in_=y_rows[:, :],
                            in_offset=bass.IndirectOffsetOnAxis(ap=slot_i[:, t, k:k + 1], axis=0))\
                            .then_inc(got[t % 2], 16)

        @blk.scalar
        def _(act):
            def square_sum(k):
                t = k % TT
                if k:
                    act.wait_ge(sumsq, k)
                nc.scalar.activation(junk, X[:, t, :], ACT.Square, accum_out=ss[:, t:t + 1]).then_inc(sumsq, 1)

            act.dma_start(cond[:, 0, :], c_ctx.rearrange("(p c) -> p c", c=DC)).then_inc(cond_in, 16)
            act.dma_start(cond[:, 1, :], c[0].rearrange("(p c) -> p c", c=DC)).then_inc(cond_in, 16)
            act.dma_start(ident, route_consts[:, 306:434]).then_inc(small_in, 16)
            for t in range(TT):
                act.dma_start(X[:, t, :], xsrc(t)).then_inc(x_in, 16)
            act.dma_start(rw, router_w.rearrange("(p c) e -> p c e", c=DC)).then_inc(small_in, 16)
            act.dma_start(kgain_b, k_gain[0:1, :].to_broadcast([P, HD])).then_inc(small_in, 16)
            act.dma_start(rb, router_b.rearrange("(o e) -> o e", o=1).to_broadcast([P, E])).then_inc(small_in, 16)
            for half in range(2):
                act.dma_start(gcol[64 * half:64 * half + 64, 0:1], q_gain.rearrange("o (d i) -> (o d) i", i=1))\
                    .then_inc(small_in, 16)
                act.dma_start(gcol[64 * half:64 * half + 64, 1:2], k_gain.rearrange("o (d i) -> (o d) i", i=1))\
                    .then_inc(small_in, 16)
            act.dma_start(srow, scale_rows).then_inc(small_in, 16)
            act.dma_start(mk.rearrange("p y k r -> p (y k r)"), mask).then_inc(z_in, 16)
            for l in range(2):
                act.wait_ge(zero_set, 1)
                act.dma_start(slot_token[l].rearrange("(e p) o -> e (p o)", p=P), zeros[0:NTILE, 0:P]).then_inc(list_zeroed, 16)
            act.dma_start(y_rows[E * P:, :].rearrange("(o p) n -> p o n", p=P),
                          zeros.unsqueeze(1).to_broadcast([P, MAXOV, D])).then_inc(y_zeroed, 16)
            for qc in range(COLS_T):
                skewed = bass.AP(tensor=rpb.tensor, offset=qc, ap=[[64, GRID_R], [15 * 64, HEADS], [1, 496]])
                act.dma_start(Z[GRID_R * qc:GRID_R * (qc + 1), :, 0:496], skewed).then_inc(z_in, 16)

            act.wait_ge(cond_in, 32)
            nc.scalar.activation(scond, cond, ACT.Silu).then_inc(cond_silu, 1)
            for l in range(2):
                for q in range(2):
                    act.dma_start(fin[l][48 * q:48 * q + 48, 1, :], ada_b[l].rearrange("(k n) -> k n", n=P))\
                        .then_inc(fin_side, 16)
            act.wait_ge(fin_memset, 2)
            for l in range(2):
                for q in range(2):
                    for kind, g in ((1, norm1_g), (4, norm2_g)):
                        r = 48 * q + 8 * kind
                        act.dma_start(fin[l][r:r + 8, 2, :], g[l].rearrange("(k n) -> k n", n=P)).then_inc(fin_side, 16)
            for l in range(2):
                for g0 in range(ADA_N):
                    b = ADA_N * l + g0
                    if l == 0 and g0 >= 2:
                        t = (g0 - 2) % TT
                        if g0 < 2 + TT:
                            act.wait_ge(x_in, 16 * TT)
                            square_sum(t)
                        else:
                            act.wait_ge(rstd, t + 1)
                            nc.scalar.activation(H[:, t, :], X[:, t, :], ACT.Copy, scale=rs[:, t:t + 1])\
                                .then_inc(normed, 1)
                    if l and g0 == 4:
                        act.wait_ge(fin_done, 1)
                        act.dma_start(mod[0].rearrange("q k (b n) -> (q k b) n", n=P), fin[0][:, 0, :])\
                            .then_inc(mod_out, 16)
                    if l and not g0:
                        act.wait_ge(rows_out, 16)
                    act.wait_ge(ada_mm, b + 1)
                    nc.scalar.activation(rows[:, 512 * g0:512 * g0 + 512], bank[5 + b % 2][0:2, :], ACT.Copy)\
                        .then_inc(ada_read, 1)
                act.wait_ge(ada_read, ADA_N * (l + 1))
                act.dma_start(raw_mod[l], rows).then_inc(rows_out, 16)
                act.wait_ge(rows_out, 16 * (l + 1))
                act.dma_start(fin[l][:, 0, :], raw_mod[l].rearrange("q (k n) -> (q k) n", n=P)).then_inc(fin_in, 16)
            act.wait_ge(fin_done, 2)
            act.dma_start(mod[1].rearrange("q k (b n) -> (q k b) n", n=P), fin[1][:, 0, :]).then_inc(mod_out, 16)
            act.wait_ge(mod_out, 32)
            for l in range(2):
                for q in range(2):
                    act.dma_start(mod1[:, l, q, :, :], mod[l][q, 0:2, :].rearrange("k (p c) -> p k c", c=DC))\
                        .then_inc(mod1_in, 16)

            def read_transposes(layer):
                act.wait_ge(mod1_in, 64)
                key = ("tc", layer, 0)
                wait_job(act, key)
                for c in range(4):
                    ins = nc.scalar.activation(HT[:, c, 0:P], jbank(key)[:, P * c:P * (c + 1)], ACT.Identity,
                                               bias=mod1[:, layer, 0, 0, c:c + 1], scale=mod1[:, layer, 0, 1, c:c + 1])
                ins.then_inc(job_read_act, 1)
                for c in range(1, DC, 2):
                    key = ("t", layer, c)
                    wait_job(act, key)
                    nc.scalar.activation(latent_out(layer, c), by_row(jbank(key)[:, :]), ACT.Identity,
                                         bias=mod1[:, layer, 1, 0, c:c + 1],
                                         scale=mod1[:, layer, 1, 1, c:c + 1]).then_inc(job_read_act, 1)

            def copy_job(key, out, in_=None):
                wait_job(act, key)
                nc.scalar.activation(out, jbank(key)[:, :] if in_ is None else in_, ACT.Copy).then_inc(job_read_act, 1)

            def out_and_norm(layer):
                def scale_rows_of(t):
                    k = (2 * layer + 1) * TT + t
                    act.wait_ge(rstd, k + 1)
                    nc.scalar.activation(H[:, t, :], X[:, t, :], ACT.Copy, scale=rs[:, t:t + 1]).then_inc(normed, 1)

                def router_rows(t):
                    for h in range(2):
                        key = ("r", layer, t, h)
                        copy_job(key, HT[:, 4 * h:4 * h + 4, P * t:P * (t + 1)],
                                 jbank(key)[:, :].rearrange("p (c n) -> p c n", c=4))

                for t in range(TT):
                    act.wait_ge(x_mid, 2 * TT * layer + 2 * (t + 1))
                    square_sum((2 * layer + 1) * TT + t)
                    scale_rows_of(t)
                    if t:
                        router_rows(t - 1)
                router_rows(TT - 1)
                act.wait_ge(logits_done, layer + 1)
                nc.scalar.activation(UV[:, 0:80], bank[7][:, 0:80], ACT.Sigmoid).then_inc(scored, 1)

            def experts(layer):
                def read_xt(e, b, n):
                    act.wait_ge(xt_mm, n)
                    nc.scalar.activation(XT[:, b, 0:4, :], bank[0][:, :].rearrange("p (c n) -> p c n", c=4), ACT.Copy)\
                        .then_inc(xt_act, 1)

                def body(e, b, last, stored):
                    base = E * layer
                    act.wait_ge(gu_mm, base + e + 1)
                    nc.scalar.activation(silu_g, bank[2][:, 0:FF], ACT.Silu).then_inc(silu_done, 1)
                    if not last:
                        read_xt(e + 1, (b + 1) % 3, base + e + 2)
                    act.wait_ge(hidT_mm, base + e + 1)
                    nc.scalar.activation(hidT, bank[4][:, 0:FF].rearrange("p (c n) -> p c n", c=2), ACT.Copy)\
                        .then_inc(hidT_read, 1)
                    if stored is not None:
                        act.wait_ge(y_stored[b], stored)
                    act.wait_ge(down_mm, base + e + 1)
                    nc.scalar.activation(YO[:, b, 0:512], bank[5][:, :], ACT.Copy).then_inc(y_act, 1)

                read_xt(0, 0, E * layer + 1)
                for e in range(3):
                    body(e, e, False, None)
                with act.Fori(1, 5) as g:
                    for u in range(3):
                        body(3 * g + u, u, False, 16 * (6 if u == 0 else 5) * layer + 16 * g)
                body(15, 0, True, 16 * 6 * layer + 16 * 5)
                o_ = ov[layer]
                for s in range(3):
                    act.wait_ge(y_stored[s], 16 * (6 if s == 0 else 5) * (layer + 1))
                act.wait_ge(routed, layer + 1)
                n_over = act.value_load(over_i[0:1, 0:1], min_val=0, max_val=MAXOV)
                with act.Fori(0, MAXOV // 3) as g:
                    for u in range(3):
                        o, s = 3 * g + u, (u + 1) % 3
                        with act.If(n_over > o):
                            act.wait_ge(o_["xt_mm"], o + 1)
                            nc.scalar.activation(XT[:, s, 0:4, :], bank[0][:, :].rearrange("p (c n) -> p c n", c=4),
                                                 ACT.Copy).then_inc(o_["xt_act"], 1)
                            act.wait_ge(o_["gu_mm"], o + 1)
                            nc.scalar.activation(silu_g, bank[2][:, 0:FF], ACT.Silu).then_inc(o_["silu"], 1)
                            act.wait_ge(o_["hidT_mm"], o + 1)
                            nc.scalar.activation(hidT, bank[4][:, 0:FF].rearrange("p (c n) -> p c n", c=2), ACT.Copy)\
                                .then_inc(o_["hidT_read"], 1)
                            act.wait_ge(o_["down_mm"], o + 1)
                            nc.scalar.activation(YO[:, s, 0:512], bank[5][:, :], ACT.Copy).then_inc(o_["y_act"], 1)
                            act.wait_ge(o_["y_act"], o + 1)
                            act.wait_ge(o_["y_dve"], o + 1)
                            act.dma_start(y_rows[E * P:, :].rearrange("(g u p) n -> g u p n", u=3, p=P)[g, u],
                                          YO[:, s, :]).then_inc(o_["stored"], 16)
                            act.wait_ge(o_["stored"], 16 * (o + 1))
                            act.sem_inc(o_["landed"], 1)
                act.sem_inc(o_["over"], 1)

            def combine(layer):
                for t in range(TT):
                    act.wait_ge(got[t % 2], 32 * ((3 if t % 2 == 0 else 2) * layer + t // 2 + 1))
                    nc.scalar.activation(G[:, t % 2, 0, :], G[:, t % 2, 0, :], ACT.Copy, scale=w12[:, 0, t:t + 1])\
                        .then_inc(g_scaled, 1)

            read_transposes(0)
            for b in range(2):
                for t in range(TT):
                    n = TT * b + t
                    key = ("p", 0, b, t)
                    wait_job(act, key)
                    if n >= 2:
                        act.wait_ge(qk_summed, n - 1)
                    nc.scalar.activation(sq[n % 2], jbank(key)[:, :], ACT.Square).then_inc(qk_ss, 1)
                    nc.scalar.activation(H[:, t, 512 * b:512 * b + 512], jbank(key)[:, :], ACT.Copy)\
                        .then_inc(job_read_act, 1)
            for t in range(TT):
                copy_job(("p", 0, 2, t), V[:, t, :])
                if t == 0:
                    wait_read(act, ("p", 0, 2, 0))
                    act.dma_start(v_ctx.rearrange("b o s h d -> (b o s) (h d)"), V[:, 0, :]).then_inc(kv_out, 16)
            wait_read(act, ("p", 0, 2, TT - 1))
            act.wait_ge(list_zeroed, 32)
            act.wait_ge(y_zeroed, 16)
            act.dma_start(kraw, cache_k.rearrange("b o s h d -> (b o s) (h d)")).then_inc(cache_in, 16)
            act.dma_start(vc, cache_v.rearrange("b o s h d -> (b o s) (h d)")).then_inc(cache_in, 16)
            for i in range(3):
                act.dma_start(vs[0:64, i, :], V[64:128, 1 + i, :]).then_inc(v_shifted, 16)
                act.dma_start(vs[64:128, i, :], V[0:64, 2 + i, :]).then_inc(v_shifted, 16)
            act.wait_ge(kout_done, 1)
            act.dma_start(k_ctx.rearrange("b o s h d -> (b o s) (h d)"), kout).then_inc(kv_out, 16)
            copy_job(("fca",), fab[0][:, 0, :])
            for m in range(4):
                if m:
                    wait_job(act, ("fy", m - 2) if m >= 2 else ("fcy",))
                copy_job(("fa", m), fab[(m + 1) % 2][:, 0, :])
                if m == 0:
                    key = ("fcy",)
                    copy_job(key, HT[:, 4:8, 0:P], jbank(key)[:, :].rearrange("p (c n) -> p c n", c=4))
                else:
                    copy_job(("fy", m - 1), HT[:, 4 + m - 1, P:TOK])
            copy_job(("fy", 3), HT[:, 7, P:TOK])
            copy_job(("kct",), kcT, jbank(("kct",))[:, :].rearrange("p (g n) -> p g n", g=4))
            act.wait_ge(kv_out, 32)
            key = ("ktc",)
            wait_job(act, key)
            nc.scalar.activation(KT[:, :, 0:P], jbank(key)[:, :].rearrange("p (g n) -> p g n", g=4), ACT.Copy,
                                 scale=gcol[:, 1:2]).then_inc(job_read_act, 1)
            for hp in range(4):
                key = ("kt", hp)
                wait_job(act, key)
                nc.scalar.activation(KT[:, hp, P:TOK], jbank(key)[:, :], ACT.Copy, scale=gcol[:, 1:2])\
                    .then_inc(job_read_act, 1)

            def read_pt(u):
                w = P if u < NCTX else 3 * P
                if u >= 2:
                    act.wait_ge(pv_done, u - 1)
                copy_job(("pt", u), ptb[:, u % 2, 0:w], jbank(("pt", u))[:, 0:w])

            for u in range(len(UNITS)):
                w = P if u < NCTX else 3 * P
                key = ("s", u)
                act.wait_ge(maxed, u + 1)
                if u >= 3:
                    wait_job(act, ("pt", u - 3))
                nc.scalar.activation(pb[:, u % 3, 0:w], jbank(key)[:, 0:w], ACT.Exp, bias=nm[:, u % 4:u % 4 + 1],
                                     accum_out=rsum[:, u % 4:u % 4 + 1]).then_inc(job_read_act, 1)
                if u >= 2:
                    read_pt(u - 2)
            for u in range(len(UNITS) - 2, len(UNITS)):
                read_pt(u)
            out_and_norm(0)
            experts(0)
            combine(0)

            act.dma_start(ws, sg_w_s[0].rearrange("g p q -> p g q")).then_inc(sg_in, 16)
            act.dma_start(vgain, sg_v_gain[0:1, :].to_broadcast([P, D])).then_inc(sg_in, 16)
            with nc.allow_non_contiguous_dma(reason="512 scalars, one per partition and group"):
                act.dma_start(bs, sg_b_s[0].rearrange("g p -> p g")).then_inc(sg_in, 16)
            for t in range(TT):
                act.wait_ge(x_out, t + 1)
                square_sum(2 * TT + t)
            for t in range(TT):
                act.wait_ge(rstd, 2 * TT + t + 1)
                nc.scalar.activation(H[:, t, :], X[:, t, :], ACT.Copy, scale=rs[:, t:t + 1]).then_inc(normed, 1)
            read_transposes(1)
            copy_job(("ws",), wst, jbank(("ws",))[:, :].rearrange("p (g n) -> p g n", g=SG))
            for b in (2, 3, 0, 1):
                for t in range(TT):
                    key = ("p", 1, b, t)
                    dst = V1 if b >= 2 else U1
                    wait_job(act, key)
                    nc.scalar.activation(dst[:, t, 512 * (b % 2):512 * (b % 2) + 512], jbank(key)[:, :],
                                         ACT.Gelu_apprx_tanh).then_inc(job_read_act, 1)
            for t in range(TT):
                for h in range(2):
                    key = ("ut", t, h)
                    copy_job(key, HT[:, 4 * h:4 * h + 4, P * t:P * (t + 1)],
                             jbank(key)[:, :].rearrange("p (c n) -> p c n", c=4))
            out_and_norm(1)
            experts(1)
            combine(1)

        @blk.vector
        def _(dve):
            steps = [0]

            def link(ins):
                steps[0] += 1
                ins.then_inc(dve_step, 1)
                dve.wait_ge(dve_step, steps[0])

            nc.vector.memset(zeros, 0.0).then_inc(zero_set, 1)
            link(nc.vector.memset(nhalf, -0.5))
            for l in range(2):
                nc.vector.memset(fin[l][:, 2, :], 1.0).then_inc(fin_memset, 1)
            dve.wait_ge(z_in, 16 * (1 + COLS_T))
            for y in range(3):
                ins = nc.vector.tensor_tensor(
                    ZM[:, :, y, :, :],
                    bass.AP(tensor=HTr, offset=64 * (GRID_R - 1) + 47 - W0[y],
                            ap=[[DC * TOK, P], [512, HEADS], [-1, 32], [-64, GRID_R]]),
                    mk[:, y, :, :].unsqueeze(1).to_broadcast([P, HEADS, 32, GRID_R]), ALU.add)
            ins.then_inc(zm_done, 1)

            def mean_square(k):
                t = k % TT
                dve.wait_ge(sumsq, k + 1)
                nc.vector.tensor_scalar(ms[:, t:t + 1], ss[:, t:t + 1], 1.0 / D, EPS, ALU.mult, ALU.add)\
                    .then_inc(meansq, 1)

            dve.wait_ge(small_in, 16 * 9)
            link(nc.vector.tensor_scalar(gcol[:, 0:1], gcol[:, 0:1], HD ** -0.5, None, ALU.mult))

            def finish_rows(l):
                dve.wait_ge(fin_side, 16 * 12)
                dve.wait_ge(fin_in, 16 * (l + 1))
                f = fin[l]
                link(nc.vector.tensor_tensor(f[:, 0, :], f[:, 0, :], f[:, 1, :], ALU.add))
                nc.vector.scalar_tensor_tensor(f[:, 0, :], f[:, 0, :], srow, f[:, 2, :], ALU.add, ALU.mult)\
                    .then_inc(fin_done, 1)

            for t in range(TT):
                mean_square(t)
            finish_rows(0)
            finish_rows(1)

            def read_transposes(layer):
                dve.wait_ge(mod1_in, 64)
                key = ("tc", layer, 1)
                wait_job(dve, key)
                for c in range(4):
                    ins = nc.vector.tensor_scalar(HT[:, 4 + c, 0:P], jbank(key)[:, P * c:P * (c + 1)],
                                                  mod1[:, layer, 0, 1, 4 + c:5 + c], mod1[:, layer, 0, 0, 4 + c:5 + c],
                                                  ALU.mult, ALU.add)
                ins.then_inc(job_read_dve, 1)
                for c in range(0, DC, 2):
                    key = ("t", layer, c)
                    wait_job(dve, key)
                    nc.vector.tensor_scalar(latent_out(layer, c), by_row(jbank(key)[:, :]), mod1[:, layer, 1, 1, c:c + 1],
                                            mod1[:, layer, 1, 0, c:c + 1], ALU.mult, ALU.add).then_inc(job_read_dve, 1)

            def out_and_norm(layer):
                for t in range(TT):
                    for b in range(2):
                        key = ("o", layer, t, b)
                        cols = slice(512 * b, 512 * b + 512)
                        dve.wait_ge(bcast_in, 96 * (layer + 1))
                        wait_job(dve, key)
                        nc.vector.tensor_tensor(tmp[b], jbank(key)[:, :], g_b[:, cnd(t), cols], ALU.mult)\
                            .then_inc(job_read_dve, 1)
                        wait_read(dve, key)
                        nc.vector.tensor_tensor(X[:, t, cols], X[:, t, cols], tmp[b], ALU.add).then_inc(x_mid, 1)
                        dve.wait_ge(x_mid, 2 * TT * layer + 2 * t + b + 1)
                    k = (2 * layer + 1) * TT + t
                    mean_square(k)
                    dve.wait_ge(normed, k + 1)
                    nc.vector.tensor_tensor(H[:, t, :], H[:, t, :], sc_b[:, cnd(t), :], ALU.mult).then_inc(h2_scaled, 1)

            def route(layer):
                def tmp80(i):
                    return UV[:, 80 * i:80 * i + 80]

                def te(i):
                    return tmp80(i).rearrange("p (t e) -> p t e", t=TT)

                def tg(i):
                    return tmp80(i).rearrange("p (g j) -> p g j", j=4)

                def red(out, in_, op=ALU.max):
                    link(nc.vector.tensor_reduce(out, in_, AX, op))

                def bc(a, n):
                    return a.unsqueeze(2).to_broadcast([P, a.shape[1], n])

                def row(a, n):
                    return a.unsqueeze(1).to_broadcast([P, n, a.shape[1]])

                def tt(out, a, b, op):
                    link(nc.vector.tensor_tensor(out, a, b, op))

                dve.wait_ge(scored, layer + 1)
                dve.wait_ge(rc_in, 16 * (layer + 1))
                score, sel = te(0), te(1)
                tt(sel, score, row(rb, TT), ALU.add)
                v = tg(1)
                pairs = UV[:, 160:280].rearrange("p (g j) -> p g j", j=6)
                tt(pairs[:, :, 0:3], v[:, :, 0:3], v[:, :, 1:4], ALU.add)
                tt(pairs[:, :, 3:5], v[:, :, 0:2], v[:, :, 2:4], ALU.add)
                tt(pairs[:, :, 5:6], v[:, :, 0:1], v[:, :, 3:4], ALU.add)
                gs, gmax, gpick = UV[:, 280:300], UV[:, 300:305], UV[:, 305:325]
                red(gs, pairs)
                gs3, gp3 = gs.rearrange("p (t g) -> p t g", g=4), gpick.rearrange("p (t g) -> p t g", g=4)
                red(gmax, gs3)
                tt(gp3, gs3, bc(gmax, 4), ALU.is_equal)
                tt(gp3, gp3, row(rank4, TT), ALU.mult)
                red(gmax, gp3)
                tt(gp3, gp3, bc(gmax, 4), ALU.is_equal)
                off = UV[:, 325:345]
                link(nc.vector.tensor_scalar(off, gpick, -NEG, NEG, ALU.mult, ALU.add))
                tt(v, v, bc(gpick, 4), ALU.mult)
                tt(v, v, bc(off, 4), ALU.add)
                m5 = UV[:, 345:350]
                picks = [te(5), te(6)]
                for k in range(2):
                    red(m5, sel)
                    tt(picks[k], sel, bc(m5, E), ALU.is_equal)
                    tt(picks[k], picks[k], row(rank16, TT), ALU.mult)
                    red(m5, picks[k])
                    tt(picks[k], picks[k], bc(m5, E), ALU.is_equal)
                    if k == 0:
                        link(nc.vector.scalar_tensor_tensor(sel, picks[0], 2 * NEG, sel, ALU.mult, ALU.add))
                both = te(7)
                nc.vector.tensor_tensor(both, picks[0], picks[1], ALU.add).then_inc(picked, 1)
                prod = te(8)
                for k in range(2):
                    tt(prod, picks[k], score, ALU.mult)
                    red(w12[:, k, :], prod, ALU.add)
                wsum = UV[:, 350:355]
                tt(wsum, w12[:, 0, :], w12[:, 1, :], ALU.add)
                link(nc.vector.reciprocal(wsum, wsum))
                tt(w12, w12, row(wsum, 2), ALU.mult)
                dve.wait_ge(pos_done, layer + 1)
                pos, cnt = te(9), UV[:, 800:816]
                link(nc.vector.tensor_copy(UV[:, 720:816], bank[6][:, 0:96]))
                ovf, inc, one16 = UV[:, 816:832], UV[:, 832:848], UV[:, 848:864]
                link(nc.vector.memset(one16, 1.0))
                link(nc.vector.tensor_scalar(ovf, cnt, P + 0.5, None, ALU.is_gt))
                for k in range(2, TT):
                    link(nc.vector.scalar_tensor_tensor(ovf, cnt, k * P + 0.5, ovf, ALU.is_gt, ALU.add))
                link(nc.vector.tensor_tensor_scan(inc, one16, ovf, 0.0, ALU.mult, ALU.add))
                delta = UV[:, 864:880]
                tt(delta, inc, ovf, ALU.subtract)
                link(nc.vector.tensor_scalar(delta, delta, float(P), float((E - 1) * P), ALU.mult, ALU.add))
                tt(delta, delta, e128, ALU.subtract)
                big, rowno = te(11), te(12)
                link(nc.vector.tensor_scalar(big, pos, P - 0.5, None, ALU.is_gt))
                tt(big, big, row(delta, TT), ALU.mult)
                tt(big, big, pos, ALU.add)
                tt(rowno, big, row(e128, TT), ALU.add)
                sl = UV[:, 1040:1050].rearrange("p (s t) -> p s t", s=2)
                for k in range(2):
                    tt(prod, picks[k], rowno, ALU.mult)
                    red(sl[:, k, :], prod, ALU.add)
                link(nc.vector.tensor_copy(slot_i, sl.rearrange("p s t -> p t s")))
                le = UV[:, 1056:1200].rearrange("p (o e) -> p o e", o=MAXOV)
                ovx = UV[:, 1200:1200 + MAXOV + 1]
                tt(le, row(inc, MAXOV), bc(oi, E), ALU.is_le)
                red(ovx[:, 1:1 + MAXOV], le, ALU.add)
                link(nc.vector.tensor_scalar(ovx[:, 1:1 + MAXOV], ovx[:, 1:1 + MAXOV], float(E - 1), None, ALU.min))
                link(nc.vector.tensor_copy(ovx[:, 0:1], inc[:, E - 1:E]))
                nc.vector.tensor_copy(over_i, ovx).then_inc(routed, 1)
                dve.wait_ge(listT_done, layer + 1)
                nc.vector.tensor_copy(idx_i, bank[6][:, 128:128 + NTILE]).then_inc(idx_ready, 1)

            def experts(layer):
                base = E * layer

                def read_xt(b, n):
                    dve.wait_ge(xt_mm, n)
                    nc.vector.tensor_copy(XT[:, b, 4:8, :], bank[1][:, :].rearrange("p (c n) -> p c n", c=4))\
                        .then_inc(xt_dve, 1)

                def body(e, b, last, stored):
                    dve.wait_ge(silu_done, base + e + 1)
                    nc.vector.tensor_tensor(hid, silu_g, bank[2][:, FF:2 * FF], ALU.mult).then_inc(hid_done, 1)
                    if not last:
                        read_xt((b + 1) % 3, base + e + 2)
                    if stored is not None:
                        dve.wait_ge(y_stored[b], stored)
                    dve.wait_ge(down_mm, base + e + 1)
                    nc.vector.tensor_copy(YO[:, b, 512:1024], bank[6][:, :]).then_inc(y_dve, 1)

                read_xt(0, base + 1)
                for e in range(3):
                    body(e, e, False, None)
                with dve.Fori(1, 5) as g:
                    for u in range(3):
                        body(3 * g + u, u, False, 16 * (6 if u == 0 else 5) * layer + 16 * g)
                body(15, 0, True, 16 * 6 * layer + 16 * 5)
                o_ = ov[layer]
                for s in range(3):
                    dve.wait_ge(y_stored[s], 16 * (6 if s == 0 else 5) * (layer + 1))
                n_over = dve.value_load(over_i[0:1, 0:1], min_val=0, max_val=MAXOV)
                with dve.Fori(0, MAXOV // 3) as g:
                    for u in range(3):
                        o, s = 3 * g + u, (u + 1) % 3
                        with dve.If(n_over > o):
                            dve.wait_ge(o_["xt_mm"], o + 1)
                            nc.vector.tensor_copy(XT[:, s, 4:8, :], bank[1][:, :].rearrange("p (c n) -> p c n", c=4))\
                                .then_inc(o_["xt_dve"], 1)
                            dve.wait_ge(o_["silu"], o + 1)
                            nc.vector.tensor_tensor(hid, silu_g, bank[2][:, FF:2 * FF], ALU.mult)\
                                .then_inc(o_["hid"], 1)
                            dve.wait_ge(o_["down_mm"], o + 1)
                            nc.vector.tensor_copy(YO[:, s, 512:1024], bank[6][:, :]).then_inc(o_["y_dve"], 1)

            def combine(layer):
                dve.wait_ge(bcast_g_in, 32 * (layer + 1))
                for t in range(TT):
                    n = TT * layer + t
                    y1, y2 = G[:, t % 2, 0, :], G[:, t % 2, 1, :]
                    dve.wait_ge(g_scaled, n + 1)
                    link(nc.vector.scalar_tensor_tensor(y1, y2, w12[:, 1, t:t + 1], y1, ALU.mult, ALU.add))
                    link(nc.vector.tensor_tensor(y2, y1, g_b[:, cnd(t), :], ALU.mult))
                    nc.vector.tensor_tensor(X[:, t, :], X[:, t, :], y2, ALU.add).then_inc(x_out, 1)

            read_transposes(0)
            for b in range(2):
                for t in range(TT):
                    n = TT * b + t
                    dve.wait_ge(qk_ss, n + 1)
                    nc.vector.tensor_reduce(ssq[:, t, 8 * b:8 * b + 8], sq[n % 2].rearrange("p (h d) -> p h d", d=HD),
                                            AX, ALU.add).then_inc(qk_summed, 1)
            dve.wait_ge(qk_summed, 2 * TT)
            nc.vector.tensor_scalar(msq, ssq.rearrange("p t h -> p (t h)"), 1.0 / HD, EPS, ALU.mult, ALU.add)\
                .then_inc(qk_ms, 1)
            dve.wait_ge(qk_rs, 1)
            for t in range(TT):
                wait_read(dve, ("p", 0, 1, t))
                hq = H[:, t, :].rearrange("p (h d) -> p h d", d=HD)
                r = rsq.rearrange("p (t h) -> p t h", t=TT)[:, t, :].unsqueeze(2).to_broadcast([P, 2 * HEADS, HD])
                nc.vector.tensor_tensor(hq, hq, r, ALU.mult).then_inc(qk_normed, 1)
            dve.wait_ge(qk_normed, TT)
            nc.vector.tensor_tensor(kout.rearrange("p (h d) -> p h d", d=HD),
                                    H[:, 0, 512:1024].rearrange("p (h d) -> p h d", d=HD),
                                    kgain_b.unsqueeze(1).to_broadcast([P, HEADS, HD]), ALU.mult).then_inc(kout_done, 1)

            def copy_job(key, out, in_=None):
                wait_job(dve, key)
                nc.vector.tensor_copy(out, jbank(key)[:, :] if in_ is None else in_).then_inc(job_read_dve, 1)

            for t in range(TT):
                copy_job(("p", 0, 3, t), U[:, t, :])
            copy_job(("fcb",), fab[0][:, 1, :])
            for m in range(4):
                if m:
                    wait_job(dve, ("fy", m - 2) if m >= 2 else ("fcy",))
                copy_job(("fb", m), fab[(m + 1) % 2][:, 1, :])
            dve.wait_ge(kv_out, 32)
            wait_job(dve, ("kct",))
            key = ("qtc",)
            wait_job(dve, key)
            nc.vector.tensor_scalar(QT[:, :, 0:P], jbank(key)[:, :].rearrange("p (g n) -> p g n", g=4), gcol[:, 0:1],
                                    None, ALU.mult).then_inc(job_read_dve, 1)
            for hp in range(4):
                key = ("qt", hp)
                wait_job(dve, key)
                nc.vector.tensor_scalar(QT[:, hp, P:TOK], jbank(key)[:, :], gcol[:, 0:1], None, ALU.mult)\
                    .then_inc(job_read_dve, 1)

            def normalise(u):
                w = P if u < NCTX else 3 * P
                wait_read(dve, ("s", u))
                link(nc.vector.reciprocal(rinv[:, u % 4:u % 4 + 1], rsum[:, u % 4:u % 4 + 1]))
                nc.vector.tensor_scalar(pb[:, u % 3, 0:w], pb[:, u % 3, 0:w], rinv[:, u % 4:u % 4 + 1], None, ALU.mult)\
                    .then_inc(p_normed, 1)

            def read_o(n):
                dve.wait_ge(pv_done, 8 * (n + 1))
                if n == 0:
                    nc.vector.tensor_copy(HT[:, 0:4, 0:P], bank[7][:, :].rearrange("p (g n) -> p g n", g=4))\
                        .then_inc(o_read, 1)
                else:
                    hp = n - 1
                    nc.vector.tensor_copy(HT[:, hp, P:TOK].rearrange("p (r c) -> p c r", r=GRID_R),
                                          bank[5 + hp % 2][:, :].rearrange("p (c r) -> p c r", r=GRID_R))\
                        .then_inc(o_read, 1)

            for u in range(len(UNITS)):
                w = P if u < NCTX else 3 * P
                wait_job(dve, ("s", u))
                nc.vector.tensor_reduce(nm[:, u % 4:u % 4 + 1], jbank(("s", u))[:, 0:w], AX, ALU.max, negate=True)\
                    .then_inc(maxed, 1)
                if u:
                    normalise(u - 1)
                if u >= 12 and (u - 12) % 8 == 0:
                    read_o((u - 12) // 8)
            normalise(len(UNITS) - 1)
            read_o(4)
            out_and_norm(0)
            route(0)
            experts(0)
            combine(0)

            for t in range(TT):
                mean_square(2 * TT + t)
            read_transposes(1)
            dve.wait_ge(sg_in, 48)
            wait_job(dve, ("t", 1, DC - 1))
            for t in range(TT):
                wait_read(dve, ("p", 1, 3, t))
                link(nc.vector.tensor_tensor(sqv, V1[:, t, :], V1[:, t, :], ALU.mult))
                link(nc.vector.tensor_reduce(ssv[:, SG * t:SG * t + SG], sqv.rearrange("p (g d) -> p g d", g=SG), AX,
                                             ALU.add))
            nc.vector.tensor_scalar(msv, ssv, SG / D, EPS, ALU.mult, ALU.add).then_inc(v_ms, 1)
            dve.wait_ge(v_rs, 1)
            for t in range(TT):
                r = rsv[:, SG * t:SG * t + SG].unsqueeze(2).to_broadcast([P, SG, D // SG])
                vv = V1[:, t, :].rearrange("p (g d) -> p g d", g=SG)
                link(nc.vector.tensor_tensor(vv, vv, r, ALU.mult))
                nc.vector.tensor_tensor(V1[:, t, :], V1[:, t, :], vgain, ALU.mult).then_inc(v_normed, 1)
            for t in range(TT):
                for b in range(2):
                    key = ("sp", t, b)
                    wait_job(dve, key)
                    wait_read(dve, ("p", 1, b, t))
                    for i in range(2):
                        g = 2 * b + i
                        u_ = U1[:, t, 256 * g:256 * g + 256]
                        ins = nc.vector.scalar_tensor_tensor(u_, jbank(key)[:, 256 * i:256 * i + 256], bs[:, g:g + 1],
                                                             u_, ALU.add, ALU.mult)
                    ins.then_inc(job_read_dve, 1)
            out_and_norm(1)
            route(1)
            experts(1)
            combine(1)

        @blk.tensor
        def _(pe):
            mm = nc.tensor.matmul

            def transposes(key, srcs, wdt=P):
                job_free(pe, key)
                for i, s in enumerate(srcs):
                    last = nc.tensor.transpose(jbank(key)[:, wdt * i:wdt * (i + 1)], s, ident)
                last.then_inc(job_done, 1)

            pe.wait_ge(cond_silu, 1)

            def ada(b, g, u, first):
                if not first:
                    pe.wait_ge(ada_read, b - 1)
                pe.wait_ge(block_in[u], 16 * (g + 1))
                for cc in range(DC):
                    last = mm(bank[5 + u % 2][0:2, :], scond[:, :, cc], block(u)[:, cc, :], start=cc == 0,
                              stop=cc == DC - 1)
                last.then_inc(ada_mm, 1)

            for b in range(4):
                ada(b, 0, b, b < 2)
            with pe.Fori(1, NB // 4) as g:
                for u in range(4):
                    ada(4 * g + u, g, u, False)

            def norm_transposes(layer):
                if layer == 0:
                    pe.wait_ge(small_in, 16 * 9)
                pe.wait_ge(normed, TT * (2 * layer + 1))
                for h in range(2):
                    transposes(("tc", layer, h), [H[:, 0, 4 * h + i::DC] for i in range(4)])
                for cc in range(DC):
                    transposes(("t", layer, cc), [H[:, t, cc::DC] for t in range(1, TT)])

            def project(layer, b, t):
                key = ("p", layer, b, t)
                job_free(pe, key)
                w = blk_ap(("in", layer, b))
                for cc in range(DC):
                    last = mm(jbank(key)[:, :], HT[:, cc, P * t:P * (t + 1)], w[:, cc, :], start=cc == 0,
                              stop=cc == DC - 1)
                last.then_inc(job_done, 1)

            def out_projection(layer):
                def router(t):
                    pe.wait_ge(h2_ready, TT * layer + t + 1)
                    for h in range(2):
                        transposes(("r", layer, t, h), [H[:, t, 4 * h + i::DC] for i in range(4)])
                    wait_read(pe, ("r", layer, t, 1))
                    for cc in range(DC):
                        last = mm(bank[7][:, E * t:E * t + E], HT[:, cc, P * t:P * (t + 1)], rw[:, cc, :],
                                  start=cc == 0, stop=cc == DC - 1)
                    return last

                for t in range(TT):
                    for b in range(2):
                        key = ("o", layer, t, b)
                        job_free(pe, key)
                        wait_block(pe, ("out", layer, b))
                        for cc in range(DC):
                            last = mm(jbank(key)[:, :], HT[:, cc, P * t:P * (t + 1)], blk_ap(("out", layer, b))[:, cc, :],
                                      start=cc == 0, stop=cc == DC - 1)
                        last.then_inc(job_done, 1)
                    if t:
                        router(t - 1)
                router(TT - 1).then_inc(logits_done, 1)
                pe.wait_ge(picked, layer + 1)
                pe.wait_ge(rc_in, 16 * (layer + 1))
                both = UV[:, 560:640].rearrange("p (t e) -> p t e", t=TT)
                for t in range(TT + 1):
                    terms = [(ones, i) for i in range(t)] + ([(triu, t)] if t < TT else [])
                    for i, (w, src) in enumerate(terms):
                        last = mm(bank[6][:, E * t:E * t + E], w, both[:, src, :], start=i == 0,
                                  stop=i == len(terms) - 1)
                last.then_inc(pos_done, 1)
                pe.wait_ge(list_in, 16 * (layer + 1))
                nc.tensor.transpose(bank[6][:, 128:128 + NTILE], lists, ident[0:NTILE, 0:NTILE]).then_inc(listT_done, 1)

            def xt_transposes(b):
                for i in range(DC):
                    last = nc.tensor.transpose(bank[i // 4][:, P * (i % 4):P * (i % 4) + P], XG[:, b, i::DC], ident)
                return last

            def gate_up(b, s):
                w = xslot(s)[:, 0:4096].rearrange("p (k c n) -> p k c n", k=2, c=DC)
                for cc in range(DC):
                    last = mm(bank[2][:, :], XT[:, b, cc, :], w[:, :, cc, :], start=cc == 0, stop=cc == DC - 1)
                return last

            def hid_transposes():
                for i in range(2):
                    last = nc.tensor.transpose(bank[4][:, P * i:P * (i + 1)], hid[:, i::2], ident)
                return last

            def down(s):
                w = xslot(s)[:, 4096:6144].rearrange("p (c n) -> p c n", c=2)
                for half in range(2):
                    for i in range(2):
                        last = mm(bank[5 + half][:, :], hidT[:, i, :], w[:, i, 512 * half:512 * half + 512],
                                  start=i == 0, stop=i == 1)
                return last

            def experts(layer):
                base = E * layer

                def body(e, b, first, last_one, arrived, next_gathered):
                    pe.wait_ge(xt_act, base + e + 1)
                    pe.wait_ge(xt_dve, base + e + 1)
                    pe.wait_ge(expert_in[b], arrived)
                    gate_up(b, b).then_inc(gu_mm, 1)
                    if not last_one:
                        pe.wait_ge(gathered[(b + 1) % 3], next_gathered)
                        xt_transposes((b + 1) % 3).then_inc(xt_mm, 1)
                    pe.wait_ge(hid_done, base + e + 1)
                    hid_transposes().then_inc(hidT_mm, 1)
                    pe.wait_ge(hidT_read, base + e + 1)
                    if not first:
                        pe.wait_ge(y_act, base + e)
                        pe.wait_ge(y_dve, base + e)
                    down(b).then_inc(down_mm, 1)

                def arrivals(n, s, each):
                    return each * ((6 if s == 0 else 5) * layer + n)

                pe.wait_ge(gathered[0], arrivals(1, 0, 16))
                wait_read(pe, ("r", layer, TT - 1, 1))
                wait_read(pe, ("o", layer, TT - 1, 1))
                xt_transposes(0).then_inc(xt_mm, 1)
                for e in range(3):
                    body(e, e, e == 0, False, arrivals(1, e, 48), arrivals(1 + (e == 2), (e + 1) % 3, 16))
                with pe.Fori(1, 5) as g:
                    for u in range(3):
                        body(3 * g + u, u, False, False, arrivals(g + 1, u, 48),
                             arrivals(g + 1 + (u == 2), (u + 1) % 3, 16))
                body(15, 0, False, True, arrivals(6, 0, 48), None)
                pe.wait_ge(y_act, base + E)
                pe.wait_ge(y_dve, base + E)
                o_ = ov[layer]
                n_over = pe.value_load(over_i[0:1, 0:1], min_val=0, max_val=MAXOV)
                with pe.Fori(0, MAXOV // 3) as g:
                    for u in range(3):
                        o, s = 3 * g + u, (u + 1) % 3
                        with pe.If(n_over > o):
                            pe.wait_ge(o_[f"gathered{s}"], 16 * (g + 1))
                            xt_transposes(s).then_inc(o_["xt_mm"], 1)
                            pe.wait_ge(o_["xt_act"], o + 1)
                            pe.wait_ge(o_["xt_dve"], o + 1)
                            pe.wait_ge(o_[f"in{s}"], 48 * (g + 1))
                            gate_up(s, s).then_inc(o_["gu_mm"], 1)
                            pe.wait_ge(o_["hid"], o + 1)
                            hid_transposes().then_inc(o_["hidT_mm"], 1)
                            pe.wait_ge(o_["hidT_read"], o + 1)
                            down(s).then_inc(o_["down_mm"], 1)
                            pe.wait_ge(o_["y_act"], o + 1)
                            pe.wait_ge(o_["y_dve"], o + 1)

            norm_transposes(0)
            for cc in range(DC - 2, DC):
                wait_read(pe, ("t", 0, cc))
            wait_read(pe, ("tc", 0, 0))
            wait_read(pe, ("tc", 0, 1))
            for b in range(4):
                wait_block(pe, ("in", 0, b))
                for t in range(TT):
                    project(0, b, t)

            wait_block(pe, ("dft",))
            wait_block(pe, ("tab",))
            wait_read(pe, ("p", 0, 3, TT - 1))
            tab = blk_ap(("tab",))[:, 0, :].rearrange("p (k n) -> p k n", k=4)
            dftb = blk_ap(("dft",))
            for k, key in enumerate((("fca",), ("fcb",))):
                job_free(pe, key)
                for m in range(4):
                    last = mm(jbank(key)[:, P * m:P * (m + 1)], U[:, 0, P * m:P * (m + 1)], tab[:, k, :], start=True,
                              stop=True)
                last.then_inc(job_done, 1)

            def channels(key, b):
                job_free(pe, key)
                for s in range(2):
                    last = mm(jbank(key)[:, :], tab[:, 2 + s, :], fab[b][:, s, :], start=s == 0, stop=s == 1)
                last.then_inc(job_done, 1)

            for m in range(4):
                for k, name in enumerate(("fa", "fb")):
                    key = (name, m)
                    job_free(pe, key)
                    for i in range(4):
                        last = mm(jbank(key)[:, :], U[:, 1 + i, P * m:P * (m + 1)], dftb[:, 4 * k + i, :], start=i == 0,
                                  stop=i == 3)
                    last.then_inc(job_done, 1)
                if m == 0:
                    wait_read(pe, ("fca",))
                    wait_read(pe, ("fcb",))
                    channels(("fcy",), 0)
                else:
                    wait_read(pe, ("fa", m - 1))
                    wait_read(pe, ("fb", m - 1))
                    channels(("fy", m - 1), m % 2)
            wait_read(pe, ("fa", 3))
            wait_read(pe, ("fb", 3))
            channels(("fy", 3), 0)

            pe.wait_ge(cache_in, 32)
            transposes(("kct",), [kraw[:, P * g:P * (g + 1)] for g in range(4)])
            pe.wait_ge(qk_normed, TT)
            transposes(("qtc",), [H[:, 0, P * g:P * (g + 1)] for g in range(4)])
            transposes(("ktc",), [H[:, 0, 512 + P * g:512 + P * (g + 1)] for g in range(4)])
            for hp in range(4):
                transposes(("qt", hp), [H[:, t, P * hp:P * (hp + 1)] for t in range(1, TT)])
                transposes(("kt", hp), [H[:, t, 512 + P * hp:512 + P * (hp + 1)] for t in range(1, TT)])
            wait_read(pe, ("qt", 3))
            wait_read(pe, ("kt", 3))
            pe.wait_ge(zm_done, 1)
            pe.wait_ge(v_shifted, 96)

            def scores(u):
                hp, qt, par = UNITS[u]
                key = ("s", u)
                out = jbank(key)
                job_free(pe, key)
                at_ = slice(64 * par, 64 * par + 64)
                q = QT[at_, hp, P * qt:P * (qt + 1)]
                if qt == 0:
                    last = mm(out[:, 0:P], q, KT[at_, hp, 0:P], start=True, stop=True)
                else:
                    k0 = P + KEY_START[qt - 1]
                    h = 2 * hp + par
                    mm(out[:, BAND:BAND + P], q, kcT[at_, hp, :], start=True, stop=True)
                    mm(out[:, 0:BAND], q, KT[at_, hp, k0:k0 + BAND], start=True, stop=False)
                    last = mm(out[:, 0:BAND], ident, ZM[:, h, BIAS_TYPE[qt - 1], :, :].rearrange("p k r -> p (k r)"),
                              start=False, stop=True)
                last.then_inc(job_done, 1)

            def probs_t(u):
                w = 1 if u < NCTX else 3
                pe.wait_ge(p_normed, u + 1)
                transposes(("pt", u), [pb[:, u % 3, P * i:P * (i + 1)] for i in range(w)])

            def values(u):
                hp, qt, par = UNITS[u]
                wait_read(pe, ("pt", u))
                cols = slice(64 * (2 * hp + par), 64 * (2 * hp + par) + 64)
                if qt == 0:
                    out, vals = bank[7][64 * par:64 * par + 64, P * hp:P * (hp + 1)], [V[:, 0, cols]]
                else:
                    if u % 8 == 0 and hp >= 2:
                        pe.wait_ge(o_read, hp)
                    out = bank[5 + hp % 2][64 * par:64 * par + 64, P * (qt - 1):P * qt]
                    vals = {1: [V[:, 1, cols], V[:, 2, cols]], 2: [vs[:, 0, cols], vs[:, 1, cols]],
                            3: [vs[:, 1, cols], vs[:, 2, cols]], 4: [V[:, 3, cols], V[:, 4, cols]]}[qt]
                    vals = vals + [vc[:, cols]]
                for i, v in enumerate(vals):
                    last = mm(out, v, ptb[:, u % 2, P * i:P * (i + 1)], start=i == 0, stop=i == len(vals) - 1)
                last.then_inc(pv_done, 1)

            n = len(UNITS)
            for u in range(n + 3):
                if u < n:
                    scores(u)
                if 2 <= u < n + 2:
                    probs_t(u - 2)
                if u >= 3:
                    values(u - 3)
            pe.wait_ge(o_read, 5)
            out_projection(0)
            experts(0)

            norm_transposes(1)
            pe.wait_ge(sg_in, 48)
            transposes(("ws",), [ws[:, g, :] for g in range(SG)])
            for cc in range(DC - 2, DC):
                wait_read(pe, ("t", 1, cc))
            wait_read(pe, ("tc", 1, 0))
            wait_read(pe, ("tc", 1, 1))
            for b in (2, 3, 0, 1):
                wait_block(pe, ("in", 1, b))
                for t in range(TT):
                    project(1, b, t)
            wait_read(pe, ("ws",))

            def us_transposes(t):
                wait_read(pe, ("sp", t, 1))
                for h in range(2):
                    transposes(("ut", t, h), [U1[:, t, P * (4 * h + i):P * (4 * h + i + 1)] for i in range(4)])

            for t in range(TT):
                pe.wait_ge(v_normed, t + 1)
                for b in range(2):
                    key = ("sp", t, b)
                    job_free(pe, key)
                    for i in range(2):
                        g = 2 * b + i
                        last = mm(jbank(key)[:, 256 * i:256 * i + 256], wst[:, g, :], V1[:, t, 256 * g:256 * g + 256],
                                  start=True, stop=True)
                    last.then_inc(job_done, 1)
                if t:
                    us_transposes(t - 1)
            us_transposes(TT - 1)
            wait_read(pe, ("ut", TT - 1, 1))
            out_projection(1)
            experts(1)


def shape_constants():
    def dft_pair(n):
        a = 2.0 * np.pi * (np.outer(np.arange(n), np.arange(n)) % n) / n
        return np.cos(a), np.sin(a)

    lat = GRID_R * GRID_W
    c_, s_ = dft_pair(lat)
    n = np.arange(lat)
    by_column = n % GRID_R * GRID_W + n // GRID_R
    dft = np.concatenate([m[by_column].reshape(4, P, lat).transpose(1, 0, 2) for m in (c_, s_)], axis=1) / np.sqrt(lat)
    cc, cs = dft_pair(P)
    g_, gs_ = dft_pair(HD)
    pair = np.eye(2)
    tables = np.concatenate([cc / np.sqrt(P), cs / np.sqrt(P), np.kron(pair, g_) / 8, -np.kron(pair, gs_) / 8], axis=1)
    mask = np.zeros((P, 3, 32, GRID_R))
    for y, tile in enumerate((0, 1, 3)):
        qc = COLS_T * tile + np.arange(P) // GRID_R
        kc = KEY_START[tile] // GRID_R + np.arange(32)
        start = np.clip(qc - 8, 0, GRID_W - 16)
        ok = (kc[None] >= start[:, None]) & (kc[None] < start[:, None] + 16)
        mask[:, y] = np.where(ok, 0.0, NEG)[:, :, None]
    rc = np.zeros((P, 434))
    rc[:, 0:128] = np.triu(np.ones((P, P)), 1)
    rc[:, 128:256] = 1.0
    rc[:, 256:261] = np.arange(P)[:, None] + P * np.arange(TT)[None]
    rc[:, 261:265] = np.arange(4, 0, -1)
    rc[:, 265:281] = np.arange(E, 0, -1)
    rc[:, 281:297] = P * np.arange(E)
    rc[:, 297:306] = np.arange(MAXOV)
    rc[:, 306:434] = np.eye(P)
    rows = np.zeros((2, 6, 8))
    rows[:, (1, 4), :] = 1.0
    return {"dft": dft, "tables": tables, "mask": mask.reshape(P, -1), "route_consts": rc,
            "scale_rows": rows.reshape(96, 1)}


_INS = ["x_prompt", "x_sample", "cache_k", "cache_v", "c", "c_ctx", "ada_w", "ada_b", "norm1_g", "norm2_g", "na_w_in",
        "na_w_out", "q_gain", "k_gain", "rpb", "sg_w_in", "sg_w_out", "sg_v_gain", "sg_w_s", "sg_b_s", "router_w",
        "router_b", "moe_w_gate", "moe_w_up", "moe_w_down"]
_OUTS = [(1, P, D), (1, 512, D), (1, 1, P, HEADS, HD), (1, 1, P, HEADS, HD)]


def kernel(**inputs):
    import concourse.bacc as _bacc
    from concourse.bass_utils import run_bass_kernel_spmd as _run

    nc = _bacc.Bacc("TRN2", target_bir_lowering=False, num_devices=1)
    arrays, args = {}, []
    given = {name: np.ascontiguousarray(inputs[name]) for name in _INS}
    given["rpb"] = np.pad(given["rpb"][0, :, ::-1, ::-1], ((0, 0), (0, 0), (16, 17)))
    for name, a in shape_constants().items():
        given[name] = np.ascontiguousarray(a, dtype=np.float32)
    for name, a in given.items():
        arrays[f"in_{name}"] = a
        args.append(nc.dram_tensor(f"in_{name}", a.shape, F32, kind="ExternalInput").ap())
    for i, shape in enumerate(_OUTS):
        args.append(nc.dram_tensor(f"out_{i}", shape, F32, kind="ExternalOutput").ap())
    build(nc, *args)
    r = _run(nc, [arrays], core_ids=[0])
    return tuple(r.results[0][f"out_{i}"] for i in range(len(_OUTS)))
```

```python
from contextlib import ExitStack

import numpy as np

import concourse.bass as bass
from concourse import mybir

F32 = mybir.dt.float32
I32 = mybir.dt.int32
ALU = mybir.AluOpType
ACT = mybir.ActivationFunctionType
AX = mybir.AxisListType.X

P = 128
D = 1024
DC = D // P
GRID_W, GRID_R = 64, 8
TT = 5
TOK = TT * P
HEADS, HD = 8, 64
NAW = HEADS * HD
E, EG, FF = 16, 4, 256
SG = 4
EPS = 1e-6
NEG = -1e30
PARTS = [(0, 2), (2, 5), (5, 6)]
PART_BLOCKS = [2 * k1 for _, k1 in PARTS]
SCALES, GAIN_KIND = (1, 4), {0: 1, 1: 4}
SIDE_LOADS = [6, 6, 3]
MAXOV = (2 * TOK - 3) // P
NTILE = E + MAXOV
RING_BANKS = 5
ADA_N = 6 * D // 512
COLS_T = P // GRID_R
KEY_START = [0, 64, 192, 256]
BIAS_TYPE = [0, 1, 1, 2]
BAND = 256
W0 = [16, 8, 0]

UNITS = [(hp, 0, par) for hp in range(4) for par in range(2)]
UNITS += [(hp, qt, par) for hp in range(4) for qt in range(1, TT) for par in range(2)]
NCTX = HEADS
LAG = 3
ADA_UNITS = [16, 28]
HALF = 512 // 2 + 1
RC_N = 306 + P + NTILE


TILE_STEPS = [("t", 0), ("p", 0), ("t", 1), ("t", 2), ("p", 1), ("t", 3), ("p", 2), ("t", 4), ("p", 3), ("p", 4)]


def plan_jobs():
    jobs = []

    def add(key, reader):
        jobs.append((key, reader))

    def out_and_router(layer):
        for t in range(TT):
            for b in range(2):
                add(("o", layer, t, b), "dve")
            if t >= 1:
                for h in range(2):
                    add(("r", layer, t - 1, h), "act")
        for h in range(2):
            add(("r", layer, TT - 1, h), "act")

    for h in range(2):
        add(("tc", h), "dve" if h else "act")
    for c in range(DC):
        add(("t", c), "act" if c % 2 else "dve")
    for blk in range(4):
        for t in range(TT):
            add(("p", 0, blk, t), "dve" if blk == 3 else "act")
    add(("fca",), "act")
    add(("fcb",), "dve")
    for m in range(4):
        add(("fa", m), "act")
        add(("fb", m), "dve")
        add(("fy", m - 1) if m else ("fcy",), "act")
    add(("fy", 3), "act")
    add(("kct",), "act")
    add(("qtc",), "dve")
    add(("ktc",), "act")
    for hp in range(4):
        add(("qt", hp), "dve")
        add(("kt", hp), "act")
    for u in range(len(UNITS)):
        add(("s", u), "act")
        if u >= LAG:
            add(("pt", u - LAG), "act")
    for u in range(len(UNITS) - LAG, len(UNITS)):
        add(("pt", u), "act")
    out_and_router(0)
    for step in TILE_STEPS:
        if step[0] == "t":
            for h in range(2):
                add(("tt", step[1], h), "dve" if h else "act")
        else:
            add(("p", 1, 2, step[1]), "act")
    for blk in (3, 1, 0):
        for t in range(TT):
            add(("p", 1, blk, t), "act")
    add(("ws",), "act")
    for t in range(TT):
        for b in range(2):
            add(("sp", t, b), "dve")
        if t >= 1:
            for h in range(2):
                add(("ut", t - 1, h), "act")
    for h in range(2):
        add(("ut", TT - 1, h), "act")
    out_and_router(1)
    return jobs


JOBS = plan_jobs()
JOB = {key: k for k, (key, _) in enumerate(JOBS)}


def build(nc, x_prompt, x_sample, cache_k, cache_v, c, c_ctx, ada_w, ada_b, norm1_g, norm2_g, na_w_in, na_w_out,
          q_gain, k_gain, rpb, sg_w_in, sg_w_out, sg_v_gain, sg_w_s, sg_b_s, router_w, router_b, moe_w_gate,
          moe_w_up, moe_w_down, dft, tables, mask, route_consts, scale_rows, y_prompt, y_sample, k_ctx, v_ctx):
    with ExitStack() as ctx:
        def sb(name, n):
            return ctx.enter_context(nc.sbuf_tensor(name, [P, n], F32))

        def sem(name):
            return ctx.enter_context(nc.semaphore(name))

        def dram(name, shape):
            return nc.dram_tensor(name, shape, F32, kind="Internal").ap()

        Xr, Hr, HTr = sb("x_res", TT * D), sb("h_tok", TT * D), sb("h_feat", DC * TOK)
        UV_N = 10240
        UV, RING, BZ, PS, SM = sb("uv", UV_N), sb("ring", 9 * 2048), sb("bz", 6144), sb("ps", 2560), sb("small", 472)

        X = Xr[:, :].rearrange("p (t d) -> p t d", t=TT)
        H = Hr[:, :].rearrange("p (t d) -> p t d", t=TT)
        HT = HTr[:, :].rearrange("p (c n) -> p c n", c=DC)

        H_FEAT, H_TOK, BCAST = 4, 5, 6

        def block(s):
            if s >= 4:
                a = {H_FEAT: HTr[:, 0:4096], H_TOK: Hr[:, 0:4096], BCAST: BZ[:, 2048:6144]}[s]
                return a.rearrange("p (c n) -> p c n", c=DC)
            return RING[:, 4096 * s:4096 * (s + 1)].rearrange("p (c n) -> p c n", c=DC)

        def xslot(s):
            return RING[:, 6144 * (2 - s):6144 * (3 - s)]

        at = [0]

        def small(n):
            at[0] += n
            assert at[0] <= 472
            return SM[:, at[0] - n:at[0]]

        ident = small(P)
        rw = small(DC * E).rearrange("p (c e) -> p c e", c=DC)
        mod1 = small(64).rearrange("p (l q k c) -> p l q k c", l=2, q=2, k=2)
        kgain_b = UV[:, 7500:7564]
        ss, ms, rs = small(TT), small(TT), small(TT)
        nhalf = small(1)
        gcol = small(2)
        rb = small(E)
        slot_i = small(2 * TT).bitcast(I32).rearrange("p (t s) -> p t s", t=TT)
        w12 = small(2 * TT).rearrange("p (s t) -> p s t", s=2)
        idx_i = small(NTILE).bitcast(I32)
        over_i = small(1 + MAXOV).bitcast(I32)
        bs = small(SG)
        cond = small(16).rearrange("p (q c) -> p q c", q=2)
        scond = small(16).rearrange("p (q c) -> p q c", q=2)
        plus1 = small(len(PARTS))

        def ada_row(layer, b):
            if layer == 0:
                return UV[0:2, 512 * b:512 * b + 512]
            if b < 2:
                return UV[0:2, 2560 + 512 * b:3072 + 512 * b]
            return PS[0:2, 1408 + 512 * (b % 2):1920 + 512 * (b % 2)]

        def fin_tile(layer, part):
            k0, k1 = PARTS[part]
            if layer == 0:
                a = UV[0:16 * (k1 - k0), 6144 + 384 * part:6528 + 384 * part]
            else:
                a = PS[0:16 * (k1 - k0), 1024:1408]
            return a.rearrange("p (k n) -> p k n", k=3)

        zeros = UV[:, 4992:5120]
        Z = UV[:, 0:4096].rearrange("p (h w) -> p h w", h=HEADS)
        mk = UV[:, 4096:4864].rearrange("p (y k r) -> p y k r", y=3, r=GRID_R)
        ZM = BZ[:, :].rearrange("p (h y k r) -> p h y k r", h=HEADS, y=3, r=GRID_R)
        junk = PS[:, 0:1024]
        V = UV[:, 0:2560].rearrange("p (t n) -> p t n", t=TT)
        U = UV[:, 2560:5120].rearrange("p (t n) -> p t n", t=TT)
        QT = UV[:, 5120:7680].rearrange("p (g n) -> p g n", g=4)
        KT = UV[:, 7680:10240].rearrange("p (g n) -> p g n", g=4)
        sq = [UV[:, 5120:5632], UV[:, 5632:6144]]
        ssq = UV[:, 6144:6224].rearrange("p (t h) -> p t h", t=TT)
        msq, rsq = UV[:, 6224:6304], UV[:, 6304:6384]
        kout = UV[:, 6464:6976]
        kraw = UV[:, 6976:7488]
        kcT, vc = PS[:, 0:512].rearrange("p (g n) -> p g n", g=4), PS[:, 512:1024]
        vs = PS[:, 1024:2560].rearrange("p (i n) -> p i n", i=3)
        pb = Hr[:, 0:384 * (LAG + 1)].rearrange("p (b n) -> p b n", b=LAG + 1)
        ptb = Hr[:, 1920:2688].rearrange("p (b n) -> p b n", b=2)
        nm, rsum, rinv = Hr[:, 4992:4996], Hr[:, 4996:5000], Hr[:, 5000:5004]
        fab = [KT[:, :, :].rearrange("p g n -> p (g n)")[:, 1024 * b:1024 * (b + 1)].rearrange("p (s n) -> p s n", s=2)
               for b in range(2)]
        V1 = UV[:, 0:5120].rearrange("p (t n) -> p t n", t=TT)
        U1 = UV[:, 5120:10240].rearrange("p (t n) -> p t n", t=TT)
        ws = PS[:, 0:512].rearrange("p (g n) -> p g n", g=SG)
        wst = PS[:, 512:1024].rearrange("p (g n) -> p g n", g=SG)
        vgain = PS[:, 1024:2048]
        sqv = Hr[:, 0:1024]
        ssv = Hr[:, 1024:1044]
        msv, rsv = Hr[:, 1044:1064], Hr[:, 1064:1084]
        g_b = BZ[:, 0:2048].rearrange("p (q n) -> p q n", q=2)
        sc_b = BZ[:, 2048:4096].rearrange("p (q n) -> p q n", q=2)
        sh_b = BZ[:, 4096:6144].rearrange("p (q n) -> p q n", q=2)
        tmp = [UV[:, 0:512], UV[:, 512:1024]]
        XG = UV[:, 0:3072].rearrange("p (b n) -> p b n", b=3)
        XT = UV[:, 3072:6144].rearrange("p (b c n) -> p b c n", b=3, c=DC)
        YO = UV[:, 6144:9216].rearrange("p (b n) -> p b n", b=3)
        silu_g, hid, hidT = UV[:, 9216:9472], UV[:, 9472:9728], UV[:, 9728:9984].rearrange("p (c n) -> p c n", c=2)
        def picked_rows(t):
            return UV[:, 2048 * t:2048 * (t + 1)].rearrange("p (s n) -> p s n", s=2)

        rc = UV[:, 6144:6144 + RC_N]
        triu, ones, tokid = rc[:, 0:128], rc[:, 128:256], rc[:, 256:261]
        rank4, rank16, e128, oi = rc[:, 261:265], rc[:, 265:281], rc[:, 281:297], rc[:, 297:306]
        iota, tile_lo = rc[:, 306:434], rc[:, 434:434 + NTILE]

        def onehots():
            return (UV[:, 2560:2560 + 2 * TT * NTILE].rearrange("p (k n) -> p k n", n=NTILE),
                    UV[:, 1280:2560].rearrange("p (k n) -> p k n", n=P))


        bank = [ctx.enter_context(nc.psum_tensor(f"bank{i}", [P, 512], F32)) for i in range(8)]

        raw_mod = [[dram(f"raw_mod{l}_{i}", (2, (k1 - k0) * D)) for i, (k0, k1) in enumerate(PARTS)] for l in range(2)]
        mod_parts = [[dram(f"mod{l}_{i}", (2, k1 - k0, D)) for i, (k0, k1) in enumerate(PARTS)] for l in range(2)]
        h2_rows = [dram(f"h2_rows{l}", (TOK, D)) for l in range(2)]
        y_rows = dram("y_rows", (NTILE * P, D))

        x_in = [sem(f"x_in{t}") for t in range(TT)]
        small_in = sem("small_in")
        cond_in = sem("cond_in")
        cond_silu = sem("cond_silu")
        block_in = [sem(f"block_in{s}") for s in range(7)]
        ada_mm, ada_read = sem("ada_mm"), sem("ada_read")
        fin_in, fin_done = sem("fin_in"), sem("fin_done")
        raw_stored = [[sem(f"raw_stored{i}_{j}") for j in range(2)] for i in range(len(PARTS))]
        mod_out = [sem(f"mod_out{i}") for i in range(len(PARTS))]
        fin_side = [sem(f"fin_side{i}") for i in range(len(PARTS))]
        mod1_in = sem("mod1_in")
        z_in, zm_done = sem("z_in"), sem("zm_done")
        y_zeroed = sem("y_zeroed")
        zero_set = sem("zero_set")
        job_done, job_read_act, job_read_dve = sem("job_done"), sem("job_read_act"), sem("job_read_dve")
        sumsq, meansq, rstd, normed = sem("sumsq"), sem("meansq"), sem("rstd"), sem("normed")
        x_mid, x_out = sem("x_mid"), sem("x_out")
        dve_step = sem("dve_step")
        qk_ss, qk_ms, qk_rs, qk_normed = sem("qk_ss"), sem("qk_ms"), sem("qk_rs"), sem("qk_normed")
        cache_in, v_shifted = sem("cache_in"), sem("v_shifted")
        kout_done, kv_out = sem("kout_done"), sem("kv_out")
        maxed, p_normed, pv_done, o_read = sem("maxed"), sem("p_normed"), sem("pv_done"), sem("o_read")
        bcast_in, bcast_g_in = sem("bcast_in"), sem("bcast_g_in")
        h2_ready, h2_stored = sem("h2_ready"), sem("h2_stored")
        logits_done, scored, picked, pos_done, routed = (sem("logits_done"), sem("scored"), sem("picked"),
                                                         sem("pos_done"), sem("routed"))
        rc_in, slots_onehot, idx_mm, idx_ready = sem("rc_in"), sem("slots_onehot"), sem("idx_mm"), sem("idx_ready")
        sg_in, v_done, v_ms, v_rs = sem("sg_in"), sem("v_done"), sem("v_ms"), sem("v_rs")
        qk_summed = sem("qk_summed")
        slots_set, rows_complete = sem("slots_set"), sem("rows_complete")
        v_normed, ring_free = sem("v_normed"), sem("ring_free")
        expert_in = [sem(f"expert_in{s}") for s in range(3)]
        gathered = [sem(f"gathered{s}") for s in range(3)]
        y_stored = [sem(f"y_stored{s}") for s in range(3)]
        xt_mm, xt_act, xt_dve = sem("xt_mm"), sem("xt_act"), sem("xt_dve")
        gu_mm, silu_done, hid_done = sem("gu_mm"), sem("silu_done"), sem("hid_done")
        hidT_mm, hidT_read, down_mm, y_act, y_dve = (sem("hidT_mm"), sem("hidT_read"), sem("down_mm"), sem("y_act"),
                                                    sem("y_dve"))
        OVN = ["gathered0", "gathered1", "gathered2", "in0", "in1", "in2", "xt_mm", "xt_act", "xt_dve", "gu_mm",
               "silu", "hid", "hidT_mm", "hidT_read", "down_mm", "y_act", "y_dve", "stored0", "stored1", "stored2", "landed"]
        ov = [{n: sem(f"ov{l}_{n}") for n in OVN} for l in range(2)]
        got = [sem(f"got{t}") for t in range(TT)]
        g_scaled = sem("g_scaled")
        out_done = sem("out_done")

        reads = {"act": 0, "dve": 0}
        read_after = []
        for _, reader in JOBS:
            reads[reader] += 1
            read_after.append((reader, reads[reader]))

        def wait_read(eng, key):
            reader, n = read_after[JOB[key]]
            eng.wait_ge(job_read_act if reader == "act" else job_read_dve, n)

        def jbank(key):
            return bank[JOB[key] % RING_BANKS]

        def job_free(pe, key):
            k = JOB[key]
            if k >= RING_BANKS:
                wait_read(pe, JOBS[k - RING_BANKS][0])

        def wait_job(eng, key):
            eng.wait_ge(job_done, JOB[key] + 1)

        def mod(layer, q, kind):
            part = 0 if kind < 2 else 1 if kind < 5 else 2
            k = kind - PARTS[part][0]
            return mod_parts[layer][part][q, k:k + 1, :]

        def wait_mod(eng, layer, part):
            eng.wait_ge(mod_out[part], 16 * (layer + 1))

        def cnd(t):
            return 0 if t == 0 else 1

        AFTER = [("in", 0, 0), ("in", 0, 1), ("in", 0, 2), ("in", 0, 3), ("dft",), ("tab",), ("out", 0, 0), ("out", 0, 1),
                 ("ada", 0), ("ada", 1), ("ada", 2), ("ada", 3), ("ada", 4), ("ada", 5),
                 ("ada", 6), ("ada", 7), ("ada", 8), ("ada", 9),
                 ("in", 1, 2), ("in", 1, 3), ("in", 1, 0), ("in", 1, 1), ("out", 1, 0), ("out", 1, 1),
                 ("ada", 10), ("ada", 11)]
        SLOT = [0, 1, 2, 3, 0, 1, 2, 3] + [0, 1, 0, 1, 0, H_FEAT] + [H_FEAT, H_TOK, H_FEAT, BCAST] + [2, 3, 0, 1, 2, 3] + [0, 0]
        place = {}
        loads = [ADA_N // 4] * 4 + [0, 0, 0]
        for key, s in zip(AFTER, SLOT):
            loads[s] += 1
            place[key] = (s, loads[s])

        def ada_bank(layer, b):
            if layer == 1 and b < 2:
                return bank[7]
            if layer == 1 and 6 <= b < 10:
                return bank[7 if b % 2 == 0 else 3]
            return bank[5 + b % 2] if layer == 0 else bank[5]

        def wait_block(eng, key):
            s, n = place[key]
            eng.wait_ge(block_in[s], 16 * n)

        def blk_ap(key):
            return block(place[key][0])

        ada_v = ada_w.rearrange("l (p c) (g u n) -> l g u p c n", c=DC, u=4, n=512)
        win_v = na_w_in[0].rearrange("(p c) (b n) -> b p c n", c=DC, n=512)
        wout_v = na_w_out[0].rearrange("(c p) (b n) -> b p c n", p=P, n=512)
        sgin_v = sg_w_in[0].rearrange("(p c) (b n) -> b p c n", c=DC, n=512)
        sgout_v = sg_w_out[0].rearrange("(c p) (b n) -> b p c n", p=P, n=512)

        def latent_out(cc):
            return HT[:, cc, P:TOK].rearrange("p (c r) -> p r c", r=GRID_R)

        def by_row(a):
            return a.rearrange("p (r c) -> p r c", r=GRID_R)

        def xsrc(t):
            return x_prompt[0] if t == 0 else x_sample[0, P * (t - 1):P * t, :]

        def ydst(t):
            return y_prompt[0] if t == 0 else y_sample[0, P * (t - 1):P * t, :]

        blk = ctx.enter_context(nc.Block())

        @blk.sync
        def _(sp):
            def load_block(key, src):
                s, n = place[key]
                sp.dma_start(block(s), src).then_inc(block_in[s], 16)

            def load_ada(b):
                load_block(("ada", b), ada_v[1, b // 4, b % 4])

            sp.dma_start(cond[:, 0, :], c_ctx.rearrange("(p c) -> p c", c=DC)).then_inc(cond_in, 16)
            sp.dma_start(cond[:, 1, :], c[0].rearrange("(p c) -> p c", c=DC)).then_inc(cond_in, 16)
            for u in range(4):
                sp.dma_start(block(u), ada_v[0, 0, u]).then_inc(block_in[u], 16)
            with sp.Fori(1, ADA_N // 4) as g:
                for u in range(4):
                    sp.wait_ge(ada_mm, 4 * g + u - 3)
                    sp.dma_start(block(u), ada_v[0, g, u]).then_inc(block_in[u], 16)

            for b in range(4):
                sp.wait_ge(ada_mm, ADA_N - 3 + b)
                load_block(("in", 0, b), win_v[b])
            wait_job(sp, ("p", 0, 0, TT - 1))
            s, _ = place[("dft",)]
            sp.dma_start(block(s)[:, :, 0:HALF], dft).then_inc(block_in[s], 16)
            wait_job(sp, ("p", 0, 1, TT - 1))
            s, _ = place[("tab",)]
            sp.dma_start(block(s)[:, 0, :], tables).then_inc(block_in[s], 16)
            for b in range(2):
                wait_job(sp, ("p", 0, 2 + b, TT - 1))
                load_block(("out", 0, b), wout_v[b])

            def load_expert(layer, e, s):
                w = xslot(s)
                sp.dma_start(w[:, 0:2048], moe_w_gate[layer].rearrange("e (p c) f -> e p (c f)", c=DC)[e])\
                    .then_inc(expert_in[s], 16)
                sp.dma_start(w[:, 2048:4096], moe_w_up[layer].rearrange("e (p c) f -> e p (c f)", c=DC)[e])\
                    .then_inc(expert_in[s], 16)
                sp.dma_start(w[:, 4096:6144], moe_w_down[layer].rearrange("e (p c) n -> e p (c n)", c=2)[e])\
                    .then_inc(expert_in[s], 16)

            for layer in range(2):
                if layer == 0:
                    wait_job(sp, ("fy", 3))
                    for b in range(4):
                        if b >= 2:
                            sp.wait_ge(ada_mm, ADA_N + b - 1)
                        load_ada(b)
                else:
                    wait_job(sp, ("p", 1, 0, TT - 1))
                    load_ada(10)
                if layer == 0:
                    sp.wait_ge(maxed, len(UNITS))
                else:
                    sp.wait_ge(h2_ready, TT)
                    sp.wait_ge(x_out, TT)
                if layer == 1:
                    wait_job(sp, ("ut", TT - 1, 1))
                sp.dma_start(rc, route_consts[:, 0:RC_N]).then_inc(rc_in, 16)
                wait_mod(sp, layer, 1)
                for q in range(2):
                    for dst, kind in ((g_b, 2), (sc_b, 4), (sh_b, 3)):
                        sp.dma_start(dst[:, q, :], mod(layer, q, kind).to_broadcast([P, D])).then_inc(bcast_in, 16)
                wait_job(sp, ("o", layer, TT - 1, 1))
                load_expert(layer, 0, 0)
                n = 4 if layer == 0 else 11
                sp.wait_ge(ada_mm, ADA_N + (3 if layer == 0 else 11))
                load_ada(n)
                if layer == 0:
                    sp.wait_ge(ada_mm, ADA_N + 4)
                load_expert(layer, 1, 1)
                if layer == 0:
                    sp.wait_ge(logits_done, 1)
                    load_ada(5)
                sp.wait_ge(ada_mm, ADA_N + n + 1)
                sp.wait_ge(idx_ready, layer + 1)
                load_expert(layer, 2, 2)

                def store_y(e, s):
                    base = E * layer
                    sp.wait_ge(y_act, base + e + 1)
                    sp.wait_ge(y_dve, base + e + 1)
                    sp.dma_start(y_rows.rearrange("(e p) n -> e p n", p=P)[e], YO[:, s, :])\
                        .then_inc(y_stored[s], 16)

                with sp.Fori(0, 4) as g:
                    for u in range(3):
                        sp.wait_ge(down_mm, E * layer + 3 * g + u + 1)
                        load_expert(layer, 3 * g + u + 3, u)
                        store_y(3 * g + u, u)
                sp.wait_ge(down_mm, E * layer + 13)
                load_expert(layer, 15, 0)
                store_y(12, 0)
                sp.wait_ge(x_mid, 2 * TT * (layer + 1))
                wait_mod(sp, layer, 2)
                for q in range(2):
                    sp.dma_start(g_b[:, q, :], mod(layer, q, 5).to_broadcast([P, D])).then_inc(bcast_g_in, 16)
                if layer == 0:
                    sp.wait_ge(ada_mm, ADA_N + 6)
                    load_ada(6)
                sp.wait_ge(routed, layer + 1)
                n_over = sp.value_load(over_i[0:1, 0:1], min_val=0, max_val=MAXOV)
                for o in range(MAXOV):
                    s = (o + 1) % 3
                    if o == 0:
                        store_y(13, 1)
                    elif o == 1:
                        store_y(14, 2)
                    elif o == 2:
                        sp.wait_ge(down_mm, E * layer + 16)
                        store_y(15, 0)
                    with sp.If(n_over > o):
                        ex = sp.value_load(over_i[0:1, o + 1:o + 2], min_val=0, max_val=E - 1)
                        if o >= 3:
                            sp.wait_ge(ov[layer]["down_mm"], o - 2)
                        w, arrived = xslot(s), ov[layer][f"in{s}"]
                        sp.dma_start(w[:, 0:2048], moe_w_gate[layer].rearrange("e (p c) f -> e p (c f)", c=DC)[ex])\
                            .then_inc(arrived, 16)
                        sp.dma_start(w[:, 2048:4096], moe_w_up[layer].rearrange("e (p c) f -> e p (c f)", c=DC)[ex])\
                            .then_inc(arrived, 16)
                        sp.dma_start(w[:, 4096:6144], moe_w_down[layer].rearrange("e (p c) n -> e p (c n)", c=2)[ex])\
                            .then_inc(arrived, 16)
                if layer == 0:
                    sp.wait_ge(h2_stored, 16 * TT)
                    load_ada(7)
                    sp.wait_ge(h2_ready, TT)
                    load_ada(9)
                    sp.wait_ge(ada_mm, ADA_N + 7)
                    load_ada(8)
                o_ = ov[layer]
                for s in range(3):
                    sp.wait_ge(y_stored[s], 16 * (6 if s == 0 else 5) * (layer + 1))
                sp.sem_inc(o_["landed"], 16)
                with sp.Fori(0, MAXOV // 3) as g:
                    for u in range(3):
                        o, s = 3 * g + u, (u + 1) % 3
                        with sp.If(n_over > o):
                            sp.wait_ge(o_["y_act"], o + 2)
                            sp.wait_ge(o_["y_dve"], o + 2)
                            sp.dma_start(y_rows[E * P:, :].rearrange("(g u p) n -> g u p n", u=3, p=P)[g, u],
                                         YO[:, s, :]).then_inc(o_["landed"], 16)
                            sp.wait_ge(o_["landed"], 16 * (o + 2))
                            sp.sem_inc(o_[f"stored{s}"], 1)
                if layer == 0:
                    sp.wait_ge(ring_free, 1)
                    for b in (2, 3, 1, 0):
                        if b == 2:
                            sp.wait_ge(got[0], 32)
                        if b == 3:
                            sp.wait_ge(got[TT - 1], 32)
                        load_block(("in", 1, b), sgin_v[b])
                    for b in range(2):
                        wait_job(sp, ("p", 1, 2 + b, TT - 1))
                        load_block(("out", 1, b), sgout_v[b])
            for t in range(TT):
                sp.wait_ge(x_out, TT + t + 1)
                sp.dma_start(ydst(t), X[:, t, :]).then_inc(out_done, 16)
            sp.wait_ge(out_done, 16 * TT)
            sp.wait_ge(kv_out, 32)

        @blk.gpsimd
        def _(pool):
            def rstd_of(k):
                t = k % TT
                pool.wait_ge(meansq, k + 1)
                nc.gpsimd.tensor_tensor(rs[:, t:t + 1], ms[:, t:t + 1], nhalf[:, :], ALU.pow).then_inc(rstd, 1)

            for k in range(TT):
                rstd_of(k)
            pool.wait_ge(qk_ms, 1)
            nc.gpsimd.tensor_tensor(rsq, msq, nhalf.to_broadcast([P, 80]), ALU.pow).then_inc(qk_rs, 1)

            for layer in range(2):
                if layer == 1:
                    for t in range(TT):
                        rstd_of(2 * TT + t)
                    pool.wait_ge(v_ms, 1)
                    nc.gpsimd.tensor_tensor(rsv, msv, nhalf.to_broadcast([P, 20]), ALU.pow).then_inc(v_rs, 1)
                for t in range(TT):
                    rstd_of((2 * layer + 1) * TT + t)
                    n = TT * layer + t
                    pool.wait_ge(h2_ready, n + 1)
                    pool.dma_start(h2_rows[layer][P * t:P * (t + 1), :], H[:, t, :]).then_inc(h2_stored, 16)
                pool.wait_ge(idx_ready, layer + 1)
                pool.wait_ge(h2_stored, 16 * TT * (layer + 1))

                def gather(e, s, signal):
                    nc.gpsimd.indirect_dma_start(
                        out=XG[:, s, :], out_offset=None, in_=h2_rows[layer][:, :],
                        in_offset=bass.IndirectOffsetOnAxis(ap=idx_i[:, e:e + 1], axis=0)).then_inc(signal, 16)

                for e in range(E):
                    if e >= 3:
                        pool.wait_ge(xt_mm, E * layer + e - 2)
                    gather(e, e % 3, gathered[e % 3])
                pool.wait_ge(routed, layer + 1)
                n_over = pool.value_load(over_i[0:1, 0:1], min_val=0, max_val=MAXOV)
                pool.wait_ge(xt_mm, E * (layer + 1))
                for o in range(MAXOV):
                    s = (o + 1) % 3
                    with pool.If(n_over > o):
                        if o >= 3:
                            pool.wait_ge(ov[layer]["xt_mm"], o - 2)
                        gather(E + o, s, ov[layer][f"gathered{s}"])
                pool.wait_ge(slots_set, layer + 1)
                pool.wait_ge(ov[layer]["landed"], n_over * 16 + 16)
                pool.sem_inc(rows_complete, 1)
                for t in range(TT):
                    for k in range(2):
                        nc.gpsimd.indirect_dma_start(
                            out=picked_rows(t)[:, k, :], out_offset=None, in_=y_rows[:, :],
                            in_offset=bass.IndirectOffsetOnAxis(ap=slot_i[:, t, k:k + 1], axis=0))\
                            .then_inc(got[t], 16)

        @blk.scalar
        def _(act):
            def square_sum(k):
                t = k % TT
                if k:
                    act.wait_ge(sumsq, k)
                nc.scalar.activation(junk, X[:, t, :], ACT.Square, accum_out=ss[:, t:t + 1]).then_inc(sumsq, 1)

            act.dma_start(ident, route_consts[:, RC_N:RC_N + P]).then_inc(small_in, 16)
            act.dma_start(plus1[0:48, :], scale_rows).then_inc(small_in, 16)
            act.wait_ge(cond_in, 32)
            nc.scalar.activation(scond, cond, ACT.Silu).then_inc(cond_silu, 1)
            act.dma_start(rw, router_w.rearrange("(p c) e -> p c e", c=DC)).then_inc(small_in, 16)
            act.dma_start(kgain_b, k_gain[0:1, :].to_broadcast([P, HD])).then_inc(small_in, 16)
            act.dma_start(rb, router_b.rearrange("(o e) -> o e", o=1).to_broadcast([P, E])).then_inc(small_in, 16)
            for half in range(2):
                act.dma_start(gcol[64 * half:64 * half + 64, 0:1], q_gain.rearrange("o (d i) -> (o d) i", i=1))\
                    .then_inc(small_in, 16)
                act.dma_start(gcol[64 * half:64 * half + 64, 1:2], k_gain.rearrange("o (d i) -> (o d) i", i=1))\
                    .then_inc(small_in, 16)
            def fin_sides(layer, part):
                k0, k1 = PARTS[part]
                f, n = fin_tile(layer, part), 8 * (k1 - k0)
                for q in range(2):
                    act.dma_start(f[n * q:n * q + n, 1, :], ada_b[layer, D * k0:D * k1].rearrange("(k n) -> k n", n=P))\
                        .then_inc(fin_side[part], 16)
                    if part in GAIN_KIND:
                        plain = 8 * (GAIN_KIND[part] - k0)
                        g = (norm1_g, norm2_g)[part]
                        act.dma_start(f[n * q:n * q + plain, 2, :], route_consts[0:plain, 128:256])\
                            .then_inc(fin_side[part], 16)
                        act.dma_start(f[n * q + plain:n * q + n, 2, :], g[layer].rearrange("(k n) -> k n", n=P))\
                            .then_inc(fin_side[part], 16)
                if part not in GAIN_KIND:
                    act.dma_start(f[:, 2, :], route_consts[0:2 * n, 128:256]).then_inc(fin_side[part], 16)

            def read_ada(layer, b):
                n = ADA_N * layer + b
                part = [b < e for e in PART_BLOCKS].index(True)
                at_ = 512 * b - D * PARTS[part][0]
                if layer == 1 and 4 <= b < 10:
                    if b < 6:
                        act.wait_ge(raw_stored[0][b % 2], 16 * 4)
                    else:
                        act.wait_ge(raw_stored[1][b % 2], 16 * (3 + (b - 4) // 2))
                act.wait_ge(ada_mm, n + 1)
                nc.scalar.activation(ada_row(layer, b), ada_bank(layer, b)[0:2, :], ACT.Copy).then_inc(ada_read, 1)
                act.wait_ge(ada_read, n + 1)
                act.dma_start(raw_mod[layer][part][:, at_:at_ + 512], ada_row(layer, b))\
                    .then_inc(raw_stored[part][b % 2], 16)

            def reload_rows(layer, part):
                for j in range(2):
                    act.wait_ge(raw_stored[part][j], 16 * (PARTS[part][1] - PARTS[part][0]) * (layer + 1))
                act.dma_start(fin_tile(layer, part)[:, 0, :],
                              raw_mod[layer][part].rearrange("q (k n) -> (q k) n", n=P)).then_inc(fin_in, 16)

            def store_mod(layer, part):
                act.wait_ge(fin_done, len(PARTS) * layer + part + 1)
                act.dma_start(mod_parts[layer][part].rearrange("q k (b n) -> (q k b) n", n=P),
                              fin_tile(layer, part)[:, 0, :]).then_inc(mod_out[part], 16)

            def load_mod1(layer):
                wait_mod(act, layer, 0)
                for q in range(2):
                    act.dma_start(mod1[:, layer, q, :, :],
                                  mod_parts[layer][0][q].rearrange("k (p c) -> p k c", c=DC)).then_inc(mod1_in, 16)

            for part in range(len(PARTS)):
                fin_sides(0, part)
            for b in range(ADA_N):
                if b < TT:
                    act.dma_start(X[:, b, :], xsrc(b)).then_inc(x_in[b], 16)
                if 2 <= b < 2 + TT:
                    act.wait_ge(x_in[b - 2], 16)
                    square_sum(b - 2)
                if 2 + TT <= b < 2 + 2 * TT:
                    t = b - 2 - TT
                    act.wait_ge(rstd, t + 1)
                    nc.scalar.activation(H[:, t, :], X[:, t, :], ACT.Copy, scale=rs[:, t:t + 1]).then_inc(normed, 1)
                read_ada(0, b)
                if b == 5:
                    reload_rows(0, 0)
                if b == 7:
                    store_mod(0, 0)
                if b == 9:
                    load_mod1(0)
                if b == 11:
                    reload_rows(0, 1)

            def read_tile(layer, key, t):
                act.wait_ge(mod1_in, 32 * (layer + 1))
                wait_job(act, key)
                for c in range(4):
                    ins = nc.scalar.activation(HT[:, c, P * t:P * (t + 1)], jbank(key)[:, P * c:P * (c + 1)],
                                               ACT.Identity, bias=mod1[:, layer, cnd(t), 0, c:c + 1],
                                               scale=mod1[:, layer, cnd(t), 1, c:c + 1])
                ins.then_inc(job_read_act, 1)

            def read_transposes():
                read_tile(0, ("tc", 0), 0)
                for c in range(1, DC, 2):
                    key = ("t", c)
                    wait_job(act, key)
                    nc.scalar.activation(latent_out(c), by_row(jbank(key)[:, :]), ACT.Identity,
                                         bias=mod1[:, 0, 1, 0, c:c + 1],
                                         scale=mod1[:, 0, 1, 1, c:c + 1]).then_inc(job_read_act, 1)

            def copy_job(key, out, in_=None):
                wait_job(act, key)
                nc.scalar.activation(out, jbank(key)[:, :] if in_ is None else in_, ACT.Copy).then_inc(job_read_act, 1)

            def out_and_norm(layer):
                def scale_rows_of(t):
                    k = (2 * layer + 1) * TT + t
                    act.wait_ge(rstd, k + 1)
                    nc.scalar.activation(H[:, t, :], X[:, t, :], ACT.Copy, scale=rs[:, t:t + 1]).then_inc(normed, 1)

                def router_rows(t):
                    for h in range(2):
                        key = ("r", layer, t, h)
                        copy_job(key, HT[:, 4 * h:4 * h + 4, P * t:P * (t + 1)],
                                 jbank(key)[:, :].rearrange("p (c n) -> p c n", c=4))

                for t in range(TT):
                    act.wait_ge(x_mid, 2 * TT * layer + 2 * (t + 1))
                    square_sum((2 * layer + 1) * TT + t)
                    scale_rows_of(t)
                    if t:
                        router_rows(t - 1)
                first = 2 if layer == 0 else 10
                if layer == 0:
                    for j in range(2):
                        act.wait_ge(raw_stored[0][j], 16 * 3)
                read_ada(1, first)
                router_rows(TT - 1)
                act.wait_ge(logits_done, layer + 1)
                nc.scalar.activation(UV[:, 0:80], bank[7][:, 0:80], ACT.Sigmoid).then_inc(scored, 1)
                for b in range(3, 6) if layer == 0 else (11,):
                    read_ada(1, b)
                fin_sides(1, 0 if layer == 0 else 2)
                reload_rows(1, 0 if layer == 0 else 2)

            def experts(layer):
                def read_xt(e, b, n):
                    act.wait_ge(xt_mm, n)
                    nc.scalar.activation(XT[:, b, 0:4, :], bank[0][:, :].rearrange("p (c n) -> p c n", c=4), ACT.Copy)\
                        .then_inc(xt_act, 1)

                def body(e, b, last, stored):
                    base = E * layer
                    act.wait_ge(gu_mm, base + e + 1)
                    nc.scalar.activation(silu_g, bank[2][:, 0:FF], ACT.Silu).then_inc(silu_done, 1)
                    if not last:
                        read_xt(e + 1, (b + 1) % 3, base + e + 2)
                    act.wait_ge(hidT_mm, base + e + 1)
                    nc.scalar.activation(hidT, bank[4][:, 0:FF].rearrange("p (c n) -> p c n", c=2), ACT.Copy)\
                        .then_inc(hidT_read, 1)
                    if stored is not None:
                        act.wait_ge(y_stored[b], stored)
                    act.wait_ge(down_mm, base + e + 1)
                    nc.scalar.activation(YO[:, b, 0:512], bank[5][:, :], ACT.Copy).then_inc(y_act, 1)

                read_xt(0, 0, E * layer + 1)
                for e in range(3):
                    body(e, e, False, None)
                store_mod(1, 0 if layer == 0 else 2)
                if layer == 0:
                    load_mod1(1)
                    fin_sides(1, 1)
                with act.Fori(1, 5) as g:
                    for u in range(3):
                        body(3 * g + u, u, False, 16 * (6 if u == 0 else 5) * layer + 16 * g)
                body(15, 0, True, 16 * 6 * layer + 16 * 5)
                if layer == 0:
                    read_ada(1, 6)
                o_ = ov[layer]
                act.sem_inc(o_["y_act"], 1)
                for s in range(3):
                    act.wait_ge(y_stored[s], 16 * (6 if s == 0 else 5) * (layer + 1))
                for s in range(3):
                    act.sem_inc(o_[f"stored{s}"], 1)
                act.wait_ge(routed, layer + 1)
                n_over = act.value_load(over_i[0:1, 0:1], min_val=0, max_val=MAXOV)

                def read_xt_over(n, s):
                    act.wait_ge(o_["xt_mm"], n)
                    nc.scalar.activation(XT[:, s, 0:4, :], bank[0][:, :].rearrange("p (c n) -> p c n", c=4),
                                         ACT.Copy).then_inc(o_["xt_act"], 1)

                with act.If(n_over > 0):
                    read_xt_over(1, 1)
                with act.Fori(0, MAXOV // 3) as g:
                    for u in range(3):
                        o, s = 3 * g + u, (u + 1) % 3
                        with act.If(n_over > o):
                            act.wait_ge(o_["gu_mm"], o + 1)
                            nc.scalar.activation(silu_g, bank[2][:, 0:FF], ACT.Silu).then_inc(o_["silu"], 1)
                            with act.If(n_over > o + 1):
                                read_xt_over(o + 2, (s + 1) % 3)
                            act.wait_ge(o_["hidT_mm"], o + 1)
                            nc.scalar.activation(hidT, bank[4][:, 0:FF].rearrange("p (c n) -> p c n", c=2), ACT.Copy)\
                                .then_inc(o_["hidT_read"], 1)
                            act.wait_ge(o_[f"stored{s}"], g + 1)
                            act.wait_ge(o_["down_mm"], o + 1)
                            nc.scalar.activation(YO[:, s, 0:512], bank[5][:, :], ACT.Copy).then_inc(o_["y_act"], 1)

            def scale_first(layer, t):
                act.wait_ge(got[t], 32 * (layer + 1))
                y1 = picked_rows(t)[:, 0, :]
                nc.scalar.activation(y1, y1, ACT.Copy, scale=w12[:, 0, t:t + 1]).then_inc(g_scaled, 1)

            read_transposes()
            for b in range(2):
                for t in range(TT):
                    n = TT * b + t
                    if n == 0:
                        for j in range(2):
                            act.wait_ge(raw_stored[2][j], 16)
                    if n == 2:
                        store_mod(0, 1)
                        reload_rows(0, 2)
                        act.dma_start(mk.rearrange("p y k r -> p (y k r)"), mask).then_inc(z_in, 16)
                        for qc in range(COLS_T):
                            skewed = bass.AP(tensor=rpb.tensor, offset=qc, ap=[[64, GRID_R], [15 * 64, HEADS], [1, 496]])
                            act.dma_start(Z[GRID_R * qc:GRID_R * (qc + 1), :, 0:496], skewed).then_inc(z_in, 16)
                    if n == 5:
                        store_mod(0, 2)
                    key = ("p", 0, b, t)
                    wait_job(act, key)
                    if n >= 2:
                        act.wait_ge(qk_summed, n - 1)
                    nc.scalar.activation(sq[n % 2], jbank(key)[:, :], ACT.Square).then_inc(qk_ss, 1)
                    nc.scalar.activation(H[:, t, 512 * b:512 * b + 512], jbank(key)[:, :], ACT.Copy)\
                        .then_inc(job_read_act, 1)
            act.wait_ge(zm_done, 1)
            for t in range(TT):
                copy_job(("p", 0, 2, t), V[:, t, :])
                if t == 0:
                    wait_read(act, ("p", 0, 2, 0))
                    act.dma_start(v_ctx.rearrange("b o s h d -> (b o s) (h d)"), V[:, 0, :]).then_inc(kv_out, 16)
            wait_read(act, ("p", 0, 2, TT - 1))
            wait_mod(act, 0, 1)
            wait_mod(act, 0, 2)
            act.dma_start(kraw, cache_k.rearrange("b o s h d -> (b o s) (h d)")).then_inc(cache_in, 16)
            act.dma_start(vc, cache_v.rearrange("b o s h d -> (b o s) (h d)")).then_inc(cache_in, 16)
            for i in range(3):
                act.dma_start(vs[0:64, i, :], V[64:128, 1 + i, :]).then_inc(v_shifted, 16)
                act.dma_start(vs[64:128, i, :], V[0:64, 2 + i, :]).then_inc(v_shifted, 16)
            act.wait_ge(kout_done, 1)
            act.dma_start(k_ctx.rearrange("b o s h d -> (b o s) (h d)"), kout).then_inc(kv_out, 16)
            copy_job(("fca",), fab[0][:, 0, :])
            for m in range(4):
                if m:
                    wait_job(act, ("fy", m - 2) if m >= 2 else ("fcy",))
                sums, out = jbank(("fa", m)), fab[(m + 1) % 2][:, 0, :]
                wait_job(act, ("fa", m))
                nc.scalar.activation(out[:, 0:HALF], sums[:, 0:HALF], ACT.Copy)
                nc.scalar.activation(out[:, HALF:512], sums[:, HALF - 2:0:-1], ACT.Copy).then_inc(job_read_act, 1)
                if m == 0:
                    key = ("fcy",)
                    copy_job(key, HT[:, 4:8, 0:P], jbank(key)[:, :].rearrange("p (c n) -> p c n", c=4))
                else:
                    copy_job(("fy", m - 1), HT[:, 4 + m - 1, P:TOK])
            copy_job(("fy", 3), HT[:, 7, P:TOK])
            copy_job(("kct",), kcT, jbank(("kct",))[:, :].rearrange("p (g n) -> p g n", g=4))
            act.wait_ge(kv_out, 32)
            key = ("ktc",)
            wait_job(act, key)
            nc.scalar.activation(KT[:, :, 0:P], jbank(key)[:, :].rearrange("p (g n) -> p g n", g=4), ACT.Copy,
                                 scale=gcol[:, 1:2]).then_inc(job_read_act, 1)
            for hp in range(4):
                key = ("kt", hp)
                wait_job(act, key)
                nc.scalar.activation(KT[:, hp, P:TOK], jbank(key)[:, :], ACT.Copy, scale=gcol[:, 1:2])\
                    .then_inc(job_read_act, 1)

            def read_pt(u):
                w = P if u < NCTX else 3 * P
                if u >= 2:
                    act.wait_ge(pv_done, u - 1)
                copy_job(("pt", u), ptb[:, u % 2, 0:w], jbank(("pt", u))[:, 0:w])

            act.wait_ge(zero_set, 1)
            act.dma_start(y_rows[E * P:, :].rearrange("(p o) (b n) -> p (o b) n", p=P, n=P),
                          zeros.unsqueeze(1).to_broadcast([P, MAXOV * DC, P])).then_inc(y_zeroed, 16)
            for u in range(len(UNITS)):
                w = P if u < NCTX else 3 * P
                key = ("s", u)
                if u - 1 in ADA_UNITS:
                    read_ada(1, ADA_UNITS.index(u - 1))
                act.wait_ge(maxed, u + 1)
                if u > LAG:
                    wait_job(act, ("pt", u - LAG - 1))
                nc.scalar.activation(pb[:, u % (LAG + 1), 0:w], jbank(key)[:, 0:w], ACT.Exp, bias=nm[:, u % 4:u % 4 + 1],
                                     accum_out=rsum[:, u % 4:u % 4 + 1]).then_inc(job_read_act, 1)
                if u >= LAG:
                    read_pt(u - LAG)
            for u in range(len(UNITS) - LAG, len(UNITS)):
                read_pt(u)
            out_and_norm(0)
            act.wait_ge(y_zeroed, 16)
            experts(0)

            def norm_rows(t):
                act.wait_ge(x_out, t + 1)
                square_sum(2 * TT + t)
                act.wait_ge(rstd, 2 * TT + t + 1)
                nc.scalar.activation(H[:, t, :], X[:, t, :], ACT.Copy, scale=rs[:, t:t + 1]).then_inc(normed, 1)

            def gelu(b, t):
                key = ("p", 1, b, t)
                dst = V1 if b >= 2 else U1
                wait_job(act, key)
                nc.scalar.activation(dst[:, t, 512 * (b % 2):512 * (b % 2) + 512], jbank(key)[:, :],
                                     ACT.Gelu_apprx_tanh).then_inc(job_read_act, 1)

            read_ada(1, 7)
            read_ada(1, 8)
            scale_first(0, 0)
            read_ada(1, 9)
            scale_first(0, 1)
            norm_rows(0)
            scale_first(0, 2)
            read_tile(1, ("tt", 0, 0), 0)
            reload_rows(1, 1)
            norm_rows(1)
            scale_first(0, 3)
            norm_rows(2)
            scale_first(0, 4)
            gelu(2, 0)
            read_tile(1, ("tt", 1, 0), 1)
            read_tile(1, ("tt", 2, 0), 2)
            norm_rows(3)
            gelu(2, 1)
            read_tile(1, ("tt", 3, 0), 3)
            norm_rows(4)
            gelu(2, 2)
            read_tile(1, ("tt", 4, 0), 4)
            gelu(2, 3)
            gelu(2, 4)
            store_mod(1, 1)
            act.wait_ge(sumsq, 3 * TT)
            act.dma_start(ws, sg_w_s[0].rearrange("g p q -> p g q")).then_inc(sg_in, 16)
            wait_mod(act, 1, 1)
            act.dma_start(vgain, sg_v_gain[0:1, :].to_broadcast([P, D])).then_inc(sg_in, 16)
            with nc.allow_non_contiguous_dma(reason="512 scalars, one per partition and group"):
                act.dma_start(bs, sg_b_s[0].rearrange("g p -> p g")).then_inc(sg_in, 16)
            for b in (3, 1, 0):
                for t in range(TT):
                    gelu(b, t)
            copy_job(("ws",), wst, jbank(("ws",))[:, :].rearrange("p (g n) -> p g n", g=SG))
            for t in range(TT):
                for h in range(2):
                    key = ("ut", t, h)
                    copy_job(key, HT[:, 4 * h:4 * h + 4, P * t:P * (t + 1)],
                             jbank(key)[:, :].rearrange("p (c n) -> p c n", c=4))
            out_and_norm(1)
            experts(1)
            for t in range(TT):
                scale_first(1, t)

        @blk.vector
        def _(dve):
            steps = [0]

            def link(ins):
                steps[0] += 1
                ins.then_inc(dve_step, 1)
                dve.wait_ge(dve_step, steps[0])

            link(nc.vector.memset(nhalf, -0.5))

            def mean_square(k):
                t = k % TT
                dve.wait_ge(sumsq, k + 1)
                nc.vector.tensor_scalar(ms[:, t:t + 1], ss[:, t:t + 1], 1.0 / D, EPS, ALU.mult, ALU.add)\
                    .then_inc(meansq, 1)

            dve.wait_ge(small_in, 16 * 9)
            link(nc.vector.tensor_scalar(gcol[:, 0:1], gcol[:, 0:1], HD ** -0.5, None, ALU.mult))

            def finish_rows(layer, part):
                dve.wait_ge(fin_side[part], 16 * SIDE_LOADS[part] * (layer + 1))
                dve.wait_ge(fin_in, 16 * (len(PARTS) * layer + part + 1))
                f = fin_tile(layer, part)
                link(nc.vector.tensor_tensor(f[:, 0, :], f[:, 0, :], f[:, 1, :], ALU.add))
                nc.vector.scalar_tensor_tensor(f[:, 0, :], f[:, 0, :], plus1[0:f.shape[0], part:part + 1], f[:, 2, :],
                                               ALU.add, ALU.mult).then_inc(fin_done, 1)

            for t in range(TT):
                mean_square(t)
            finish_rows(0, 0)

            def read_tile(layer, key, t):
                dve.wait_ge(mod1_in, 32 * (layer + 1))
                wait_job(dve, key)
                for c in range(4):
                    ins = nc.vector.tensor_scalar(HT[:, 4 + c, P * t:P * (t + 1)], jbank(key)[:, P * c:P * (c + 1)],
                                                  mod1[:, layer, cnd(t), 1, 4 + c:5 + c],
                                                  mod1[:, layer, cnd(t), 0, 4 + c:5 + c], ALU.mult, ALU.add)
                ins.then_inc(job_read_dve, 1)

            def read_transposes():
                read_tile(0, ("tc", 1), 0)
                for c in range(0, DC, 2):
                    key = ("t", c)
                    wait_job(dve, key)
                    nc.vector.tensor_scalar(latent_out(c), by_row(jbank(key)[:, :]), mod1[:, 0, 1, 1, c:c + 1],
                                            mod1[:, 0, 1, 0, c:c + 1], ALU.mult, ALU.add).then_inc(job_read_dve, 1)

            def out_and_norm(layer):
                for t in range(TT):
                    for b in range(2):
                        key = ("o", layer, t, b)
                        cols = slice(512 * b, 512 * b + 512)
                        dve.wait_ge(bcast_in, 96 * (layer + 1))
                        wait_job(dve, key)
                        nc.vector.tensor_tensor(tmp[b], jbank(key)[:, :], g_b[:, cnd(t), cols], ALU.mult)\
                            .then_inc(job_read_dve, 1)
                        wait_read(dve, key)
                        nc.vector.tensor_tensor(X[:, t, cols], X[:, t, cols], tmp[b], ALU.add).then_inc(x_mid, 1)
                        dve.wait_ge(x_mid, 2 * TT * layer + 2 * t + b + 1)
                    k = (2 * layer + 1) * TT + t
                    mean_square(k)
                    dve.wait_ge(normed, k + 1)
                    link(nc.vector.tensor_tensor(H[:, t, :], H[:, t, :], sc_b[:, cnd(t), :], ALU.mult))
                    nc.vector.tensor_tensor(H[:, t, :], H[:, t, :], sh_b[:, cnd(t), :], ALU.add).then_inc(h2_ready, 1)

            def route(layer):
                def tmp80(i):
                    return UV[:, 80 * i:80 * i + 80]

                def te(i):
                    return tmp80(i).rearrange("p (t e) -> p t e", t=TT)

                def tg(i):
                    return tmp80(i).rearrange("p (g j) -> p g j", j=4)

                def red(out, in_, op=ALU.max):
                    link(nc.vector.tensor_reduce(out, in_, AX, op))

                def bc(a, n):
                    return a.unsqueeze(2).to_broadcast([P, a.shape[1], n])

                def row(a, n):
                    return a.unsqueeze(1).to_broadcast([P, n, a.shape[1]])

                def tt(out, a, b, op):
                    link(nc.vector.tensor_tensor(out, a, b, op))

                dve.wait_ge(scored, layer + 1)
                dve.wait_ge(rc_in, 16 * (layer + 1))
                score, sel = te(0), te(1)
                tt(sel, score, row(rb, TT), ALU.add)
                v = tg(1)
                pairs = UV[:, 160:280].rearrange("p (g j) -> p g j", j=6)
                tt(pairs[:, :, 0:3], v[:, :, 0:3], v[:, :, 1:4], ALU.add)
                tt(pairs[:, :, 3:5], v[:, :, 0:2], v[:, :, 2:4], ALU.add)
                tt(pairs[:, :, 5:6], v[:, :, 0:1], v[:, :, 3:4], ALU.add)
                gs, gmax, gpick = UV[:, 280:300], UV[:, 300:305], UV[:, 305:325]
                red(gs, pairs)
                gs3, gp3 = gs.rearrange("p (t g) -> p t g", g=4), gpick.rearrange("p (t g) -> p t g", g=4)
                red(gmax, gs3)
                tt(gp3, gs3, bc(gmax, 4), ALU.is_equal)
                tt(gp3, gp3, row(rank4, TT), ALU.mult)
                red(gmax, gp3)
                tt(gp3, gp3, bc(gmax, 4), ALU.is_equal)
                off = UV[:, 325:345]
                link(nc.vector.tensor_scalar(off, gpick, -NEG, NEG, ALU.mult, ALU.add))
                tt(v, v, bc(gpick, 4), ALU.mult)
                tt(v, v, bc(off, 4), ALU.add)
                m5 = UV[:, 345:350]
                picks = [te(5), te(6)]
                for k in range(2):
                    red(m5, sel)
                    tt(picks[k], sel, bc(m5, E), ALU.is_equal)
                    tt(picks[k], picks[k], row(rank16, TT), ALU.mult)
                    red(m5, picks[k])
                    tt(picks[k], picks[k], bc(m5, E), ALU.is_equal)
                    if k == 0:
                        link(nc.vector.scalar_tensor_tensor(sel, picks[0], 2 * NEG, sel, ALU.mult, ALU.add))
                both = te(7)
                nc.vector.tensor_tensor(both, picks[0], picks[1], ALU.add).then_inc(picked, 1)
                prod = te(8)
                for k in range(2):
                    tt(prod, picks[k], score, ALU.mult)
                    red(w12[:, k, :], prod, ALU.add)
                wsum = UV[:, 350:355]
                tt(wsum, w12[:, 0, :], w12[:, 1, :], ALU.add)
                link(nc.vector.reciprocal(wsum, wsum))
                tt(w12, w12, row(wsum, 2), ALU.mult)
                dve.wait_ge(pos_done, layer + 1)
                pos, cnt = te(9), UV[:, 800:816]
                link(nc.vector.tensor_copy(UV[:, 720:816], bank[6][:, 0:96]))
                ovf, inc, one16 = UV[:, 816:832], UV[:, 832:848], UV[:, 848:864]
                link(nc.vector.memset(one16, 1.0))
                link(nc.vector.tensor_scalar(ovf, cnt, P + 0.5, None, ALU.is_gt))
                for k in range(2, TT):
                    link(nc.vector.scalar_tensor_tensor(ovf, cnt, k * P + 0.5, ovf, ALU.is_gt, ALU.add))
                link(nc.vector.tensor_tensor_scan(inc, one16, ovf, 0.0, ALU.mult, ALU.add))
                delta = UV[:, 864:880]
                tt(delta, inc, ovf, ALU.subtract)
                link(nc.vector.tensor_scalar(delta, delta, float(P), float((E - 1) * P), ALU.mult, ALU.add))
                tt(delta, delta, e128, ALU.subtract)
                big, rowno = te(11), te(12)
                link(nc.vector.tensor_scalar(big, pos, P - 0.5, None, ALU.is_gt))
                tt(big, big, row(delta, TT), ALU.mult)
                tt(big, big, pos, ALU.add)
                tt(rowno, big, row(e128, TT), ALU.add)
                sl = UV[:, 1040:1050].rearrange("p (s t) -> p s t", s=2)
                for k in range(2):
                    tt(prod, picks[k], rowno, ALU.mult)
                    red(sl[:, k, :], prod, ALU.add)
                nc.vector.tensor_copy(slot_i, sl.rearrange("p s t -> p t s")).then_inc(slots_set, 1)
                s10, hi, lo = UV[:, 1040:1050], UV[:, 1210:1220], UV[:, 1220:1230]
                tile_oh, place_oh = onehots()
                tt(tile_oh, bc(s10, NTILE), row(tile_lo, 2 * TT), ALU.is_ge)
                red(hi, tile_oh, ALU.add)
                link(nc.vector.tensor_scalar(hi, hi, -1.0, None, ALU.add))
                link(nc.vector.scalar_tensor_tensor(lo, hi, -float(P), s10, ALU.mult, ALU.add))
                tt(place_oh, bc(lo, P), row(iota, 2 * TT), ALU.is_equal)
                link(nc.vector.tensor_scalar(hi, hi, float(P), None, ALU.mult))
                tt(tile_oh, bc(hi, NTILE), row(tile_lo, 2 * TT), ALU.is_equal)
                toks = tokid.unsqueeze(1).unsqueeze(3).to_broadcast([P, 2, TT, NTILE])
                oh4 = tile_oh.rearrange("p (s t) n -> p s t n", s=2)
                nc.vector.tensor_tensor(oh4, oh4, toks, ALU.mult).then_inc(slots_onehot, 1)
                le = UV[:, 1056:1200].rearrange("p (o e) -> p o e", o=MAXOV)
                ovx = UV[:, 1200:1200 + MAXOV + 1]
                tt(le, row(inc, MAXOV), bc(oi, E), ALU.is_le)
                red(ovx[:, 1:1 + MAXOV], le, ALU.add)
                link(nc.vector.tensor_scalar(ovx[:, 1:1 + MAXOV], ovx[:, 1:1 + MAXOV], float(E - 1), None, ALU.min))
                link(nc.vector.tensor_copy(ovx[:, 0:1], inc[:, E - 1:E]))
                nc.vector.tensor_copy(over_i, ovx).then_inc(routed, 1)
                dve.wait_ge(idx_mm, layer + 1)
                nc.vector.tensor_copy(idx_i, bank[6][:, 128:128 + NTILE]).then_inc(idx_ready, 1)

            def experts(layer):
                base = E * layer

                def read_xt(b, n):
                    dve.wait_ge(xt_mm, n)
                    nc.vector.tensor_copy(XT[:, b, 4:8, :], bank[1][:, :].rearrange("p (c n) -> p c n", c=4))\
                        .then_inc(xt_dve, 1)

                def body(e, b, last, stored):
                    dve.wait_ge(silu_done, base + e + 1)
                    nc.vector.tensor_tensor(hid, silu_g, bank[2][:, FF:2 * FF], ALU.mult).then_inc(hid_done, 1)
                    if not last:
                        read_xt((b + 1) % 3, base + e + 2)
                    if stored is not None:
                        dve.wait_ge(y_stored[b], stored)
                    dve.wait_ge(down_mm, base + e + 1)
                    nc.vector.tensor_copy(YO[:, b, 512:1024], bank[6][:, :]).then_inc(y_dve, 1)

                read_xt(0, base + 1)
                for e in range(3):
                    body(e, e, False, None)
                    if e == 1:
                        finish_rows(1, 0 if layer == 0 else 2)
                with dve.Fori(1, 5) as g:
                    for u in range(3):
                        body(3 * g + u, u, False, 16 * (6 if u == 0 else 5) * layer + 16 * g)
                body(15, 0, True, 16 * 6 * layer + 16 * 5)
                o_ = ov[layer]
                dve.sem_inc(o_["y_dve"], 1)
                n_over = dve.value_load(over_i[0:1, 0:1], min_val=0, max_val=MAXOV)

                def read_xt_over(n, s):
                    dve.wait_ge(o_["xt_mm"], n)
                    nc.vector.tensor_copy(XT[:, s, 4:8, :], bank[1][:, :].rearrange("p (c n) -> p c n", c=4))\
                        .then_inc(o_["xt_dve"], 1)

                with dve.If(n_over > 0):
                    read_xt_over(1, 1)
                with dve.Fori(0, MAXOV // 3) as g:
                    for u in range(3):
                        o, s = 3 * g + u, (u + 1) % 3
                        with dve.If(n_over > o):
                            dve.wait_ge(o_["silu"], o + 1)
                            nc.vector.tensor_tensor(hid, silu_g, bank[2][:, FF:2 * FF], ALU.mult)\
                                .then_inc(o_["hid"], 1)
                            with dve.If(n_over > o + 1):
                                read_xt_over(o + 2, (s + 1) % 3)
                            dve.wait_ge(o_[f"stored{s}"], g + 1)
                            dve.wait_ge(o_["down_mm"], o + 1)
                            nc.vector.tensor_copy(YO[:, s, 512:1024], bank[6][:, :]).then_inc(o_["y_dve"], 1)

            def combine(layer, t):
                dve.wait_ge(bcast_g_in, 32 * (layer + 1))
                y1, y2 = picked_rows(t)[:, 0, :], picked_rows(t)[:, 1, :]
                dve.wait_ge(g_scaled, TT * layer + t + 1)
                link(nc.vector.scalar_tensor_tensor(y1, y2, w12[:, 1, t:t + 1], y1, ALU.mult, ALU.add))
                link(nc.vector.tensor_tensor(y2, y1, g_b[:, cnd(t), :], ALU.mult))
                nc.vector.tensor_tensor(X[:, t, :], X[:, t, :], y2, ALU.add).then_inc(x_out, 1)

            read_transposes()
            for b in range(2):
                if b == 1:
                    dve.wait_ge(z_in, 16 * (1 + COLS_T))
                    for y in range(3):
                        ins = nc.vector.tensor_tensor(
                            ZM[:, :, y, :, :],
                            bass.AP(tensor=UV, offset=64 * (GRID_R - 1) + 47 - W0[y],
                                    ap=[[UV_N, P], [512, HEADS], [-1, 32], [-64, GRID_R]]),
                            mk[:, y, :, :].unsqueeze(1).to_broadcast([P, HEADS, 32, GRID_R]), ALU.add)
                    ins.then_inc(zm_done, 1)
                for t in range(TT):
                    n = TT * b + t
                    if n in (1, 4):
                        finish_rows(0, 1 if n == 1 else 2)
                    dve.wait_ge(qk_ss, n + 1)
                    nc.vector.tensor_reduce(ssq[:, t, 8 * b:8 * b + 8], sq[n % 2].rearrange("p (h d) -> p h d", d=HD),
                                            AX, ALU.add).then_inc(qk_summed, 1)
            dve.wait_ge(qk_summed, 2 * TT)
            nc.vector.tensor_scalar(msq, ssq.rearrange("p t h -> p (t h)"), 1.0 / HD, EPS, ALU.mult, ALU.add)\
                .then_inc(qk_ms, 1)
            dve.wait_ge(qk_rs, 1)
            for t in range(TT):
                wait_read(dve, ("p", 0, 1, t))
                hq = H[:, t, :].rearrange("p (h d) -> p h d", d=HD)
                r = rsq.rearrange("p (t h) -> p t h", t=TT)[:, t, :].unsqueeze(2).to_broadcast([P, 2 * HEADS, HD])
                nc.vector.tensor_tensor(hq, hq, r, ALU.mult).then_inc(qk_normed, 1)
            dve.wait_ge(qk_normed, TT)
            wait_mod(dve, 0, 1)
            wait_mod(dve, 0, 2)
            nc.vector.tensor_tensor(kout.rearrange("p (h d) -> p h d", d=HD),
                                    H[:, 0, 512:1024].rearrange("p (h d) -> p h d", d=HD),
                                    kgain_b.unsqueeze(1).to_broadcast([P, HEADS, HD]), ALU.mult).then_inc(kout_done, 1)

            def copy_job(key, out, in_=None):
                wait_job(dve, key)
                nc.vector.tensor_copy(out, jbank(key)[:, :] if in_ is None else in_).then_inc(job_read_dve, 1)

            for t in range(TT):
                copy_job(("p", 0, 3, t), U[:, t, :])
            copy_job(("fcb",), fab[0][:, 1, :])
            for m in range(4):
                if m:
                    wait_job(dve, ("fy", m - 2) if m >= 2 else ("fcy",))
                sums, out = jbank(("fb", m)), fab[(m + 1) % 2][:, 1, :]
                wait_job(dve, ("fb", m))
                nc.vector.tensor_copy(out[:, 0:HALF], sums[:, 0:HALF])
                nc.vector.tensor_scalar(out[:, HALF:512], sums[:, HALF - 2:0:-1], -1.0, None, ALU.mult)\
                    .then_inc(job_read_dve, 1)
            dve.wait_ge(kv_out, 32)
            wait_job(dve, ("fb", 3))
            nc.vector.memset(zeros, 0.0).then_inc(zero_set, 1)
            wait_job(dve, ("kct",))
            key = ("qtc",)
            wait_job(dve, key)
            nc.vector.tensor_scalar(QT[:, :, 0:P], jbank(key)[:, :].rearrange("p (g n) -> p g n", g=4), gcol[:, 0:1],
                                    None, ALU.mult).then_inc(job_read_dve, 1)
            for hp in range(4):
                key = ("qt", hp)
                wait_job(dve, key)
                nc.vector.tensor_scalar(QT[:, hp, P:TOK], jbank(key)[:, :], gcol[:, 0:1], None, ALU.mult)\
                    .then_inc(job_read_dve, 1)

            def normalise(u):
                w = P if u < NCTX else 3 * P
                wait_read(dve, ("s", u))
                link(nc.vector.reciprocal(rinv[:, u % 4:u % 4 + 1], rsum[:, u % 4:u % 4 + 1]))
                nc.vector.tensor_scalar(pb[:, u % (LAG + 1), 0:w], pb[:, u % (LAG + 1), 0:w], rinv[:, u % 4:u % 4 + 1], None, ALU.mult)\
                    .then_inc(p_normed, 1)

            def read_o(n):
                dve.wait_ge(pv_done, 8 * (n + 1))
                if n == 0:
                    nc.vector.tensor_copy(HT[:, 0:4, 0:P], bank[7][:, :].rearrange("p (g n) -> p g n", g=4))\
                        .then_inc(o_read, 1)
                else:
                    hp = n - 1
                    nc.vector.tensor_copy(HT[:, hp, P:TOK].rearrange("p (r c) -> p c r", r=GRID_R),
                                          bank[5 + hp % 2][:, :].rearrange("p (c r) -> p c r", r=GRID_R))\
                        .then_inc(o_read, 1)

            for u in range(len(UNITS)):
                w = P if u < NCTX else 3 * P
                wait_job(dve, ("s", u))
                if u == NCTX:
                    dve.wait_ge(zm_done, 1)
                if u >= NCTX:
                    hp, qt, par = UNITS[u]
                    band = jbank(("s", u))[:, 0:BAND].rearrange("p (k r) -> p k r", r=GRID_R)
                    link(nc.vector.tensor_tensor(band, band, ZM[:, 2 * hp + par, BIAS_TYPE[qt - 1], :, :], ALU.add))
                nc.vector.tensor_reduce(nm[:, u % 4:u % 4 + 1], jbank(("s", u))[:, 0:w], AX, ALU.max, negate=True)\
                    .then_inc(maxed, 1)
                if u:
                    normalise(u - 1)
                if u >= 12 and (u - 12) % 8 == 0:
                    read_o((u - 12) // 8)
            normalise(len(UNITS) - 1)
            read_o(4)
            out_and_norm(0)
            route(0)
            experts(0)

            for t in range(TT):
                combine(0, t)
                mean_square(2 * TT + t)
                if t:
                    read_tile(1, ("tt", t - 1, 1), t - 1)
            finish_rows(1, 1)
            read_tile(1, ("tt", TT - 1, 1), TT - 1)
            dve.wait_ge(sg_in, 48)
            wait_job(dve, ("tt", TT - 1, 1))
            for t in range(TT):
                wait_read(dve, ("p", 1, 3, t))
                link(nc.vector.tensor_tensor(sqv, V1[:, t, :], V1[:, t, :], ALU.mult))
                link(nc.vector.tensor_reduce(ssv[:, SG * t:SG * t + SG], sqv.rearrange("p (g d) -> p g d", g=SG), AX,
                                             ALU.add))
            nc.vector.tensor_scalar(msv, ssv, SG / D, EPS, ALU.mult, ALU.add).then_inc(v_ms, 1)
            dve.wait_ge(v_rs, 1)
            for t in range(TT):
                r = rsv[:, SG * t:SG * t + SG].unsqueeze(2).to_broadcast([P, SG, D // SG])
                vv = V1[:, t, :].rearrange("p (g d) -> p g d", g=SG)
                link(nc.vector.tensor_tensor(vv, vv, r, ALU.mult))
                nc.vector.tensor_tensor(V1[:, t, :], V1[:, t, :], vgain, ALU.mult).then_inc(v_normed, 1)
            for t in range(TT):
                for b in range(2):
                    key = ("sp", t, b)
                    wait_job(dve, key)
                    wait_read(dve, ("p", 1, b, t))
                    for i in range(2):
                        g = 2 * b + i
                        u_ = U1[:, t, 256 * g:256 * g + 256]
                        ins = nc.vector.scalar_tensor_tensor(u_, jbank(key)[:, 256 * i:256 * i + 256], bs[:, g:g + 1],
                                                             u_, ALU.add, ALU.mult)
                    ins.then_inc(job_read_dve, 1)
            out_and_norm(1)
            route(1)
            experts(1)
            for t in range(TT):
                combine(1, t)

        @blk.tensor
        def _(pe):
            mm = nc.tensor.matmul

            def transposes(key, srcs, wdt=P):
                job_free(pe, key)
                for i, s in enumerate(srcs):
                    last = nc.tensor.transpose(jbank(key)[:, wdt * i:wdt * (i + 1)], s, ident)
                last.then_inc(job_done, 1)

            pe.wait_ge(cond_silu, 1)

            def ada(b, g, u, first):
                if not first:
                    pe.wait_ge(ada_read, b - 1)
                pe.wait_ge(block_in[u], 16 * (g + 1))
                for cc in range(DC):
                    last = mm(bank[5 + u % 2][0:2, :], scond[:, :, cc], block(u)[:, cc, :], start=cc == 0,
                              stop=cc == DC - 1)
                last.then_inc(ada_mm, 1)

            for b in range(4):
                ada(b, 0, b, b < 2)
            with pe.Fori(1, ADA_N // 4) as g:
                for u in range(4):
                    ada(4 * g + u, g, u, False)

            def ada1(b):
                bank_ = ada_bank(1, b)
                pe.wait_ge(ada_read, ADA_N + (b - 1 if b in (7, 8, 9) else b))
                wait_block(pe, ("ada", b))
                for cc in range(DC):
                    last = mm(bank_[0:2, :], scond[:, :, cc], blk_ap(("ada", b))[:, cc, :], start=cc == 0,
                              stop=cc == DC - 1)
                last.then_inc(ada_mm, 1)

            def norm_transposes():
                pe.wait_ge(small_in, 16 * 9)
                pe.wait_ge(normed, TT)
                for h in range(2):
                    transposes(("tc", h), [H[:, 0, 4 * h + i::DC] for i in range(4)])
                for cc in range(DC):
                    transposes(("t", cc), [H[:, t, cc::DC] for t in range(1, TT)])

            def project(layer, b, t):
                key = ("p", layer, b, t)
                job_free(pe, key)
                w = blk_ap(("in", layer, b))
                for cc in range(DC):
                    last = mm(jbank(key)[:, :], HT[:, cc, P * t:P * (t + 1)], w[:, cc, :], start=cc == 0,
                              stop=cc == DC - 1)
                last.then_inc(job_done, 1)

            def out_projection(layer):
                def router_transposes(t):
                    pe.wait_ge(h2_ready, TT * layer + t + 1)
                    for h in range(2):
                        transposes(("r", layer, t, h), [H[:, t, 4 * h + i::DC] for i in range(4)])

                def logits(t):
                    wait_read(pe, ("r", layer, t, 1))
                    for cc in range(DC):
                        last = mm(bank[7][:, E * t:E * t + E], HT[:, cc, P * t:P * (t + 1)], rw[:, cc, :],
                                  start=cc == 0, stop=cc == DC - 1)
                    return last

                for t in range(TT):
                    for b in range(2):
                        key = ("o", layer, t, b)
                        job_free(pe, key)
                        wait_block(pe, ("out", layer, b))
                        for cc in range(DC):
                            last = mm(jbank(key)[:, :], HT[:, cc, P * t:P * (t + 1)], blk_ap(("out", layer, b))[:, cc, :],
                                      start=cc == 0, stop=cc == DC - 1)
                        last.then_inc(job_done, 1)
                    if t:
                        router_transposes(t - 1)
                    if t >= 2:
                        logits(t - 2)
                first = 2 if layer == 0 else 10
                ada1(first)
                router_transposes(TT - 1)
                logits(TT - 2)
                logits(TT - 1).then_inc(logits_done, 1)
                if layer == 0:
                    ada1(3)
                pe.wait_ge(picked, layer + 1)
                pe.wait_ge(rc_in, 16 * (layer + 1))
                both = UV[:, 560:640].rearrange("p (t e) -> p t e", t=TT)
                for t in range(TT + 1):
                    terms = [(ones, i) for i in range(t)] + ([(triu, t)] if t < TT else [])
                    for i, (w, src) in enumerate(terms):
                        last = mm(bank[6][:, E * t:E * t + E], w, both[:, src, :], start=i == 0,
                                  stop=i == len(terms) - 1)
                last.then_inc(pos_done, 1)
                ada1(4 if layer == 0 else 11)
                tile_oh, place_oh = onehots()
                pe.wait_ge(slots_onehot, layer + 1)
                for k in range(2 * TT):
                    last = mm(bank[6][:, 128:128 + NTILE], place_oh[:, k, :], tile_oh[:, k, :], start=k == 0,
                              stop=k == 2 * TT - 1)
                last.then_inc(idx_mm, 1)
                if layer == 0:
                    ada1(5)

            def xt_transposes(b):
                for i in range(DC):
                    last = nc.tensor.transpose(bank[i // 4][:, P * (i % 4):P * (i % 4) + P], XG[:, b, i::DC], ident)
                return last

            def gate_up(b, s):
                w = xslot(s)[:, 0:4096].rearrange("p (k c n) -> p k c n", k=2, c=DC)
                for cc in range(DC):
                    last = mm(bank[2][:, :], XT[:, b, cc, :], w[:, :, cc, :], start=cc == 0, stop=cc == DC - 1)
                return last

            def hid_transposes():
                for i in range(2):
                    last = nc.tensor.transpose(bank[4][:, P * i:P * (i + 1)], hid[:, i::2], ident)
                return last

            def down(s):
                w = xslot(s)[:, 4096:6144].rearrange("p (c n) -> p c n", c=2)
                for half in range(2):
                    for i in range(2):
                        last = mm(bank[5 + half][:, :], hidT[:, i, :], w[:, i, 512 * half:512 * half + 512],
                                  start=i == 0, stop=i == 1)
                return last

            def experts(layer):
                base = E * layer

                def body(e, b, first, last_one, arrived, next_gathered):
                    pe.wait_ge(xt_act, base + e + 1)
                    pe.wait_ge(xt_dve, base + e + 1)
                    pe.wait_ge(expert_in[b], arrived)
                    gate_up(b, b).then_inc(gu_mm, 1)
                    if not last_one:
                        pe.wait_ge(gathered[(b + 1) % 3], next_gathered)
                        xt_transposes((b + 1) % 3).then_inc(xt_mm, 1)
                    pe.wait_ge(hid_done, base + e + 1)
                    hid_transposes().then_inc(hidT_mm, 1)
                    pe.wait_ge(hidT_read, base + e + 1)
                    if not first:
                        pe.wait_ge(y_act, base + e)
                        pe.wait_ge(y_dve, base + e)
                    down(b).then_inc(down_mm, 1)

                def arrivals(n, s, each):
                    return each * ((6 if s == 0 else 5) * layer + n)

                pe.wait_ge(gathered[0], arrivals(1, 0, 16))
                wait_read(pe, ("r", layer, TT - 1, 1))
                wait_read(pe, ("o", layer, TT - 1, 1))
                pe.wait_ge(ada_read, ADA_N + (6 if layer == 0 else ADA_N))
                xt_transposes(0).then_inc(xt_mm, 1)
                for e in range(3):
                    body(e, e, e == 0, False, arrivals(1, e, 48), arrivals(1 + (e == 2), (e + 1) % 3, 16))
                with pe.Fori(1, 5) as g:
                    for u in range(3):
                        body(3 * g + u, u, False, False, arrivals(g + 1, u, 48),
                             arrivals(g + 1 + (u == 2), (u + 1) % 3, 16))
                body(15, 0, False, True, arrivals(6, 0, 48), None)
                if layer == 0:
                    ada1(6)
                o_ = ov[layer]
                n_over = pe.value_load(over_i[0:1, 0:1], min_val=0, max_val=MAXOV)
                with pe.If(n_over > 0):
                    pe.wait_ge(o_["gathered1"], 16)
                    xt_transposes(1).then_inc(o_["xt_mm"], 1)
                with pe.Fori(0, MAXOV // 3) as g:
                    for u in range(3):
                        o, s = 3 * g + u, (u + 1) % 3
                        with pe.If(n_over > o):
                            pe.wait_ge(o_["xt_act"], o + 1)
                            pe.wait_ge(o_["xt_dve"], o + 1)
                            pe.wait_ge(o_[f"in{s}"], 48 * (g + 1))
                            gate_up(s, s).then_inc(o_["gu_mm"], 1)
                            with pe.If(n_over > o + 1):
                                nxt = (s + 1) % 3
                                pe.wait_ge(o_[f"gathered{nxt}"], 16 * (g + (2 if u == 2 else 1)))
                                xt_transposes(nxt).then_inc(o_["xt_mm"], 1)
                            pe.wait_ge(o_["hid"], o + 1)
                            hid_transposes().then_inc(o_["hidT_mm"], 1)
                            pe.wait_ge(o_["hidT_read"], o + 1)
                            pe.wait_ge(o_["y_act"], o + 1)
                            pe.wait_ge(o_["y_dve"], o + 1)
                            down(s).then_inc(o_["down_mm"], 1)
                pe.sem_inc(ring_free, 1)

            norm_transposes()
            for cc in range(DC - 2, DC):
                wait_read(pe, ("t", cc))
            wait_read(pe, ("tc", 0))
            wait_read(pe, ("tc", 1))
            for b in range(4):
                wait_block(pe, ("in", 0, b))
                for t in range(TT):
                    project(0, b, t)

            wait_block(pe, ("dft",))
            wait_block(pe, ("tab",))
            wait_read(pe, ("p", 0, 3, TT - 1))
            tab = blk_ap(("tab",))[:, 0, :].rearrange("p (k n) -> p k n", k=4)
            dftb = blk_ap(("dft",))
            for k, key in enumerate((("fca",), ("fcb",))):
                job_free(pe, key)
                for m in range(4):
                    last = mm(jbank(key)[:, P * m:P * (m + 1)], U[:, 0, P * m:P * (m + 1)], tab[:, k, :], start=True,
                              stop=True)
                last.then_inc(job_done, 1)

            def channels(key, b):
                job_free(pe, key)
                for s in range(2):
                    last = mm(jbank(key)[:, :], tab[:, 2 + s, :], fab[b][:, s, :], start=s == 0, stop=s == 1)
                last.then_inc(job_done, 1)

            for m in range(4):
                for k, name in enumerate(("fa", "fb")):
                    key = (name, m)
                    job_free(pe, key)
                    for i in range(4):
                        last = mm(jbank(key)[:, 0:HALF], U[:, 1 + i, P * m:P * (m + 1)], dftb[:, 4 * k + i, 0:HALF],
                                  start=i == 0, stop=i == 3)
                    last.then_inc(job_done, 1)
                if m == 0:
                    wait_read(pe, ("fca",))
                    wait_read(pe, ("fcb",))
                    channels(("fcy",), 0)
                else:
                    wait_read(pe, ("fa", m - 1))
                    wait_read(pe, ("fb", m - 1))
                    channels(("fy", m - 1), m % 2)
            wait_read(pe, ("fa", 3))
            wait_read(pe, ("fb", 3))
            channels(("fy", 3), 0)

            pe.wait_ge(cache_in, 32)
            transposes(("kct",), [kraw[:, P * g:P * (g + 1)] for g in range(4)])
            pe.wait_ge(qk_normed, TT)
            transposes(("qtc",), [H[:, 0, P * g:P * (g + 1)] for g in range(4)])
            transposes(("ktc",), [H[:, 0, 512 + P * g:512 + P * (g + 1)] for g in range(4)])
            for hp in range(4):
                transposes(("qt", hp), [H[:, t, P * hp:P * (hp + 1)] for t in range(1, TT)])
                transposes(("kt", hp), [H[:, t, 512 + P * hp:512 + P * (hp + 1)] for t in range(1, TT)])
            wait_read(pe, ("qt", 3))
            wait_read(pe, ("kt", 3))
            pe.wait_ge(zm_done, 1)
            pe.wait_ge(v_shifted, 96)

            def scores(u):
                hp, qt, par = UNITS[u]
                key = ("s", u)
                out = jbank(key)
                job_free(pe, key)
                at_ = slice(64 * par, 64 * par + 64)
                q = QT[at_, hp, P * qt:P * (qt + 1)]
                if qt == 0:
                    last = mm(out[:, 0:P], q, KT[at_, hp, 0:P], start=True, stop=True)
                else:
                    k0 = P + KEY_START[qt - 1]
                    mm(out[:, BAND:BAND + P], q, kcT[at_, hp, :], start=True, stop=True)
                    last = mm(out[:, 0:BAND], q, KT[at_, hp, k0:k0 + BAND], start=True, stop=True)
                last.then_inc(job_done, 1)

            def probs_t(u):
                w = 1 if u < NCTX else 3
                pe.wait_ge(p_normed, u + 1)
                transposes(("pt", u), [pb[:, u % (LAG + 1), P * i:P * (i + 1)] for i in range(w)])

            def values(u):
                hp, qt, par = UNITS[u]
                wait_read(pe, ("pt", u))
                cols = slice(64 * (2 * hp + par), 64 * (2 * hp + par) + 64)
                if qt == 0:
                    out, vals = bank[7][64 * par:64 * par + 64, P * hp:P * (hp + 1)], [V[:, 0, cols]]
                else:
                    if u % 8 == 0 and hp >= 2:
                        pe.wait_ge(o_read, hp)
                    out = bank[5 + hp % 2][64 * par:64 * par + 64, P * (qt - 1):P * qt]
                    vals = {1: [V[:, 1, cols], V[:, 2, cols]], 2: [vs[:, 0, cols], vs[:, 1, cols]],
                            3: [vs[:, 1, cols], vs[:, 2, cols]], 4: [V[:, 3, cols], V[:, 4, cols]]}[qt]
                    vals = vals + [vc[:, cols]]
                for i, v in enumerate(vals):
                    last = mm(out, v, ptb[:, u % 2, P * i:P * (i + 1)], start=i == 0, stop=i == len(vals) - 1)
                last.then_inc(pv_done, 1)

            n = len(UNITS)
            for u in range(n + LAG + 1):
                if u < n:
                    scores(u)
                if LAG <= u < n + LAG:
                    probs_t(u - LAG)
                if u > LAG:
                    values(u - LAG - 1)
                if u in ADA_UNITS:
                    if u == ADA_UNITS[0]:
                        pe.wait_ge(o_read, 1)
                    ada1(ADA_UNITS.index(u))
            pe.wait_ge(o_read, 5)
            out_projection(0)
            experts(0)
            for b in range(7, 10):
                ada1(b)

            pe.wait_ge(ada_read, ADA_N + 10)
            for kind, t in TILE_STEPS:
                if kind == "t":
                    pe.wait_ge(normed, 2 * TT + t + 1)
                    for h in range(2):
                        transposes(("tt", t, h), [H[:, t, 4 * h + i::DC] for i in range(4)])
                else:
                    wait_read(pe, ("tt", t, 0))
                    wait_read(pe, ("tt", t, 1))
                    wait_block(pe, ("in", 1, 2))
                    project(1, 2, t)
            for b in (3, 1, 0):
                wait_block(pe, ("in", 1, b))
                for t in range(TT):
                    project(1, b, t)
            pe.wait_ge(sg_in, 48)
            transposes(("ws",), [ws[:, g, :] for g in range(SG)])
            wait_read(pe, ("ws",))

            def us_transposes(t):
                wait_read(pe, ("sp", t, 1))
                for h in range(2):
                    transposes(("ut", t, h), [U1[:, t, P * (4 * h + i):P * (4 * h + i + 1)] for i in range(4)])

            for t in range(TT):
                pe.wait_ge(v_normed, t + 1)
                for b in range(2):
                    key = ("sp", t, b)
                    job_free(pe, key)
                    for i in range(2):
                        g = 2 * b + i
                        last = mm(jbank(key)[:, 256 * i:256 * i + 256], wst[:, g, :], V1[:, t, 256 * g:256 * g + 256],
                                  start=True, stop=True)
                    last.then_inc(job_done, 1)
                if t:
                    us_transposes(t - 1)
            us_transposes(TT - 1)
            wait_read(pe, ("ut", TT - 1, 1))
            out_projection(1)
            experts(1)


def shape_constants():
    def dft_pair(n):
        a = 2.0 * np.pi * (np.outer(np.arange(n), np.arange(n)) % n) / n
        return np.cos(a), np.sin(a)

    lat = GRID_R * GRID_W
    c_, s_ = dft_pair(lat)
    n = np.arange(lat)
    by_column = n % GRID_R * GRID_W + n // GRID_R
    dft = np.concatenate([m[by_column].reshape(4, P, lat).transpose(1, 0, 2) for m in (c_, s_)], axis=1) / np.sqrt(lat)
    cc, cs = dft_pair(P)
    g_, gs_ = dft_pair(HD)
    pair = np.eye(2)
    dft = dft[:, :, 0:HALF]
    tables = np.concatenate([cc / np.sqrt(P), cs / np.sqrt(P), np.kron(pair, g_) / 8, -np.kron(pair, gs_) / 8], axis=1)
    mask = np.zeros((P, 3, 32, GRID_R))
    for y, tile in enumerate((0, 1, 3)):
        qc = COLS_T * tile + np.arange(P) // GRID_R
        kc = KEY_START[tile] // GRID_R + np.arange(32)
        start = np.clip(qc - 8, 0, GRID_W - 16)
        ok = (kc[None] >= start[:, None]) & (kc[None] < start[:, None] + 16)
        mask[:, y] = np.where(ok, 0.0, NEG)[:, :, None]
    rc = np.zeros((P, RC_N + P))
    rc[:, 0:128] = np.triu(np.ones((P, P)), 1)
    rc[:, 128:256] = 1.0
    rc[:, 256:261] = np.arange(P)[:, None] + P * np.arange(TT)[None]
    rc[:, 261:265] = np.arange(4, 0, -1)
    rc[:, 265:281] = np.arange(E, 0, -1)
    rc[:, 281:297] = P * np.arange(E)
    rc[:, 297:306] = np.arange(MAXOV)
    rc[:, 306:434] = np.arange(P)
    rc[:, 434:RC_N] = P * np.arange(NTILE)
    rc[:, RC_N:] = np.eye(P)
    rows = np.zeros((48, len(PARTS)))
    for i, (k0, k1) in enumerate(PARTS):
        kinds = np.tile(np.repeat(np.arange(k0, k1), 8), 2)
        rows[:len(kinds), i] = np.isin(kinds, SCALES)
    return {"dft": dft, "tables": tables, "mask": mask.reshape(P, -1), "route_consts": rc,
            "scale_rows": rows}


_INS = ["x_prompt", "x_sample", "cache_k", "cache_v", "c", "c_ctx", "ada_w", "ada_b", "norm1_g", "norm2_g", "na_w_in",
        "na_w_out", "q_gain", "k_gain", "rpb", "sg_w_in", "sg_w_out", "sg_v_gain", "sg_w_s", "sg_b_s", "router_w",
        "router_b", "moe_w_gate", "moe_w_up", "moe_w_down"]
_OUTS = [(1, P, D), (1, 512, D), (1, 1, P, HEADS, HD), (1, 1, P, HEADS, HD)]


def kernel(**inputs):
    import concourse.bacc as _bacc
    from concourse.bass_utils import run_bass_kernel_spmd as _run

    nc = _bacc.Bacc("TRN2", target_bir_lowering=False, num_devices=1)
    arrays, args = {}, []
    given = {name: np.ascontiguousarray(inputs[name]) for name in _INS}
    given["rpb"] = np.pad(given["rpb"][0, :, ::-1, ::-1], ((0, 0), (0, 0), (16, 17)))
    for name, a in shape_constants().items():
        given[name] = np.ascontiguousarray(a, dtype=np.float32)
    for name, a in given.items():
        arrays[f"in_{name}"] = a
        args.append(nc.dram_tensor(f"in_{name}", a.shape, F32, kind="ExternalInput").ap())
    for i, shape in enumerate(_OUTS):
        args.append(nc.dram_tensor(f"out_{i}", shape, F32, kind="ExternalOutput").ap())
    build(nc, *args)
    r = _run(nc, [arrays], core_ids=[0])
    return tuple(r.results[0][f"out_{i}"] for i in range(len(_OUTS)))
```

```python
from contextlib import ExitStack

import numpy as np

import concourse.bass as bass
from concourse import mybir

F32 = mybir.dt.float32
I32 = mybir.dt.int32
ALU = mybir.AluOpType
ACT = mybir.ActivationFunctionType
AX = mybir.AxisListType.X

P = 128
D = 1024
DC = D // P
GRID_W, GRID_R = 64, 8
TT = 5
TOK = TT * P
HEADS, HD = 8, 64
E, FF = 16, 256
SG = 4
EPS = 1e-6
NEG = -1e30
PARTS = [(0, 2), (2, 5), (5, 6)]
PART_BLOCKS = [2 * k1 for _, k1 in PARTS]
SCALES, GAIN_KIND = (1, 4), {0: 1, 1: 4}
SIDE_LOADS = [6, 6, 3]
MAXOV = (2 * TOK - 3) // P
NTILE = E + MAXOV
RING_BANKS = 5
ADA_N = 6 * D // 512
COLS_T = P // GRID_R
KEY_START = [0, 64, 192, 256]
BIAS_TYPE = [0, 1, 1, 2]
BAND = 256
W0 = [16, 8, 0]

UNITS = [(hp, 0, par) for hp in range(4) for par in range(2)]
UNITS += [(hp, qt, par) for hp in range(4) for qt in range(1, TT) for par in range(2)]
NCTX = HEADS
LAG = 3
POOL_ADDS = (1, 3)
ADA_DVE = 4
HALF = 512 // 2 + 1
RC_N = 306 + P + NTILE


TILE_STEPS = [("t", 0), ("p", 0), ("t", 1), ("t", 2), ("p", 1), ("t", 3), ("p", 2), ("t", 4), ("p", 3), ("p", 4)]


def plan_jobs():
    jobs = []

    def add(key, reader):
        jobs.append((key, reader))

    def out_and_router(layer):
        for t in range(TT):
            for b in range(2):
                add(("o", layer, t, b), "dve")
            if t >= 1:
                for h in range(2):
                    add(("r", layer, t - 1, h), "act")
        for h in range(2):
            add(("r", layer, TT - 1, h), "act")

    for h in range(2):
        add(("tc", h), "dve" if h else "act")
    for c in range(DC):
        add(("t", c), "act" if c % 2 else "dve")
    for blk in range(4):
        for t in range(TT):
            add(("p", 0, blk, t), "dve" if blk == 3 else "act")
    add(("fca",), "act")
    add(("fcb",), "dve")
    for m in range(4):
        add(("fa", m), "act")
        add(("fb", m), "dve")
        add(("fy", m - 1) if m else ("fcy",), "act")
    add(("fy", 3), "act")
    add(("kct",), "act")
    add(("qtc",), "dve")
    add(("ktc",), "act")
    for hp in range(4):
        add(("qt", hp), "dve")
        add(("kt", hp), "act")
    for u in range(len(UNITS)):
        add(("s", u), "act")
        if u >= LAG:
            add(("pt", u - LAG), "act")
    for u in range(len(UNITS) - LAG, len(UNITS)):
        add(("pt", u), "act")
    out_and_router(0)
    for step in TILE_STEPS:
        if step[0] == "t":
            for h in range(2):
                add(("tt", step[1], h), "dve" if h else "act")
        else:
            add(("p", 1, 2, step[1]), "act")
    for blk in (3, 1, 0):
        for t in range(TT):
            add(("p", 1, blk, t), "act")
    add(("ws",), "act")
    for t in range(TT):
        for b in range(2):
            add(("sp", t, b), "dve")
        if t >= 1:
            for h in range(2):
                add(("ut", t - 1, h), "act")
    for h in range(2):
        add(("ut", TT - 1, h), "act")
    out_and_router(1)
    return jobs


JOBS = plan_jobs()
JOB = {key: k for k, (key, _) in enumerate(JOBS)}


def build(nc, x_prompt, x_sample, cache_k, cache_v, c, c_ctx, ada_w, ada_b, norm1_g, norm2_g, na_w_in, na_w_out,
          q_gain, k_gain, rpb, sg_w_in, sg_w_out, sg_v_gain, sg_w_s, sg_b_s, router_w, router_b, moe_w_gate,
          moe_w_up, moe_w_down, dft, tables, mask, route_consts, scale_rows, y_prompt, y_sample, k_ctx, v_ctx):
    with ExitStack() as ctx:
        def sb(name, n):
            return ctx.enter_context(nc.sbuf_tensor(name, [P, n], F32))

        def sem(name):
            return ctx.enter_context(nc.semaphore(name))

        def dram(name, shape):
            return nc.dram_tensor(name, shape, F32, kind="Internal").ap()

        Xr, Hr, HTr = sb("x_res", TT * D), sb("h_tok", TT * D), sb("h_feat", DC * TOK)
        UV_N = 10240
        UV, RING, BZ, PS, SM = sb("uv", UV_N), sb("ring", 9 * 2048), sb("bz", 6144), sb("ps", 2560), sb("small", 472)

        X = Xr[:, :].rearrange("p (t d) -> p t d", t=TT)
        H = Hr[:, :].rearrange("p (t d) -> p t d", t=TT)
        HT = HTr[:, :].rearrange("p (c n) -> p c n", c=DC)

        H_FEAT, H_TOK, BCAST = 4, 5, 6

        def block(s):
            if s >= 4:
                a = {H_FEAT: HTr[:, 0:4096], H_TOK: Hr[:, 0:4096], BCAST: BZ[:, 2048:6144]}[s]
                return a.rearrange("p (c n) -> p c n", c=DC)
            return RING[:, 4096 * s:4096 * (s + 1)].rearrange("p (c n) -> p c n", c=DC)

        def xslot(s):
            return RING[:, 6144 * (2 - s):6144 * (3 - s)]

        at = [0]

        def small(n):
            at[0] += n
            assert at[0] <= 472
            return SM[:, at[0] - n:at[0]]

        ident = small(P)
        rw = small(DC * E).rearrange("p (c e) -> p c e", c=DC)
        mod1 = small(64).rearrange("p (l q k c) -> p l q k c", l=2, q=2, k=2)
        kgain_b = UV[:, 7500:7564]
        ss, ms, rs = small(TT), small(TT), small(TT)
        nhalf = small(1)
        gcol = small(2)
        rb = small(E)
        slot_i = small(2 * TT).bitcast(I32).rearrange("p (t s) -> p t s", t=TT)
        table_fetch = small(1)
        w12 = small(2 * TT).rearrange("p (s t) -> p s t", s=2)
        idx_i = small(NTILE).bitcast(I32)
        over_i = small(1 + MAXOV).bitcast(I32)
        bs = small(SG)
        cond = small(16).rearrange("p (q c) -> p q c", q=2)
        scond = small(16).rearrange("p (q c) -> p q c", q=2)
        plus1 = small(len(PARTS))
        sel = small(4).rearrange("p (q m) -> p q m", q=2)

        def ada_row(layer, b):
            if layer == 0:
                return UV[0:2, 512 * b:512 * b + 512]
            if b < ADA_DVE:
                return UV[0:2, 9728:10240]
            return PS[0:2, 1408 + 512 * (b % 2):1920 + 512 * (b % 2)]

        def fin_tile(layer, part):
            k0, k1 = PARTS[part]
            if layer == 0:
                a = UV[0:16 * (k1 - k0), 6144 + 384 * part:6528 + 384 * part]
            else:
                a = PS[0:16 * (k1 - k0), 1024:1408]
            return a.rearrange("p (k n) -> p k n", k=3)

        def acc(b):
            return UV[:, 7680 + 1024 * (b % 2):8704 + 1024 * (b % 2)].rearrange("p (q n) -> p q n", q=2)

        zeros = UV[:, 4992:5120]
        Z = UV[:, 0:4096].rearrange("p (h w) -> p h w", h=HEADS)
        mk = UV[:, 4096:4864].rearrange("p (y k r) -> p y k r", y=3, r=GRID_R)
        ZM = BZ[:, :].rearrange("p (h y k r) -> p h y k r", h=HEADS, y=3, r=GRID_R)
        junk = PS[:, 0:1024]
        V = UV[:, 0:2560].rearrange("p (t n) -> p t n", t=TT)
        U = UV[:, 2560:5120].rearrange("p (t n) -> p t n", t=TT)
        QT = UV[:, 5120:7680].rearrange("p (g n) -> p g n", g=4)
        KT = UV[:, 7680:10240].rearrange("p (g n) -> p g n", g=4)
        sq = [UV[:, 5120:5632], UV[:, 5632:6144]]
        ssq = UV[:, 6144:6224].rearrange("p (t h) -> p t h", t=TT)
        msq, rsq = UV[:, 6224:6304], UV[:, 6304:6384]
        kout = UV[:, 6464:6976]
        kraw = UV[:, 6976:7488]
        kcT, vc = PS[:, 0:512].rearrange("p (g n) -> p g n", g=4), PS[:, 512:1024]
        vs = PS[:, 1024:2560].rearrange("p (i n) -> p i n", i=3)
        pb = Hr[:, 0:384 * (LAG + 1)].rearrange("p (b n) -> p b n", b=LAG + 1)
        ptb = Hr[:, 1920:3072].rearrange("p (b n) -> p b n", b=3)
        nm, rsum, rinv = Hr[:, 4992:4996], Hr[:, 4996:5000], Hr[:, 5000:5004]
        fab = [KT[:, :, :].rearrange("p g n -> p (g n)")[:, 1024 * b:1024 * (b + 1)].rearrange("p (s n) -> p s n", s=2)
               for b in range(2)]
        V1 = UV[:, 0:5120].rearrange("p (t n) -> p t n", t=TT)
        U1 = UV[:, 5120:10240].rearrange("p (t n) -> p t n", t=TT)
        ws = PS[:, 0:512].rearrange("p (g n) -> p g n", g=SG)
        wst = PS[:, 512:1024].rearrange("p (g n) -> p g n", g=SG)
        vgain = PS[:, 1024:2048]
        sqv = Hr[:, 0:1024]
        ssv = Hr[:, 1024:1044]
        msv, rsv = Hr[:, 1044:1064], Hr[:, 1064:1084]
        g_b = BZ[:, 0:2048].rearrange("p (q n) -> p q n", q=2)
        sc_b = BZ[:, 2048:4096].rearrange("p (q n) -> p q n", q=2)
        sh_b = BZ[:, 4096:6144].rearrange("p (q n) -> p q n", q=2)
        tmp = [UV[:, 0:512], UV[:, 512:1024]]
        XG = UV[:, 0:3072].rearrange("p (b n) -> p b n", b=3)
        XT = UV[:, 3072:6144].rearrange("p (b c n) -> p b c n", b=3, c=DC)
        YO = UV[:, 6144:9216].rearrange("p (b n) -> p b n", b=3)
        silu_g, hid, hidT = UV[:, 9216:9472], UV[:, 9472:9728], UV[:, 9728:9984].rearrange("p (c n) -> p c n", c=2)
        def picked_rows(t):
            return UV[:, 2048 * t:2048 * (t + 1)].rearrange("p (s n) -> p s n", s=2)

        rc = UV[:, 6144:6144 + RC_N]
        triu, ones, tokid = rc[:, 0:128], rc[:, 128:256], rc[:, 256:261]
        rank4, rank16, e128, oi = rc[:, 261:265], rc[:, 265:281], rc[:, 281:297], rc[:, 297:306]
        iota, tile_lo = rc[:, 306:434], rc[:, 434:434 + NTILE]

        def onehots():
            return (UV[:, 2560:2560 + 2 * TT * NTILE].rearrange("p (k n) -> p k n", n=NTILE),
                    UV[:, 1280:2560].rearrange("p (k n) -> p k n", n=P))

        bank = [ctx.enter_context(nc.psum_tensor(f"bank{i}", [P, 512], F32)) for i in range(8)]

        raw_mod = [[dram(f"raw_mod{l}_{i}", (2, (k1 - k0) * D)) for i, (k0, k1) in enumerate(PARTS)] for l in range(2)]
        mod_parts = [[dram(f"mod{l}_{i}", (2, k1 - k0, D)) for i, (k0, k1) in enumerate(PARTS)] for l in range(2)]
        h2_rows = [dram(f"h2_rows{l}", (TOK, D)) for l in range(2)]
        y_rows = dram("y_rows", (NTILE * P, D))

        x_in = [sem(f"x_in{t}") for t in range(TT)]
        small_in = sem("small_in")
        cond_in = sem("cond_in")
        cond_silu = sem("cond_silu")
        block_in = [sem(f"block_in{s}") for s in range(7)]
        ada_mm, ada_read, ada_acc, sel_set = sem("ada_mm"), sem("ada_read"), sem("ada_acc"), sem("sel_set")
        fin_in, fin_done = sem("fin_in"), sem("fin_done")
        raw_stored = [[sem(f"raw_stored{i}_{j}") for j in range(2)] for i in range(len(PARTS))]
        mod_out = [sem(f"mod_out{i}") for i in range(len(PARTS))]
        fin_side = [sem(f"fin_side{i}") for i in range(len(PARTS))]
        mod1_in = sem("mod1_in")
        z_in, zm_done = sem("z_in"), sem("zm_done")
        y_zeroed = sem("y_zeroed")
        zero_set = sem("zero_set")
        job_done, job_read_act, job_read_dve = sem("job_done"), sem("job_read_act"), sem("job_read_dve")
        sumsq, meansq, rstd, normed = sem("sumsq"), sem("meansq"), sem("rstd"), sem("normed")
        x_mid, x_out = sem("x_mid"), sem("x_out")
        y_scaled, x_out_pool = sem("y_scaled"), sem("x_out_pool")
        dve_step = sem("dve_step")
        qk_ss, qk_ms, qk_rs, qk_normed = sem("qk_ss"), sem("qk_ms"), sem("qk_rs"), sem("qk_normed")
        cache_in, v_shifted = sem("cache_in"), sem("v_shifted")
        kout_done, kv_out = sem("kout_done"), sem("kv_out")
        maxed, p_normed, pv_done, o_read = sem("maxed"), sem("p_normed"), sem("pv_done"), sem("o_read")
        bcast_in, bcast_g_in = sem("bcast_in"), sem("bcast_g_in")
        h2_ready, h2_stored = sem("h2_ready"), sem("h2_stored")
        logits_done, scored, picked, pos_done, routed = (sem("logits_done"), sem("scored"), sem("picked"),
                                                         sem("pos_done"), sem("routed"))
        rc_in, slots_onehot, idx_mm, idx_ready = sem("rc_in"), sem("slots_onehot"), sem("idx_mm"), sem("idx_ready")
        sg_in, v_ms, v_rs = sem("sg_in"), sem("v_ms"), sem("v_rs")
        qk_summed = sem("qk_summed")
        slots_set, rows_complete = sem("slots_set"), sem("rows_complete")
        def expert_steps(eng, body):
            for e in range(4):
                body(e, e % 3, e // 3, (e - 1) // 3)
            with eng.Fori(1, 4) as g:
                for u in range(3):
                    body(3 * g + u + 1, (u + 1) % 3, g if u < 2 else g + 1, g)
            for e in range(13, E):
                body(e, e % 3, e // 3, (e - 1) // 3)

        v_normed, ring_free = sem("v_normed"), sem("ring_free")
        expert_in = [sem(f"expert_in{s}") for s in range(3)]
        gathered = [sem(f"gathered{s}") for s in range(3)]
        y_stored = [sem(f"y_stored{s}") for s in range(3)]
        xt_mm, xt_act, xt_dve = sem("xt_mm"), sem("xt_act"), sem("xt_dve")
        gu_mm, silu_done, hid_done = sem("gu_mm"), sem("silu_done"), sem("hid_done")
        hidT_mm, hidT_read, down_mm, y_act, y_dve = (sem("hidT_mm"), sem("hidT_read"), sem("down_mm"), sem("y_act"),
                                                    sem("y_dve"))
        OVN = ["gathered0", "gathered1", "gathered2", "in0", "in1", "in2", "xt_mm", "xt_act", "xt_dve", "gu_mm",
               "silu", "hid", "hidT_mm", "hidT_read", "down_mm", "y_act", "y_dve", "stored0", "stored1", "stored2",
               "landed"]
        ov = [{n: sem(f"ov{l}_{n}") for n in OVN} for l in range(2)]
        got = [sem(f"got{t}") for t in range(TT)]
        g_scaled = sem("g_scaled")
        out_done = sem("out_done")

        reads = {"act": 0, "dve": 0}
        read_after = []
        for _, reader in JOBS:
            reads[reader] += 1
            read_after.append((reader, reads[reader]))

        def wait_read(eng, key):
            reader, n = read_after[JOB[key]]
            eng.wait_ge(job_read_act if reader == "act" else job_read_dve, n)

        def jbank(key):
            return bank[JOB[key] % RING_BANKS]

        def job_free(pe, key):
            k = JOB[key]
            if k >= RING_BANKS:
                wait_read(pe, JOBS[k - RING_BANKS][0])

        def wait_job(eng, key):
            eng.wait_ge(job_done, JOB[key] + 1)

        def mod(layer, q, kind):
            part = 0 if kind < 2 else 1 if kind < 5 else 2
            k = kind - PARTS[part][0]
            return mod_parts[layer][part][q, k:k + 1, :]

        def wait_mod(eng, layer, part):
            eng.wait_ge(mod_out[part], 16 * (layer + 1))

        def cnd(t):
            return 0 if t == 0 else 1

        AFTER = [("in", 0, 0), ("in", 0, 1), ("in", 0, 2), ("in", 0, 3),
                 ("ada", 0), ("ada", 2), ("ada", 1), ("dft",), ("tab",), ("ada", 3), ("out", 0, 0), ("out", 0, 1),
                 ("ada", 4), ("ada", 5), ("ada", 6), ("ada", 7), ("ada", 8), ("ada", 9),
                 ("in", 1, 2), ("in", 1, 3), ("in", 1, 0), ("in", 1, 1), ("out", 1, 0), ("out", 1, 1),
                 ("ada", 10), ("ada", 11)]
        SLOT = [0, 1, 2, 3] + [0, 0, 1, 0, 1, 2, 2, 3] + [1, 0, H_FEAT, H_TOK, H_FEAT, BCAST] + [2, 3, 0, 1, 2, 3]
        SLOT += [0, 0]
        place = {}
        loads = [ADA_N // 4] * 4 + [0, 0, 0]
        for key, s in zip(AFTER, SLOT):
            loads[s] += 1
            place[key] = (s, loads[s])

        def ada_bank(layer, b):
            if layer == 1 and b < ADA_DVE:
                return bank[7]
            if layer == 1 and 7 <= b < 10:
                return bank[7 if b % 2 == 0 else 3]
            return bank[5 + b % 2] if layer == 0 else bank[5]

        def wait_block(eng, key):
            s, n = place[key]
            eng.wait_ge(block_in[s], 16 * n)

        def blk_ap(key):
            return block(place[key][0])

        ada_v = ada_w.rearrange("l (p c) (g u n) -> l g u p c n", c=DC, u=4, n=512)
        win_v = na_w_in[0].rearrange("(p c) (b n) -> b p c n", c=DC, n=512)
        wout_v = na_w_out[0].rearrange("(c p) (b n) -> b p c n", p=P, n=512)
        sgin_v = sg_w_in[0].rearrange("(p c) (b n) -> b p c n", c=DC, n=512)
        sgout_v = sg_w_out[0].rearrange("(c p) (b n) -> b p c n", p=P, n=512)

        def latent_out(cc):
            return HT[:, cc, P:TOK].rearrange("p (c r) -> p r c", r=GRID_R)

        def by_row(a):
            return a.rearrange("p (r c) -> p r c", r=GRID_R)

        def xsrc(t):
            return x_prompt[0] if t == 0 else x_sample[0, P * (t - 1):P * t, :]

        def ydst(t):
            return y_prompt[0] if t == 0 else y_sample[0, P * (t - 1):P * t, :]

        blk = ctx.enter_context(nc.Block())

        @blk.sync
        def _(sp):
            def load_block(key, src):
                s, n = place[key]
                sp.dma_start(block(s), src).then_inc(block_in[s], 16)

            def load_ada(b):
                load_block(("ada", b), ada_v[1, b // 4, b % 4])

            sp.dma_start(cond[:, 0, :], c_ctx.rearrange("(p c) -> p c", c=DC)).then_inc(cond_in, 16)
            sp.dma_start(cond[:, 1, :], c[0].rearrange("(p c) -> p c", c=DC)).then_inc(cond_in, 16)
            for u in range(4):
                sp.dma_start(block(u), ada_v[0, 0, u]).then_inc(block_in[u], 16)
            with sp.Fori(1, ADA_N // 4) as g:
                for u in range(4):
                    sp.wait_ge(ada_mm, 4 * g + u - 3)
                    sp.dma_start(block(u), ada_v[0, g, u]).then_inc(block_in[u], 16)

            for b in range(4):
                sp.wait_ge(ada_mm, ADA_N - 3 + b)
                load_block(("in", 0, b), win_v[b])
            wait_job(sp, ("p", 0, 0, TT - 1))
            load_ada(0)
            sp.wait_ge(ada_acc, 1)
            load_ada(2)
            wait_job(sp, ("p", 0, 1, TT - 1))
            load_ada(1)
            sp.wait_ge(ada_acc, 3)
            s, _ = place[("dft",)]
            sp.dma_start(block(s)[:, :, 0:HALF], dft).then_inc(block_in[s], 16)
            s, _ = place[("tab",)]
            sp.dma_start(block(s)[:, 0, :], tables).then_inc(block_in[s], 16)
            wait_job(sp, ("p", 0, 2, TT - 1))
            load_ada(3)
            sp.wait_ge(ada_acc, ADA_DVE)
            load_block(("out", 0, 0), wout_v[0])
            wait_job(sp, ("p", 0, 3, TT - 1))
            load_block(("out", 0, 1), wout_v[1])

            def load_gate_up(layer, e, s, arrived=None):
                w, arrived = xslot(s), expert_in[s] if arrived is None else arrived
                sp.dma_start(w[:, 0:2048], moe_w_gate[layer].rearrange("e (p c) f -> e p (c f)", c=DC)[e])\
                    .then_inc(arrived, 16)
                sp.dma_start(w[:, 2048:4096], moe_w_up[layer].rearrange("e (p c) f -> e p (c f)", c=DC)[e])\
                    .then_inc(arrived, 16)

            def load_down(layer, e, s, arrived=None):
                sp.dma_start(xslot(s)[:, 4096:6144], moe_w_down[layer].rearrange("e (p c) n -> e p (c n)", c=2)[e])\
                    .then_inc(expert_in[s] if arrived is None else arrived, 16)

            def load_expert(layer, e, s):
                load_gate_up(layer, e, s)
                load_down(layer, e, s)

            for layer in range(2):
                if layer == 0:
                    wait_job(sp, ("fy", 3))
                    load_ada(4)
                    load_ada(5)
                else:
                    wait_job(sp, ("p", 1, 0, TT - 1))
                    load_ada(10)
                if layer == 0:
                    sp.wait_ge(maxed, len(UNITS))
                else:
                    sp.wait_ge(h2_ready, TT)
                    sp.wait_ge(x_out, TT)
                if layer == 1:
                    wait_job(sp, ("ut", TT - 1, 1))
                sp.dma_start(rc, route_consts[:, 0:RC_N]).then_inc(rc_in, 16)
                wait_mod(sp, layer, 1)
                for q in range(2):
                    for dst, kind in ((g_b, 2), (sc_b, 4), (sh_b, 3)):
                        sp.dma_start(dst[:, q, :], mod(layer, q, kind).to_broadcast([P, D])).then_inc(bcast_in, 16)
                wait_job(sp, ("o", layer, TT - 1, 1))
                load_expert(layer, 0, 0)
                if layer == 0:
                    sp.wait_ge(logits_done, 1)
                    load_ada(6)
                    sp.wait_ge(ada_mm, ADA_N + 5)
                else:
                    sp.wait_ge(ada_mm, ADA_N + 11)
                    load_ada(11)
                load_expert(layer, 1, 1)
                sp.wait_ge(ada_mm, ADA_N + (6 if layer == 0 else ADA_N))
                sp.wait_ge(gathered[0], 16 * (6 * layer + 1))
                load_expert(layer, 2, 2)

                def store_y(e, s):
                    base = E * layer
                    sp.wait_ge(y_act, base + e + 1)
                    sp.wait_ge(y_dve, base + e + 1)
                    sp.dma_start(y_rows.rearrange("(e p) n -> e p n", p=P)[e], YO[:, s, :])\
                        .then_inc(y_stored[s], 16)

                def replace(e, s):
                    sp.wait_ge(gu_mm, E * layer + e + 1)
                    load_gate_up(layer, e + 3, s)
                    sp.wait_ge(down_mm, E * layer + e + 1)
                    load_down(layer, e + 3, s)
                    store_y(e, s)

                with sp.Fori(0, 4) as g:
                    for u in range(3):
                        replace(3 * g + u, u)
                replace(12, 0)
                sp.wait_ge(x_mid, 2 * TT * (layer + 1))
                wait_mod(sp, layer, 2)
                for q in range(2):
                    sp.dma_start(g_b[:, q, :], mod(layer, q, 5).to_broadcast([P, D])).then_inc(bcast_g_in, 16)
                sp.wait_ge(routed, layer + 1)
                n_over = sp.value_load(over_i[0:1, 0:1], min_val=0, max_val=MAXOV)
                o_ = ov[layer]

                def load_overflow(o):
                    s = (o + 1) % 3
                    ex = sp.value_load(over_i[0:1, o + 1:o + 2], min_val=0, max_val=E - 1)
                    load_gate_up(layer, ex, s, o_[f"in{s}"])
                    load_down(layer, ex, s, o_[f"in{s}"])

                for o in range(3):
                    sp.wait_ge(down_mm, E * layer + 14 + o)
                    store_y(13 + o, (13 + o) % 3)
                    with sp.If(n_over > o):
                        load_overflow(o)
                if layer == 0:
                    sp.wait_ge(h2_stored, 16 * TT)
                    load_ada(7)
                    sp.wait_ge(h2_ready, TT)
                    load_ada(9)
                    sp.wait_ge(ada_mm, ADA_N + 7)
                    load_ada(8)
                for s in range(3):
                    sp.wait_ge(y_stored[s], 16 * (6 if s == 0 else 5) * (layer + 1))
                sp.sem_inc(o_["landed"], 16)
                for o in range(MAXOV):
                    s = (o + 1) % 3
                    with sp.If(n_over > o):
                        sp.wait_ge(o_["y_act"], o + 2)
                        sp.wait_ge(o_["y_dve"], o + 2)
                        sp.dma_start(y_rows.rearrange("(e p) n -> e p n", p=P)[E + o], YO[:, s, :])\
                            .then_inc(o_["landed"], 16)
                        sp.wait_ge(o_["landed"], 16 * (o + 2))
                        sp.sem_inc(o_[f"stored{s}"], 1)
                    if o + 3 < MAXOV:
                        with sp.If(n_over > o + 3):
                            sp.wait_ge(o_["down_mm"], o + 1)
                            load_overflow(o + 3)
                if layer == 0:
                    sp.wait_ge(ring_free, 1)
                    for b in (2, 3, 1, 0):
                        if b == 2:
                            sp.wait_ge(got[0], 32)
                        if b == 3:
                            sp.wait_ge(got[TT - 1], 32)
                        load_block(("in", 1, b), sgin_v[b])
                    for b in range(2):
                        wait_job(sp, ("p", 1, 2 + b, TT - 1))
                        load_block(("out", 1, b), sgout_v[b])
            for t in range(TT):
                before = sum(i < t for i in POOL_ADDS)
                if t in POOL_ADDS:
                    sp.wait_ge(x_out_pool, before + 1)
                else:
                    sp.wait_ge(x_out, TT + t - before + 1)
                sp.dma_start(ydst(t), X[:, t, :]).then_inc(out_done, 16)
            sp.wait_ge(out_done, 16 * TT)
            sp.wait_ge(kv_out, 32)

        @blk.gpsimd
        def _(pool):
            def rstd_of(k):
                t = k % TT
                pool.wait_ge(meansq, k + 1)
                nc.gpsimd.tensor_tensor(rs[:, t:t + 1], ms[:, t:t + 1], nhalf[:, :], ALU.pow).then_inc(rstd, 1)

            for k in range(TT):
                rstd_of(k)
            pool.wait_ge(qk_ms, 1)
            nc.gpsimd.tensor_tensor(rsq, msq, nhalf.to_broadcast([P, 80]), ALU.pow).then_inc(qk_rs, 1)

            for layer in range(2):
                if layer == 1:
                    for t in range(TT):
                        rstd_of(2 * TT + t)
                    pool.wait_ge(v_ms, 1)
                    nc.gpsimd.tensor_tensor(rsv, msv, nhalf.to_broadcast([P, 20]), ALU.pow).then_inc(v_rs, 1)
                for t in range(TT):
                    rstd_of((2 * layer + 1) * TT + t)
                    n = TT * layer + t
                    pool.wait_ge(h2_ready, n + 1)
                    pool.dma_start(h2_rows[layer][P * t:P * (t + 1), :], H[:, t, :]).then_inc(h2_stored, 16)
                pool.wait_ge(idx_ready, layer + 1)
                pool.wait_ge(h2_stored, 16 * TT * (layer + 1))

                def gather(e, s, signal):
                    nc.gpsimd.indirect_dma_start(
                        out=XG[:, s, :], out_offset=None, in_=h2_rows[layer][:, :],
                        in_offset=bass.IndirectOffsetOnAxis(ap=idx_i[:, e:e + 1], axis=0)).then_inc(signal, 16)

                for e in range(E):
                    if e >= 3:
                        pool.wait_ge(xt_mm, E * layer + e - 2)
                    gather(e, e % 3, gathered[e % 3])
                pool.wait_ge(routed, layer + 1)
                n_over = pool.value_load(over_i[0:1, 0:1], min_val=0, max_val=MAXOV)
                pool.wait_ge(xt_mm, E * (layer + 1))
                for o in range(MAXOV):
                    s = (o + 1) % 3
                    with pool.If(n_over > o):
                        if o >= 3:
                            pool.wait_ge(ov[layer]["xt_mm"], o - 2)
                        gather(E + o, s, ov[layer][f"gathered{s}"])
                pool.wait_ge(slots_set, layer + 1)
                pool.wait_ge(ov[layer]["landed"], n_over * 16 + 16)
                pool.sem_inc(rows_complete, 1)
                for t in range(TT):
                    for k in range(2):
                        nc.gpsimd.indirect_dma_start(
                            out=picked_rows(t)[:, k, :], out_offset=None, in_=y_rows[:, :],
                            in_offset=bass.IndirectOffsetOnAxis(ap=slot_i[:, t, k:k + 1], axis=0))\
                            .then_inc(got[t], 16)
            for i, t in enumerate(POOL_ADDS):
                pool.wait_ge(y_scaled, i + 1)
                nc.gpsimd.tensor_tensor(X[:, t, :], X[:, t, :], picked_rows(t)[:, 1, :], ALU.add).then_inc(x_out_pool, 1)

        @blk.scalar
        def _(act):
            def square_sum(k):
                t = k % TT
                if k:
                    act.wait_ge(sumsq, k)
                nc.scalar.activation(junk, X[:, t, :], ACT.Square, accum_out=ss[:, t:t + 1]).then_inc(sumsq, 1)

            act.dma_start(ident, route_consts[:, RC_N:RC_N + P]).then_inc(small_in, 16)
            act.dma_start(plus1[0:48, :], scale_rows).then_inc(small_in, 16)
            act.wait_ge(cond_in, 32)
            nc.scalar.activation(scond, cond, ACT.Silu).then_inc(cond_silu, 1)
            act.dma_start(rw, router_w.rearrange("(p c) e -> p c e", c=DC)).then_inc(small_in, 16)
            act.dma_start(kgain_b, k_gain[0:1, :].to_broadcast([P, HD])).then_inc(small_in, 16)
            act.dma_start(rb, router_b.rearrange("(o e) -> o e", o=1).to_broadcast([P, E])).then_inc(small_in, 16)
            for half in range(2):
                act.dma_start(gcol[64 * half:64 * half + 64, 0:1], q_gain.rearrange("o (d i) -> (o d) i", i=1))\
                    .then_inc(small_in, 16)
                act.dma_start(gcol[64 * half:64 * half + 64, 1:2], k_gain.rearrange("o (d i) -> (o d) i", i=1))\
                    .then_inc(small_in, 16)
            def fin_sides(layer, part):
                k0, k1 = PARTS[part]
                f, n = fin_tile(layer, part), 8 * (k1 - k0)
                for q in range(2):
                    act.dma_start(f[n * q:n * q + n, 1, :], ada_b[layer, D * k0:D * k1].rearrange("(k n) -> k n", n=P))\
                        .then_inc(fin_side[part], 16)
                    if part in GAIN_KIND:
                        plain = 8 * (GAIN_KIND[part] - k0)
                        g = (norm1_g, norm2_g)[part]
                        act.dma_start(f[n * q:n * q + plain, 2, :], route_consts[0:plain, 128:256])\
                            .then_inc(fin_side[part], 16)
                        act.dma_start(f[n * q + plain:n * q + n, 2, :], g[layer].rearrange("(k n) -> k n", n=P))\
                            .then_inc(fin_side[part], 16)
                if part not in GAIN_KIND:
                    act.dma_start(f[:, 2, :], route_consts[0:2 * n, 128:256]).then_inc(fin_side[part], 16)

            def read_ada(layer, b):
                n = ADA_N * layer + b
                part = [b < e for e in PART_BLOCKS].index(True)
                at_ = 512 * b - D * PARTS[part][0]
                if layer == 1 and 6 <= b < 10:
                    act.wait_ge(raw_stored[1][b % 2], 16 * (3 + (b - 4) // 2))
                if layer == 1 and 1 <= b < ADA_DVE:
                    act.wait_ge(raw_stored[0][(b - 1) % 2], 16 * (3 + (b - 1) // 2))
                act.wait_ge(ada_mm, n + 1)
                nc.scalar.activation(ada_row(layer, b), ada_bank(layer, b)[0:2, :], ACT.Copy).then_inc(ada_read, 1)
                act.wait_ge(ada_read, n + 1)
                act.dma_start(raw_mod[layer][part][:, at_:at_ + 512], ada_row(layer, b))\
                    .then_inc(raw_stored[part][b % 2], 16)

            def reload_rows(layer, part):
                for j in range(2):
                    act.wait_ge(raw_stored[part][j], 16 * (PARTS[part][1] - PARTS[part][0]) * (layer + 1))
                act.dma_start(fin_tile(layer, part)[:, 0, :],
                              raw_mod[layer][part].rearrange("q (k n) -> (q k) n", n=P)).then_inc(fin_in, 16)

            def store_mod(layer, part):
                act.wait_ge(fin_done, len(PARTS) * layer + part + 1)
                act.dma_start(mod_parts[layer][part].rearrange("q k (b n) -> (q k b) n", n=P),
                              fin_tile(layer, part)[:, 0, :]).then_inc(mod_out[part], 16)

            def load_mod1(layer):
                wait_mod(act, layer, 0)
                for q in range(2):
                    act.dma_start(mod1[:, layer, q, :, :],
                                  mod_parts[layer][0][q].rearrange("k (p c) -> p k c", c=DC)).then_inc(mod1_in, 16)

            for part in range(len(PARTS)):
                fin_sides(0, part)
            for b in range(ADA_N):
                if b < TT:
                    act.dma_start(X[:, b, :], xsrc(b)).then_inc(x_in[b], 16)
                if 2 <= b < 2 + TT:
                    act.wait_ge(x_in[b - 2], 16)
                    square_sum(b - 2)
                if 2 + TT <= b < 2 + 2 * TT:
                    t = b - 2 - TT
                    act.wait_ge(rstd, t + 1)
                    nc.scalar.activation(H[:, t, :], X[:, t, :], ACT.Copy, scale=rs[:, t:t + 1]).then_inc(normed, 1)
                read_ada(0, b)
                if b == 5:
                    reload_rows(0, 0)
                if b == 7:
                    store_mod(0, 0)
                if b == 9:
                    load_mod1(0)
                if b == 11:
                    reload_rows(0, 1)

            def read_tile(layer, key, t):
                act.wait_ge(mod1_in, 32 * (layer + 1))
                wait_job(act, key)
                for c in range(4):
                    ins = nc.scalar.activation(HT[:, c, P * t:P * (t + 1)], jbank(key)[:, P * c:P * (c + 1)],
                                               ACT.Identity, bias=mod1[:, layer, cnd(t), 0, c:c + 1],
                                               scale=mod1[:, layer, cnd(t), 1, c:c + 1])
                ins.then_inc(job_read_act, 1)

            def read_transposes():
                read_tile(0, ("tc", 0), 0)
                for c in range(1, DC, 2):
                    key = ("t", c)
                    wait_job(act, key)
                    nc.scalar.activation(latent_out(c), by_row(jbank(key)[:, :]), ACT.Identity,
                                         bias=mod1[:, 0, 1, 0, c:c + 1],
                                         scale=mod1[:, 0, 1, 1, c:c + 1]).then_inc(job_read_act, 1)

            def copy_job(key, out, in_=None):
                wait_job(act, key)
                nc.scalar.activation(out, jbank(key)[:, :] if in_ is None else in_, ACT.Copy).then_inc(job_read_act, 1)

            def out_and_norm(layer):
                def scale_rows_of(t):
                    k = (2 * layer + 1) * TT + t
                    act.wait_ge(rstd, k + 1)
                    nc.scalar.activation(H[:, t, :], X[:, t, :], ACT.Copy, scale=rs[:, t:t + 1]).then_inc(normed, 1)

                def router_rows(t):
                    for h in range(2):
                        key = ("r", layer, t, h)
                        copy_job(key, HT[:, 4 * h:4 * h + 4, P * t:P * (t + 1)],
                                 jbank(key)[:, :].rearrange("p (c n) -> p c n", c=4))

                for t in range(TT):
                    act.wait_ge(x_mid, 2 * TT * layer + 2 * (t + 1))
                    square_sum((2 * layer + 1) * TT + t)
                    scale_rows_of(t)
                    if t:
                        router_rows(t - 1)
                first = 4 if layer == 0 else 10
                read_ada(1, first)
                router_rows(TT - 1)
                nc.scalar.activation(table_fetch, nhalf, ACT.Sigmoid)
                act.wait_ge(logits_done, layer + 1)
                nc.scalar.activation(UV[:, 0:80], bank[7][:, 0:80], ACT.Sigmoid).then_inc(scored, 1)
                for b in (5, 6) if layer == 0 else (11,):
                    read_ada(1, b)
                fin_sides(1, 0 if layer == 0 else 2)
                reload_rows(1, 0 if layer == 0 else 2)

            def experts(layer):
                def read_xt(e, b, n):
                    act.wait_ge(xt_mm, n)
                    nc.scalar.activation(XT[:, b, 0:4, :], bank[0][:, :].rearrange("p (c n) -> p c n", c=4), ACT.Copy)\
                        .then_inc(xt_act, 1)

                base = E * layer

                def read_y(e, b, round_):
                    if round_ is not None:
                        act.wait_ge(y_stored[b], 16 * ((6 if b == 0 else 5) * layer + round_))
                    act.wait_ge(down_mm, base + e + 1)
                    nc.scalar.activation(YO[:, b, 0:512], bank[5][:, :], ACT.Copy).then_inc(y_act, 1)

                def body(e, b, round_, round_before):
                    act.wait_ge(gu_mm, base + e + 1)
                    nc.scalar.activation(silu_g, bank[2][:, 0:FF], ACT.Silu).then_inc(silu_done, 1)
                    if not (isinstance(e, int) and e == E - 1):
                        read_xt(e + 1, (b + 1) % 3, base + e + 2)
                    if not (isinstance(e, int) and e == 0):
                        read_y(e - 1, (b - 1) % 3, None if isinstance(e, int) and e <= 3 else round_before)
                    act.wait_ge(hidT_mm, base + e + 1)
                    nc.scalar.activation(hidT, bank[4][:, 0:FF].rearrange("p (c n) -> p c n", c=2), ACT.Copy)\
                        .then_inc(hidT_read, 1)
                    if isinstance(e, int) and e == 3:
                        store_mod(1, 0 if layer == 0 else 2)
                        if layer == 0:
                            load_mod1(1)
                            fin_sides(1, 1)

                read_xt(0, 0, E * layer + 1)
                expert_steps(act, body)
                read_y(E - 1, 0, 5)
                o_ = ov[layer]
                act.sem_inc(o_["y_act"], 1)
                for s in range(3):
                    act.wait_ge(y_stored[s], 16 * (6 if s == 0 else 5) * (layer + 1))
                for s in range(3):
                    act.sem_inc(o_[f"stored{s}"], 1)
                act.wait_ge(routed, layer + 1)
                n_over = act.value_load(over_i[0:1, 0:1], min_val=0, max_val=MAXOV)

                def read_xt_over(n, s):
                    act.wait_ge(o_["xt_mm"], n)
                    nc.scalar.activation(XT[:, s, 0:4, :], bank[0][:, :].rearrange("p (c n) -> p c n", c=4),
                                         ACT.Copy).then_inc(o_["xt_act"], 1)

                with act.If(n_over > 0):
                    read_xt_over(1, 1)
                with act.Fori(0, MAXOV // 3) as g:
                    for u in range(3):
                        o, s = 3 * g + u, (u + 1) % 3
                        with act.If(n_over > o):
                            act.wait_ge(o_["gu_mm"], o + 1)
                            nc.scalar.activation(silu_g, bank[2][:, 0:FF], ACT.Silu).then_inc(o_["silu"], 1)
                            with act.If(n_over > o + 1):
                                read_xt_over(o + 2, (s + 1) % 3)
                            act.wait_ge(o_["hidT_mm"], o + 1)
                            nc.scalar.activation(hidT, bank[4][:, 0:FF].rearrange("p (c n) -> p c n", c=2), ACT.Copy)\
                                .then_inc(o_["hidT_read"], 1)
                            act.wait_ge(o_[f"stored{s}"], g + 1)
                            act.wait_ge(o_["down_mm"], o + 1)
                            nc.scalar.activation(YO[:, s, 0:512], bank[5][:, :], ACT.Copy).then_inc(o_["y_act"], 1)

            def scale_first(layer, t):
                act.wait_ge(got[t], 32 * (layer + 1))
                y1 = picked_rows(t)[:, 0, :]
                nc.scalar.activation(y1, y1, ACT.Copy, scale=w12[:, 0, t:t + 1]).then_inc(g_scaled, 1)

            read_transposes()
            for b in range(2):
                for t in range(TT):
                    n = TT * b + t
                    if n == 0:
                        for j in range(2):
                            act.wait_ge(raw_stored[2][j], 16)
                    if n == 2:
                        store_mod(0, 1)
                        reload_rows(0, 2)
                        act.dma_start(mk.rearrange("p y k r -> p (y k r)"), mask).then_inc(z_in, 16)
                        for qc in range(COLS_T):
                            skewed = bass.AP(tensor=rpb.tensor, offset=qc, ap=[[64, GRID_R], [15 * 64, HEADS], [1, 496]])
                            act.dma_start(Z[GRID_R * qc:GRID_R * (qc + 1), :, 0:496], skewed).then_inc(z_in, 16)
                    if n == 5:
                        store_mod(0, 2)
                    key = ("p", 0, b, t)
                    wait_job(act, key)
                    if n >= 2:
                        act.wait_ge(qk_summed, n - 1)
                    nc.scalar.activation(sq[n % 2], jbank(key)[:, :], ACT.Square).then_inc(qk_ss, 1)
                    nc.scalar.activation(H[:, t, 512 * b:512 * b + 512], jbank(key)[:, :], ACT.Copy)\
                        .then_inc(job_read_act, 1)
            act.wait_ge(zm_done, 1)
            for t in range(TT):
                if t in (2, 4):
                    read_ada(1, t // 2 - 1)
                copy_job(("p", 0, 2, t), V[:, t, :])
                if t == 0:
                    wait_read(act, ("p", 0, 2, 0))
                    act.dma_start(v_ctx.rearrange("b o s h d -> (b o s) (h d)"), V[:, 0, :]).then_inc(kv_out, 16)
            wait_read(act, ("p", 0, 2, TT - 1))
            wait_mod(act, 0, 1)
            wait_mod(act, 0, 2)
            act.dma_start(kraw, cache_k.rearrange("b o s h d -> (b o s) (h d)")).then_inc(cache_in, 16)
            act.dma_start(vc, cache_v.rearrange("b o s h d -> (b o s) (h d)")).then_inc(cache_in, 16)
            for i in range(3):
                act.dma_start(vs[0:64, i, :], V[64:128, 1 + i, :]).then_inc(v_shifted, 16)
                act.dma_start(vs[64:128, i, :], V[0:64, 2 + i, :]).then_inc(v_shifted, 16)
            act.wait_ge(kout_done, 1)
            act.dma_start(k_ctx.rearrange("b o s h d -> (b o s) (h d)"), kout).then_inc(kv_out, 16)
            read_ada(1, 2)
            read_ada(1, 3)
            copy_job(("fca",), fab[0][:, 0, :])
            for m in range(4):
                if m:
                    wait_job(act, ("fy", m - 2) if m >= 2 else ("fcy",))
                sums, out = jbank(("fa", m)), fab[(m + 1) % 2][:, 0, :]
                wait_job(act, ("fa", m))
                nc.scalar.activation(out[:, 0:HALF], sums[:, 0:HALF], ACT.Copy)
                nc.scalar.activation(out[:, HALF:512], sums[:, HALF - 2:0:-1], ACT.Copy).then_inc(job_read_act, 1)
                if m == 0:
                    key = ("fcy",)
                    copy_job(key, HT[:, 4:8, 0:P], jbank(key)[:, :].rearrange("p (c n) -> p c n", c=4))
                else:
                    copy_job(("fy", m - 1), HT[:, 4 + m - 1, P:TOK])
            copy_job(("fy", 3), HT[:, 7, P:TOK])
            copy_job(("kct",), kcT, jbank(("kct",))[:, :].rearrange("p (g n) -> p g n", g=4))
            act.wait_ge(kv_out, 32)
            for j in range(2):
                act.wait_ge(raw_stored[0][j], 16 * 4)
            key = ("ktc",)
            wait_job(act, key)
            nc.scalar.activation(KT[:, :, 0:P], jbank(key)[:, :].rearrange("p (g n) -> p g n", g=4), ACT.Copy,
                                 scale=gcol[:, 1:2]).then_inc(job_read_act, 1)
            for hp in range(4):
                key = ("kt", hp)
                wait_job(act, key)
                nc.scalar.activation(KT[:, hp, P:TOK], jbank(key)[:, :], ACT.Copy, scale=gcol[:, 1:2])\
                    .then_inc(job_read_act, 1)

            def read_pt(u):
                w = P if u < NCTX else 3 * P
                if u >= 3:
                    act.wait_ge(pv_done, u - 2)
                copy_job(("pt", u), ptb[:, u % 3, 0:w], jbank(("pt", u))[:, 0:w])

            act.wait_ge(zero_set, 1)
            act.dma_start(y_rows[E * P:, :].rearrange("(p o) (b n) -> p (o b) n", p=P, n=P),
                          zeros.unsqueeze(1).to_broadcast([P, MAXOV * DC, P])).then_inc(y_zeroed, 16)
            for u in range(len(UNITS)):
                w = P if u < NCTX else 3 * P
                key = ("s", u)
                act.wait_ge(maxed, u + 1)
                if u > LAG:
                    wait_job(act, ("pt", u - LAG - 1))
                nc.scalar.activation(pb[:, u % (LAG + 1), 0:w], jbank(key)[:, 0:w], ACT.Exp, bias=nm[:, u % 4:u % 4 + 1],
                                     accum_out=rsum[:, u % 4:u % 4 + 1]).then_inc(job_read_act, 1)
                if u >= LAG:
                    read_pt(u - LAG)
            for u in range(len(UNITS) - LAG, len(UNITS)):
                read_pt(u)
            out_and_norm(0)
            act.wait_ge(y_zeroed, 16)
            experts(0)

            def norm_rows(t):
                act.wait_ge(x_out, t + 1)
                square_sum(2 * TT + t)
                act.wait_ge(rstd, 2 * TT + t + 1)
                nc.scalar.activation(H[:, t, :], X[:, t, :], ACT.Copy, scale=rs[:, t:t + 1]).then_inc(normed, 1)

            def gelu(b, t):
                key = ("p", 1, b, t)
                dst = V1 if b >= 2 else U1
                wait_job(act, key)
                nc.scalar.activation(dst[:, t, 512 * (b % 2):512 * (b % 2) + 512], jbank(key)[:, :],
                                     ACT.Gelu_apprx_tanh).then_inc(job_read_act, 1)

            read_ada(1, 7)
            read_ada(1, 8)
            scale_first(0, 0)
            read_ada(1, 9)
            scale_first(0, 1)
            norm_rows(0)
            scale_first(0, 2)
            read_tile(1, ("tt", 0, 0), 0)
            reload_rows(1, 1)
            norm_rows(1)
            scale_first(0, 3)
            norm_rows(2)
            scale_first(0, 4)
            gelu(2, 0)
            read_tile(1, ("tt", 1, 0), 1)
            read_tile(1, ("tt", 2, 0), 2)
            norm_rows(3)
            gelu(2, 1)
            read_tile(1, ("tt", 3, 0), 3)
            norm_rows(4)
            gelu(2, 2)
            read_tile(1, ("tt", 4, 0), 4)
            gelu(2, 3)
            gelu(2, 4)
            store_mod(1, 1)
            act.wait_ge(sumsq, 3 * TT)
            act.dma_start(ws, sg_w_s[0].rearrange("g p q -> p g q")).then_inc(sg_in, 16)
            wait_mod(act, 1, 1)
            act.dma_start(vgain, sg_v_gain[0:1, :].to_broadcast([P, D])).then_inc(sg_in, 16)
            with nc.allow_non_contiguous_dma(reason="512 scalars, one per partition and group"):
                act.dma_start(bs, sg_b_s[0].rearrange("g p -> p g")).then_inc(sg_in, 16)
            for b in (3, 1, 0):
                for t in range(TT):
                    gelu(b, t)
            copy_job(("ws",), wst, jbank(("ws",))[:, :].rearrange("p (g n) -> p g n", g=SG))
            for t in range(TT):
                for h in range(2):
                    key = ("ut", t, h)
                    copy_job(key, HT[:, 4 * h:4 * h + 4, P * t:P * (t + 1)],
                             jbank(key)[:, :].rearrange("p (c n) -> p c n", c=4))
            out_and_norm(1)
            experts(1)
            for t in range(TT):
                scale_first(1, t)

        @blk.vector
        def _(dve):
            steps = [0]

            def link(ins):
                steps[0] += 1
                ins.then_inc(dve_step, 1)
                dve.wait_ge(dve_step, steps[0])

            link(nc.vector.memset(nhalf, -0.5))
            link(nc.vector.memset(sel, 0.0))
            for q in range(2):
                nc.vector.memset(sel[:, q, q:q + 1], 1.0).then_inc(sel_set, 1)

            def mean_square(k):
                t = k % TT
                dve.wait_ge(sumsq, k + 1)
                nc.vector.tensor_scalar(ms[:, t:t + 1], ss[:, t:t + 1], 1.0 / D, EPS, ALU.mult, ALU.add)\
                    .then_inc(meansq, 1)

            dve.wait_ge(small_in, 16 * 9)
            link(nc.vector.tensor_scalar(gcol[:, 0:1], gcol[:, 0:1], HD ** -0.5, None, ALU.mult))

            def finish_rows(layer, part):
                dve.wait_ge(fin_side[part], 16 * SIDE_LOADS[part] * (layer + 1))
                dve.wait_ge(fin_in, 16 * (len(PARTS) * layer + part + 1))
                f = fin_tile(layer, part)
                link(nc.vector.tensor_tensor(f[:, 0, :], f[:, 0, :], f[:, 1, :], ALU.add))
                nc.vector.scalar_tensor_tensor(f[:, 0, :], f[:, 0, :], plus1[0:f.shape[0], part:part + 1], f[:, 2, :],
                                               ALU.add, ALU.mult).then_inc(fin_done, 1)

            for t in range(TT):
                mean_square(t)
            finish_rows(0, 0)

            def read_tile(layer, key, t):
                dve.wait_ge(mod1_in, 32 * (layer + 1))
                wait_job(dve, key)
                for c in range(4):
                    ins = nc.vector.tensor_scalar(HT[:, 4 + c, P * t:P * (t + 1)], jbank(key)[:, P * c:P * (c + 1)],
                                                  mod1[:, layer, cnd(t), 1, 4 + c:5 + c],
                                                  mod1[:, layer, cnd(t), 0, 4 + c:5 + c], ALU.mult, ALU.add)
                ins.then_inc(job_read_dve, 1)

            def read_transposes():
                read_tile(0, ("tc", 1), 0)
                for c in range(0, DC, 2):
                    key = ("t", c)
                    wait_job(dve, key)
                    nc.vector.tensor_scalar(latent_out(c), by_row(jbank(key)[:, :]), mod1[:, 0, 1, 1, c:c + 1],
                                            mod1[:, 0, 1, 0, c:c + 1], ALU.mult, ALU.add).then_inc(job_read_dve, 1)

            def out_and_norm(layer):
                for t in range(TT):
                    for b in range(2):
                        key = ("o", layer, t, b)
                        cols = slice(512 * b, 512 * b + 512)
                        dve.wait_ge(bcast_in, 96 * (layer + 1))
                        wait_job(dve, key)
                        nc.vector.tensor_tensor(tmp[b], jbank(key)[:, :], g_b[:, cnd(t), cols], ALU.mult)\
                            .then_inc(job_read_dve, 1)
                        wait_read(dve, key)
                        nc.vector.tensor_tensor(X[:, t, cols], X[:, t, cols], tmp[b], ALU.add).then_inc(x_mid, 1)
                        dve.wait_ge(x_mid, 2 * TT * layer + 2 * t + b + 1)
                    k = (2 * layer + 1) * TT + t
                    mean_square(k)
                    dve.wait_ge(normed, k + 1)
                    link(nc.vector.tensor_tensor(H[:, t, :], H[:, t, :], sc_b[:, cnd(t), :], ALU.mult))
                    nc.vector.tensor_tensor(H[:, t, :], H[:, t, :], sh_b[:, cnd(t), :], ALU.add).then_inc(h2_ready, 1)

            def route(layer):
                def tmp80(i):
                    return UV[:, 80 * i:80 * i + 80]

                def te(i):
                    return tmp80(i).rearrange("p (t e) -> p t e", t=TT)

                def tg(i):
                    return tmp80(i).rearrange("p (g j) -> p g j", j=4)

                def red(out, in_, op=ALU.max):
                    link(nc.vector.tensor_reduce(out, in_, AX, op))

                def bc(a, n):
                    return a.unsqueeze(2).to_broadcast([P, a.shape[1], n])

                def row(a, n):
                    return a.unsqueeze(1).to_broadcast([P, n, a.shape[1]])

                def tt(out, a, b, op):
                    link(nc.vector.tensor_tensor(out, a, b, op))

                dve.wait_ge(scored, layer + 1)
                dve.wait_ge(rc_in, 16 * (layer + 1))
                score, sel = te(0), te(1)
                tt(sel, score, row(rb, TT), ALU.add)
                v = tg(1)
                pairs = UV[:, 160:280].rearrange("p (g j) -> p g j", j=6)
                nc.vector.tensor_tensor(pairs[:, :, 0:3], v[:, :, 0:3], v[:, :, 1:4], ALU.add)
                nc.vector.tensor_tensor(pairs[:, :, 3:5], v[:, :, 0:2], v[:, :, 2:4], ALU.add)
                tt(pairs[:, :, 5:6], v[:, :, 0:1], v[:, :, 3:4], ALU.add)
                gs, gmax, gpick = UV[:, 280:300], UV[:, 300:305], UV[:, 305:325]
                red(gs, pairs)
                gs3, gp3 = gs.rearrange("p (t g) -> p t g", g=4), gpick.rearrange("p (t g) -> p t g", g=4)
                red(gmax, gs3)
                tt(gp3, gs3, bc(gmax, 4), ALU.is_equal)
                tt(gp3, gp3, row(rank4, TT), ALU.mult)
                red(gmax, gp3)
                tt(gp3, gp3, bc(gmax, 4), ALU.is_equal)
                off = UV[:, 325:345]
                link(nc.vector.tensor_scalar(off, gpick, -NEG, NEG, ALU.mult, ALU.add))
                tt(v, v, bc(off, 4), ALU.add)
                m5 = UV[:, 345:350]
                picks = [te(5), te(6)]
                for k in range(2):
                    red(m5, sel)
                    tt(picks[k], sel, bc(m5, E), ALU.is_equal)
                    tt(picks[k], picks[k], row(rank16, TT), ALU.mult)
                    red(m5, picks[k])
                    tt(picks[k], picks[k], bc(m5, E), ALU.is_equal)
                    if k == 0:
                        link(nc.vector.scalar_tensor_tensor(sel, picks[0], 2 * NEG, sel, ALU.mult, ALU.add))
                both = te(7)
                nc.vector.tensor_tensor(both, picks[0], picks[1], ALU.add).then_inc(picked, 1)
                prod = te(8)
                ovf, inc, one16 = UV[:, 816:832], UV[:, 832:848], UV[:, 848:864]
                nc.vector.memset(one16, 1.0)
                link(nc.vector.memset(UV[:, 2816:2816 + E], 0.0))
                dve.wait_ge(pos_done, layer + 1)
                before = UV[:, 2816:2816 + E * (TT + 1)].rearrange("p (t e) -> p t e", e=E)
                for t in range(TT):
                    tt(before[:, t + 1, :], before[:, t, :], bank[6][:, E * (TT + t):E * (TT + t + 1)], ALU.add)
                pos, cnt = te(9), before[:, TT, :]
                nc.vector.tensor_tensor(pos, bank[6][:, 0:TT * E].rearrange("p (t e) -> p t e", t=TT),
                                        before[:, 0:TT, :], ALU.add)
                link(nc.vector.tensor_scalar(ovf, cnt, P + 0.5, None, ALU.is_gt))
                for k in range(2, TT):
                    link(nc.vector.scalar_tensor_tensor(ovf, cnt, k * P + 0.5, ovf, ALU.is_gt, ALU.add))
                link(nc.vector.tensor_tensor_scan(inc, one16, ovf, 0.0, ALU.mult, ALU.add))
                delta = UV[:, 864:880]
                tt(delta, inc, ovf, ALU.subtract)
                link(nc.vector.tensor_scalar(delta, delta, float(P), float((E - 1) * P), ALU.mult, ALU.add))
                tt(delta, delta, e128, ALU.subtract)
                big, rowno = te(11), te(12)
                nc.vector.scalar_tensor_tensor(big, pos, P - 0.5, row(delta, TT), ALU.is_gt, ALU.mult)
                tt(rowno, pos, row(e128, TT), ALU.add)
                tt(rowno, rowno, big, ALU.add)
                sl = UV[:, 1040:1050].rearrange("p (s t) -> p s t", s=2)
                for k in range(2):
                    tt(prod, picks[k], rowno, ALU.mult)
                    red(sl[:, k, :], prod, ALU.add)
                nc.vector.tensor_copy(slot_i, sl.rearrange("p s t -> p t s")).then_inc(slots_set, 1)
                s10, hi, lo = UV[:, 1040:1050], UV[:, 1210:1220], UV[:, 1220:1230]
                tile_oh, place_oh = onehots()
                tt(tile_oh, bc(s10, NTILE), row(tile_lo, 2 * TT), ALU.is_ge)
                red(hi, tile_oh, ALU.add)
                link(nc.vector.tensor_scalar(hi, hi, -1.0, None, ALU.add))
                link(nc.vector.scalar_tensor_tensor(lo, hi, -float(P), s10, ALU.mult, ALU.add))
                tt(place_oh, bc(lo, P), row(iota, 2 * TT), ALU.is_equal)
                link(nc.vector.tensor_scalar(hi, hi, float(P), None, ALU.mult))
                tt(tile_oh, bc(hi, NTILE), row(tile_lo, 2 * TT), ALU.is_equal)
                toks = tokid.unsqueeze(1).unsqueeze(3).to_broadcast([P, 2, TT, NTILE])
                oh4 = tile_oh.rearrange("p (s t) n -> p s t n", s=2)
                nc.vector.tensor_tensor(oh4, oh4, toks, ALU.mult).then_inc(slots_onehot, 1)
                le = UV[:, 1056:1200].rearrange("p (o e) -> p o e", o=MAXOV)
                ovx = UV[:, 1200:1200 + MAXOV + 1]
                tt(le, row(inc, MAXOV), bc(oi, E), ALU.is_le)
                red(ovx[:, 1:1 + MAXOV], le, ALU.add)
                link(nc.vector.tensor_scalar(ovx[:, 1:1 + MAXOV], ovx[:, 1:1 + MAXOV], float(E - 1), None, ALU.min))
                link(nc.vector.tensor_copy(ovx[:, 0:1], inc[:, E - 1:E]))
                nc.vector.tensor_copy(over_i, ovx).then_inc(routed, 1)
                for k in range(2):
                    tt(prod, picks[k], score, ALU.mult)
                    red(w12[:, k, :], prod, ALU.add)
                wsum = UV[:, 350:355]
                tt(wsum, w12[:, 0, :], w12[:, 1, :], ALU.add)
                link(nc.vector.reciprocal(wsum, wsum))
                tt(w12, w12, row(wsum, 2), ALU.mult)
                dve.wait_ge(idx_mm, layer + 1)
                nc.vector.tensor_copy(idx_i, bank[6][:, 256:256 + NTILE]).then_inc(idx_ready, 1)

            def experts(layer):
                base = E * layer

                def read_xt(b, n):
                    dve.wait_ge(xt_mm, n)
                    nc.vector.tensor_copy(XT[:, b, 4:8, :], bank[1][:, :].rearrange("p (c n) -> p c n", c=4))\
                        .then_inc(xt_dve, 1)

                def read_y(e, b, round_):
                    if round_ is not None:
                        dve.wait_ge(y_stored[b], 16 * ((6 if b == 0 else 5) * layer + round_))
                    dve.wait_ge(down_mm, base + e + 1)
                    nc.vector.tensor_copy(YO[:, b, 512:1024], bank[6][:, :]).then_inc(y_dve, 1)

                def body(e, b, round_, round_before):
                    dve.wait_ge(silu_done, base + e + 1)
                    nc.vector.tensor_tensor(hid, silu_g, bank[2][:, FF:2 * FF], ALU.mult).then_inc(hid_done, 1)
                    if not (isinstance(e, int) and e == E - 1):
                        read_xt((b + 1) % 3, base + e + 2)
                    if not (isinstance(e, int) and e == 0):
                        read_y(e - 1, (b - 1) % 3, None if isinstance(e, int) and e <= 3 else round_before)
                    if isinstance(e, int) and e == 1:
                        finish_rows(1, 0 if layer == 0 else 2)

                read_xt(0, base + 1)
                expert_steps(dve, body)
                read_y(E - 1, 0, 5)
                o_ = ov[layer]
                dve.sem_inc(o_["y_dve"], 1)
                n_over = dve.value_load(over_i[0:1, 0:1], min_val=0, max_val=MAXOV)

                def read_xt_over(n, s):
                    dve.wait_ge(o_["xt_mm"], n)
                    nc.vector.tensor_copy(XT[:, s, 4:8, :], bank[1][:, :].rearrange("p (c n) -> p c n", c=4))\
                        .then_inc(o_["xt_dve"], 1)

                with dve.If(n_over > 0):
                    read_xt_over(1, 1)
                with dve.Fori(0, MAXOV // 3) as g:
                    for u in range(3):
                        o, s = 3 * g + u, (u + 1) % 3
                        with dve.If(n_over > o):
                            dve.wait_ge(o_["silu"], o + 1)
                            nc.vector.tensor_tensor(hid, silu_g, bank[2][:, FF:2 * FF], ALU.mult)\
                                .then_inc(o_["hid"], 1)
                            with dve.If(n_over > o + 1):
                                read_xt_over(o + 2, (s + 1) % 3)
                            dve.wait_ge(o_[f"stored{s}"], g + 1)
                            dve.wait_ge(o_["down_mm"], o + 1)
                            nc.vector.tensor_copy(YO[:, s, 512:1024], bank[6][:, :]).then_inc(o_["y_dve"], 1)

            def combine(layer, t):
                dve.wait_ge(bcast_g_in, 32 * (layer + 1))
                y1, y2 = picked_rows(t)[:, 0, :], picked_rows(t)[:, 1, :]
                dve.wait_ge(g_scaled, TT * layer + t + 1)
                link(nc.vector.scalar_tensor_tensor(y1, y2, w12[:, 1, t:t + 1], y1, ALU.mult, ALU.add))
                scaled = nc.vector.tensor_tensor(y2, y1, g_b[:, cnd(t), :], ALU.mult)
                if layer == 1 and t in POOL_ADDS:
                    scaled.then_inc(y_scaled, 1)
                else:
                    link(scaled)
                    nc.vector.tensor_tensor(X[:, t, :], X[:, t, :], y2, ALU.add).then_inc(x_out, 1)

            def ada_chunks(b, chunks):
                for cc in chunks:
                    w = blk_ap(("ada", b))[:, cc, :]
                    for q in range(2):
                        out, c_ = acc(b)[:, q, :], scond[:, q, cc:cc + 1]
                        if cc == 0:
                            ins = nc.vector.tensor_scalar(out, w, c_, None, ALU.mult)
                        else:
                            ins = nc.vector.scalar_tensor_tensor(out, w, c_, out, ALU.mult, ALU.add)
                        if q:
                            link(ins)
                if chunks[-1] == DC - 1:
                    dve.sem_inc(ada_acc, 1)

            read_transposes()
            for b in range(2):
                if b == 1:
                    dve.wait_ge(z_in, 16 * (1 + COLS_T))
                    for y in range(3):
                        ins = nc.vector.tensor_tensor(
                            ZM[:, :, y, :, :],
                            bass.AP(tensor=UV, offset=64 * (GRID_R - 1) + 47 - W0[y],
                                    ap=[[UV_N, P], [512, HEADS], [-1, 32], [-64, GRID_R]]),
                            mk[:, y, :, :].unsqueeze(1).to_broadcast([P, HEADS, 32, GRID_R]), ALU.add)
                    ins.then_inc(zm_done, 1)
                for t in range(TT):
                    n = TT * b + t
                    if n in (1, 4):
                        finish_rows(0, 1 if n == 1 else 2)
                    dve.wait_ge(qk_ss, n + 1)
                    nc.vector.tensor_reduce(ssq[:, t, 8 * b:8 * b + 8], sq[n % 2].rearrange("p (h d) -> p h d", d=HD),
                                            AX, ALU.add).then_inc(qk_summed, 1)
                    if b == 1 and t:
                        if t == 1:
                            dve.wait_ge(cond_silu, 1)
                            wait_block(dve, ("ada", 0))
                        ada_chunks(0, (2 * t - 2, 2 * t - 1))
            dve.wait_ge(qk_summed, 2 * TT)
            nc.vector.tensor_scalar(msq, ssq.rearrange("p t h -> p (t h)"), 1.0 / HD, EPS, ALU.mult, ALU.add)\
                .then_inc(qk_ms, 1)
            wait_block(dve, ("ada", 1))
            ada_chunks(1, range(DC))
            dve.wait_ge(qk_rs, 1)
            for t in range(TT):
                wait_read(dve, ("p", 0, 1, t))
                hq = H[:, t, :].rearrange("p (h d) -> p h d", d=HD)
                r = rsq.rearrange("p (t h) -> p t h", t=TT)[:, t, :].unsqueeze(2).to_broadcast([P, 2 * HEADS, HD])
                nc.vector.tensor_tensor(hq, hq, r, ALU.mult).then_inc(qk_normed, 1)
            dve.wait_ge(qk_normed, TT)
            wait_mod(dve, 0, 1)
            wait_mod(dve, 0, 2)
            nc.vector.tensor_tensor(kout.rearrange("p (h d) -> p h d", d=HD),
                                    H[:, 0, 512:1024].rearrange("p (h d) -> p h d", d=HD),
                                    kgain_b.unsqueeze(1).to_broadcast([P, HEADS, HD]), ALU.mult).then_inc(kout_done, 1)

            def copy_job(key, out, in_=None):
                wait_job(dve, key)
                nc.vector.tensor_copy(out, jbank(key)[:, :] if in_ is None else in_).then_inc(job_read_dve, 1)

            dve.wait_ge(ada_mm, ADA_N + 1)
            wait_block(dve, ("ada", 2))
            ada_chunks(2, range(DC))
            for t in range(TT):
                copy_job(("p", 0, 3, t), U[:, t, :])
                if t == 0:
                    dve.wait_ge(ada_mm, ADA_N + 2)
                    wait_block(dve, ("ada", 3))
                if t < 4:
                    ada_chunks(3, (2 * t, 2 * t + 1))
            copy_job(("fcb",), fab[0][:, 1, :])
            for m in range(4):
                if m:
                    wait_job(dve, ("fy", m - 2) if m >= 2 else ("fcy",))
                sums, out = jbank(("fb", m)), fab[(m + 1) % 2][:, 1, :]
                wait_job(dve, ("fb", m))
                nc.vector.tensor_copy(out[:, 0:HALF], sums[:, 0:HALF])
                nc.vector.tensor_scalar(out[:, HALF:512], sums[:, HALF - 2:0:-1], -1.0, None, ALU.mult)\
                    .then_inc(job_read_dve, 1)
            dve.wait_ge(kv_out, 32)
            wait_job(dve, ("fb", 3))
            nc.vector.memset(zeros, 0.0).then_inc(zero_set, 1)
            wait_job(dve, ("kct",))
            key = ("qtc",)
            wait_job(dve, key)
            nc.vector.tensor_scalar(QT[:, :, 0:P], jbank(key)[:, :].rearrange("p (g n) -> p g n", g=4), gcol[:, 0:1],
                                    None, ALU.mult).then_inc(job_read_dve, 1)
            for hp in range(4):
                key = ("qt", hp)
                wait_job(dve, key)
                nc.vector.tensor_scalar(QT[:, hp, P:TOK], jbank(key)[:, :], gcol[:, 0:1], None, ALU.mult)\
                    .then_inc(job_read_dve, 1)

            def normalise(u):
                w = P if u < NCTX else 3 * P
                wait_read(dve, ("s", u))
                link(nc.vector.reciprocal(rinv[:, u % 4:u % 4 + 1], rsum[:, u % 4:u % 4 + 1]))
                p_ = pb[:, u % (LAG + 1), 0:w]
                nc.vector.tensor_scalar(p_, p_, rinv[:, u % 4:u % 4 + 1], None, ALU.mult).then_inc(p_normed, 1)

            def read_o(n):
                dve.wait_ge(pv_done, 8 * (n + 1))
                if n == 0:
                    nc.vector.tensor_copy(HT[:, 0:4, 0:P], bank[7][:, :].rearrange("p (g n) -> p g n", g=4))\
                        .then_inc(o_read, 1)
                else:
                    hp = n - 1
                    nc.vector.tensor_copy(HT[:, hp, P:TOK].rearrange("p (r c) -> p c r", r=GRID_R),
                                          bank[5 + hp % 2][:, :].rearrange("p (c r) -> p c r", r=GRID_R))\
                        .then_inc(o_read, 1)

            for u in range(len(UNITS)):
                w = P if u < NCTX else 3 * P
                wait_job(dve, ("s", u))
                if u == NCTX:
                    dve.wait_ge(zm_done, 1)
                if u >= NCTX:
                    hp, qt, par = UNITS[u]
                    band = jbank(("s", u))[:, 0:BAND].rearrange("p (k r) -> p k r", r=GRID_R)
                    link(nc.vector.tensor_tensor(band, band, ZM[:, 2 * hp + par, BIAS_TYPE[qt - 1], :, :], ALU.add))
                nc.vector.tensor_reduce(nm[:, u % 4:u % 4 + 1], jbank(("s", u))[:, 0:w], AX, ALU.max, negate=True)\
                    .then_inc(maxed, 1)
                if u:
                    normalise(u - 1)
                if u >= 12 and (u - 12) % 8 == 0:
                    read_o((u - 12) // 8)
            normalise(len(UNITS) - 1)
            read_o(4)
            out_and_norm(0)
            route(0)
            experts(0)

            for t in range(TT):
                combine(0, t)
                mean_square(2 * TT + t)
                if t:
                    read_tile(1, ("tt", t - 1, 1), t - 1)
            finish_rows(1, 1)
            read_tile(1, ("tt", TT - 1, 1), TT - 1)
            dve.wait_ge(sg_in, 48)
            wait_job(dve, ("tt", TT - 1, 1))
            for t in range(TT):
                wait_read(dve, ("p", 1, 3, t))
                link(nc.vector.tensor_tensor(sqv, V1[:, t, :], V1[:, t, :], ALU.mult))
                link(nc.vector.tensor_reduce(ssv[:, SG * t:SG * t + SG], sqv.rearrange("p (g d) -> p g d", g=SG), AX,
                                             ALU.add))
            nc.vector.tensor_scalar(msv, ssv, SG / D, EPS, ALU.mult, ALU.add).then_inc(v_ms, 1)
            dve.wait_ge(v_rs, 1)
            for t in range(TT):
                r = rsv[:, SG * t:SG * t + SG].unsqueeze(2).to_broadcast([P, SG, D // SG])
                vv = V1[:, t, :].rearrange("p (g d) -> p g d", g=SG)
                link(nc.vector.tensor_tensor(vv, vv, r, ALU.mult))
                nc.vector.tensor_tensor(V1[:, t, :], V1[:, t, :], vgain, ALU.mult).then_inc(v_normed, 1)
            for t in range(TT):
                for b in range(2):
                    key = ("sp", t, b)
                    wait_job(dve, key)
                    wait_read(dve, ("p", 1, b, t))
                    for i in range(2):
                        g = 2 * b + i
                        u_ = U1[:, t, 256 * g:256 * g + 256]
                        ins = nc.vector.scalar_tensor_tensor(u_, jbank(key)[:, 256 * i:256 * i + 256], bs[:, g:g + 1],
                                                             u_, ALU.add, ALU.mult)
                    ins.then_inc(job_read_dve, 1)
            out_and_norm(1)
            route(1)
            experts(1)
            for t in range(TT):
                combine(1, t)

        @blk.tensor
        def _(pe):
            mm = nc.tensor.matmul

            def transposes(key, srcs, wdt=P):
                job_free(pe, key)
                for i, s in enumerate(srcs):
                    last = nc.tensor.transpose(jbank(key)[:, wdt * i:wdt * (i + 1)], s, ident)
                last.then_inc(job_done, 1)

            pe.wait_ge(cond_silu, 1)

            def ada(b, g, u, first):
                if not first:
                    pe.wait_ge(ada_read, b - 1)
                pe.wait_ge(block_in[u], 16 * (g + 1))
                for cc in range(DC):
                    last = mm(bank[5 + u % 2][0:2, :], scond[:, :, cc], block(u)[:, cc, :], start=cc == 0,
                              stop=cc == DC - 1)
                last.then_inc(ada_mm, 1)

            for b in range(4):
                ada(b, 0, b, b < 2)
            with pe.Fori(1, ADA_N // 4) as g:
                for u in range(4):
                    ada(4 * g + u, g, u, False)

            def ada1(b):
                bank_ = ada_bank(1, b)
                pe.wait_ge(ada_read, ADA_N + (b - 1 if b in (7, 8, 9) else b))
                wait_block(pe, ("ada", b))
                for cc in range(DC):
                    last = mm(bank_[0:2, :], scond[:, :, cc], blk_ap(("ada", b))[:, cc, :], start=cc == 0,
                              stop=cc == DC - 1)
                last.then_inc(ada_mm, 1)

            def ada_rows(b):
                pe.wait_ge(sel_set, 2)
                pe.wait_ge(ada_read, ADA_N + b)
                pe.wait_ge(ada_acc, b + 1)
                for q in range(2):
                    last = mm(bank[7][0:2, :], sel[:, q, :], acc(b)[:, q, :], start=q == 0, stop=q == 1)
                last.then_inc(ada_mm, 1)

            def norm_transposes():
                pe.wait_ge(small_in, 16 * 9)
                pe.wait_ge(normed, TT)
                for h in range(2):
                    transposes(("tc", h), [H[:, 0, 4 * h + i::DC] for i in range(4)])
                for cc in range(DC):
                    transposes(("t", cc), [H[:, t, cc::DC] for t in range(1, TT)])

            def project(layer, b, t):
                key = ("p", layer, b, t)
                job_free(pe, key)
                w = blk_ap(("in", layer, b))
                for cc in range(DC):
                    last = mm(jbank(key)[:, :], HT[:, cc, P * t:P * (t + 1)], w[:, cc, :], start=cc == 0,
                              stop=cc == DC - 1)
                last.then_inc(job_done, 1)

            def out_projection(layer):
                def router_transposes(t):
                    pe.wait_ge(h2_ready, TT * layer + t + 1)
                    for h in range(2):
                        transposes(("r", layer, t, h), [H[:, t, 4 * h + i::DC] for i in range(4)])

                def logits(t):
                    wait_read(pe, ("r", layer, t, 1))
                    for cc in range(DC):
                        last = mm(bank[7][:, E * t:E * t + E], HT[:, cc, P * t:P * (t + 1)], rw[:, cc, :],
                                  start=cc == 0, stop=cc == DC - 1)
                    return last

                for t in range(TT):
                    for b in range(2):
                        key = ("o", layer, t, b)
                        job_free(pe, key)
                        wait_block(pe, ("out", layer, b))
                        for cc in range(DC):
                            last = mm(jbank(key)[:, :], HT[:, cc, P * t:P * (t + 1)], blk_ap(("out", layer, b))[:, cc, :],
                                      start=cc == 0, stop=cc == DC - 1)
                        last.then_inc(job_done, 1)
                    if t:
                        router_transposes(t - 1)
                    if t >= 2:
                        logits(t - 2)
                first = 4 if layer == 0 else 10
                ada1(first)
                router_transposes(TT - 1)
                logits(TT - 2)
                logits(TT - 1).then_inc(logits_done, 1)
                if layer == 0:
                    ada1(5)
                pe.wait_ge(picked, layer + 1)
                pe.wait_ge(rc_in, 16 * (layer + 1))
                both = UV[:, 560:640]
                mm(bank[6][:, 0:TT * E], triu, both, start=True, stop=True)
                mm(bank[6][:, TT * E:2 * TT * E], ones, both, start=True, stop=True).then_inc(pos_done, 1)
                ada1(6 if layer == 0 else 11)
                tile_oh, place_oh = onehots()
                pe.wait_ge(slots_onehot, layer + 1)
                for k in range(2 * TT):
                    last = mm(bank[6][:, 256:256 + NTILE], place_oh[:, k, :], tile_oh[:, k, :], start=k == 0,
                              stop=k == 2 * TT - 1)
                last.then_inc(idx_mm, 1)

            def xt_transposes(b):
                for i in range(DC):
                    last = nc.tensor.transpose(bank[i // 4][:, P * (i % 4):P * (i % 4) + P], XG[:, b, i::DC], ident)
                return last

            def gate_up(b, s):
                w = xslot(s)[:, 0:4096].rearrange("p (k c n) -> p k c n", k=2, c=DC)
                for cc in range(DC):
                    last = mm(bank[2][:, :], XT[:, b, cc, :], w[:, :, cc, :], start=cc == 0, stop=cc == DC - 1)
                return last

            def hid_transposes():
                for i in range(2):
                    last = nc.tensor.transpose(bank[4][:, P * i:P * (i + 1)], hid[:, i::2], ident)
                return last

            def down(s):
                w = xslot(s)[:, 4096:6144].rearrange("p (c n) -> p c n", c=2)
                for half in range(2):
                    for i in range(2):
                        last = mm(bank[5 + half][:, :], hidT[:, i, :], w[:, i, 512 * half:512 * half + 512],
                                  start=i == 0, stop=i == 1)
                return last

            def experts(layer):
                base = E * layer

                def arrivals(n, s, each):
                    return each * ((6 if s == 0 else 5) * layer + n)

                def sums(e, b):
                    pe.wait_ge(hidT_read, base + e + 1)
                    if not (isinstance(e, int) and e == 0):
                        pe.wait_ge(y_act, base + e)
                        pe.wait_ge(y_dve, base + e)
                    down(b).then_inc(down_mm, 1)

                def body(e, b, round_, _):
                    pe.wait_ge(xt_act, base + e + 1)
                    pe.wait_ge(xt_dve, base + e + 1)
                    pe.wait_ge(expert_in[b], arrivals(round_ + 1, b, 48))
                    gate_up(b, b).then_inc(gu_mm, 1)
                    if not (isinstance(e, int) and e == E - 1):
                        nxt = (b + 1) % 3
                        pe.wait_ge(gathered[nxt], arrivals(round_ + (2 if nxt == 0 else 1), nxt, 16))
                        xt_transposes(nxt).then_inc(xt_mm, 1)
                    if not (isinstance(e, int) and e == 0):
                        sums(e - 1, (b - 1) % 3)
                    pe.wait_ge(hid_done, base + e + 1)
                    hid_transposes().then_inc(hidT_mm, 1)

                pe.wait_ge(gathered[0], arrivals(1, 0, 16))
                wait_read(pe, ("r", layer, TT - 1, 1))
                wait_read(pe, ("o", layer, TT - 1, 1))
                pe.wait_ge(ada_read, ADA_N + (7 if layer == 0 else ADA_N))
                xt_transposes(0).then_inc(xt_mm, 1)
                expert_steps(pe, body)
                sums(E - 1, 0)
                o_ = ov[layer]
                n_over = pe.value_load(over_i[0:1, 0:1], min_val=0, max_val=MAXOV)
                with pe.If(n_over > 0):
                    pe.wait_ge(o_["gathered1"], 16)
                    xt_transposes(1).then_inc(o_["xt_mm"], 1)
                with pe.Fori(0, MAXOV // 3) as g:
                    for u in range(3):
                        o, s = 3 * g + u, (u + 1) % 3
                        with pe.If(n_over > o):
                            pe.wait_ge(o_["xt_act"], o + 1)
                            pe.wait_ge(o_["xt_dve"], o + 1)
                            pe.wait_ge(o_[f"in{s}"], 48 * (g + 1))
                            gate_up(s, s).then_inc(o_["gu_mm"], 1)
                            with pe.If(n_over > o + 1):
                                nxt = (s + 1) % 3
                                pe.wait_ge(o_[f"gathered{nxt}"], 16 * (g + (2 if u == 2 else 1)))
                                xt_transposes(nxt).then_inc(o_["xt_mm"], 1)
                            pe.wait_ge(o_["hid"], o + 1)
                            hid_transposes().then_inc(o_["hidT_mm"], 1)
                            pe.wait_ge(o_["hidT_read"], o + 1)
                            pe.wait_ge(o_["y_act"], o + 1)
                            pe.wait_ge(o_["y_dve"], o + 1)
                            down(s).then_inc(o_["down_mm"], 1)
                pe.sem_inc(ring_free, 1)

            norm_transposes()
            for cc in range(DC - 2, DC):
                wait_read(pe, ("t", cc))
            wait_read(pe, ("tc", 0))
            wait_read(pe, ("tc", 1))
            for b in range(4):
                wait_block(pe, ("in", 0, b))
                for t in range(TT):
                    if (b, t) in ((2, 1), (2, 4), (3, 1)):
                        ada_rows(((2, 1), (2, 4), (3, 1)).index((b, t)))
                    project(0, b, t)

            ada_rows(3)
            wait_block(pe, ("dft",))
            wait_block(pe, ("tab",))
            wait_read(pe, ("p", 0, 3, TT - 1))
            tab = blk_ap(("tab",))[:, 0, :].rearrange("p (k n) -> p k n", k=4)
            dftb = blk_ap(("dft",))
            for k, key in enumerate((("fca",), ("fcb",))):
                job_free(pe, key)
                for m in range(4):
                    last = mm(jbank(key)[:, P * m:P * (m + 1)], U[:, 0, P * m:P * (m + 1)], tab[:, k, :], start=True,
                              stop=True)
                last.then_inc(job_done, 1)

            def channels(key, b):
                job_free(pe, key)
                for s in range(2):
                    last = mm(jbank(key)[:, :], tab[:, 2 + s, :], fab[b][:, s, :], start=s == 0, stop=s == 1)
                last.then_inc(job_done, 1)

            for m in range(4):
                for k, name in enumerate(("fa", "fb")):
                    key = (name, m)
                    job_free(pe, key)
                    for i in range(4):
                        last = mm(jbank(key)[:, 0:HALF], U[:, 1 + i, P * m:P * (m + 1)], dftb[:, 4 * k + i, 0:HALF],
                                  start=i == 0, stop=i == 3)
                    last.then_inc(job_done, 1)
                if m == 0:
                    wait_read(pe, ("fca",))
                    wait_read(pe, ("fcb",))
                    channels(("fcy",), 0)
                else:
                    wait_read(pe, ("fa", m - 1))
                    wait_read(pe, ("fb", m - 1))
                    channels(("fy", m - 1), m % 2)
            wait_read(pe, ("fa", 3))
            wait_read(pe, ("fb", 3))
            channels(("fy", 3), 0)

            pe.wait_ge(cache_in, 32)
            transposes(("kct",), [kraw[:, P * g:P * (g + 1)] for g in range(4)])
            pe.wait_ge(qk_normed, TT)
            transposes(("qtc",), [H[:, 0, P * g:P * (g + 1)] for g in range(4)])
            transposes(("ktc",), [H[:, 0, 512 + P * g:512 + P * (g + 1)] for g in range(4)])
            for hp in range(4):
                transposes(("qt", hp), [H[:, t, P * hp:P * (hp + 1)] for t in range(1, TT)])
                transposes(("kt", hp), [H[:, t, 512 + P * hp:512 + P * (hp + 1)] for t in range(1, TT)])
            wait_read(pe, ("qt", 3))
            wait_read(pe, ("kt", 3))
            pe.wait_ge(zm_done, 1)
            pe.wait_ge(v_shifted, 96)

            def scores(u):
                hp, qt, par = UNITS[u]
                key = ("s", u)
                out = jbank(key)
                job_free(pe, key)
                at_ = slice(64 * par, 64 * par + 64)
                q = QT[at_, hp, P * qt:P * (qt + 1)]
                if qt == 0:
                    last = mm(out[:, 0:P], q, KT[at_, hp, 0:P], start=True, stop=True)
                else:
                    k0 = P + KEY_START[qt - 1]
                    mm(out[:, BAND:BAND + P], q, kcT[at_, hp, :], start=True, stop=True)
                    last = mm(out[:, 0:BAND], q, KT[at_, hp, k0:k0 + BAND], start=True, stop=True)
                last.then_inc(job_done, 1)

            def probs_t(u):
                w = 1 if u < NCTX else 3
                pe.wait_ge(p_normed, u + 1)
                transposes(("pt", u), [pb[:, u % (LAG + 1), P * i:P * (i + 1)] for i in range(w)])

            def values(u):
                hp, qt, par = UNITS[u]
                wait_read(pe, ("pt", u))
                cols = slice(64 * (2 * hp + par), 64 * (2 * hp + par) + 64)
                if qt == 0:
                    out, vals = bank[7][64 * par:64 * par + 64, P * hp:P * (hp + 1)], [V[:, 0, cols]]
                else:
                    if u % 8 == 0 and hp >= 2:
                        pe.wait_ge(o_read, hp)
                    out = bank[5 + hp % 2][64 * par:64 * par + 64, P * (qt - 1):P * qt]
                    vals = {1: [V[:, 1, cols], V[:, 2, cols]], 2: [vs[:, 0, cols], vs[:, 1, cols]],
                            3: [vs[:, 1, cols], vs[:, 2, cols]], 4: [V[:, 3, cols], V[:, 4, cols]]}[qt]
                    vals = vals + [vc[:, cols]]
                for i, v in enumerate(vals):
                    last = mm(out, v, ptb[:, u % 3, P * i:P * (i + 1)], start=i == 0, stop=i == len(vals) - 1)
                last.then_inc(pv_done, 1)

            n = len(UNITS)
            for u in range(n + LAG + 2):
                if u < n:
                    scores(u)
                if LAG <= u < n + LAG:
                    probs_t(u - LAG)
                if u > LAG + 1:
                    values(u - LAG - 2)
            pe.wait_ge(o_read, 5)
            out_projection(0)
            experts(0)
            for b in range(7, 10):
                ada1(b)

            pe.wait_ge(ada_read, ADA_N + 10)
            for kind, t in TILE_STEPS:
                if kind == "t":
                    pe.wait_ge(normed, 2 * TT + t + 1)
                    for h in range(2):
                        transposes(("tt", t, h), [H[:, t, 4 * h + i::DC] for i in range(4)])
                else:
                    wait_read(pe, ("tt", t, 0))
                    wait_read(pe, ("tt", t, 1))
                    wait_block(pe, ("in", 1, 2))
                    project(1, 2, t)
            for b in (3, 1, 0):
                wait_block(pe, ("in", 1, b))
                for t in range(TT):
                    project(1, b, t)
            pe.wait_ge(sg_in, 48)
            transposes(("ws",), [ws[:, g, :] for g in range(SG)])
            wait_read(pe, ("ws",))

            def us_transposes(t):
                wait_read(pe, ("sp", t, 1))
                for h in range(2):
                    transposes(("ut", t, h), [U1[:, t, P * (4 * h + i):P * (4 * h + i + 1)] for i in range(4)])

            for t in range(TT):
                pe.wait_ge(v_normed, t + 1)
                for b in range(2):
                    key = ("sp", t, b)
                    job_free(pe, key)
                    for i in range(2):
                        g = 2 * b + i
                        last = mm(jbank(key)[:, 256 * i:256 * i + 256], wst[:, g, :], V1[:, t, 256 * g:256 * g + 256],
                                  start=True, stop=True)
                    last.then_inc(job_done, 1)
                if t:
                    us_transposes(t - 1)
            us_transposes(TT - 1)
            wait_read(pe, ("ut", TT - 1, 1))
            out_projection(1)
            experts(1)


def shape_constants():
    def dft_pair(n):
        a = 2.0 * np.pi * (np.outer(np.arange(n), np.arange(n)) % n) / n
        return np.cos(a), np.sin(a)

    lat = GRID_R * GRID_W
    c_, s_ = dft_pair(lat)
    n = np.arange(lat)
    by_column = n % GRID_R * GRID_W + n // GRID_R
    dft = np.concatenate([m[by_column].reshape(4, P, lat).transpose(1, 0, 2) for m in (c_, s_)], axis=1) / np.sqrt(lat)
    cc, cs = dft_pair(P)
    g_, gs_ = dft_pair(HD)
    pair = np.eye(2)
    dft = dft[:, :, 0:HALF]
    tables = np.concatenate([cc / np.sqrt(P), cs / np.sqrt(P), np.kron(pair, g_) / 8, -np.kron(pair, gs_) / 8], axis=1)
    mask = np.zeros((P, 3, 32, GRID_R))
    for y, tile in enumerate((0, 1, 3)):
        qc = COLS_T * tile + np.arange(P) // GRID_R
        kc = KEY_START[tile] // GRID_R + np.arange(32)
        start = np.clip(qc - 8, 0, GRID_W - 16)
        ok = (kc[None] >= start[:, None]) & (kc[None] < start[:, None] + 16)
        mask[:, y] = np.where(ok, 0.0, NEG)[:, :, None]
    rc = np.zeros((P, RC_N + P))
    rc[:, 0:128] = np.triu(np.ones((P, P)), 1)
    rc[:, 128:256] = 1.0
    rc[:, 256:261] = np.arange(P)[:, None] + P * np.arange(TT)[None]
    rc[:, 261:265] = np.arange(4, 0, -1)
    rc[:, 265:281] = np.arange(E, 0, -1)
    rc[:, 281:297] = P * np.arange(E)
    rc[:, 297:306] = np.arange(MAXOV)
    rc[:, 306:434] = np.arange(P)
    rc[:, 434:RC_N] = P * np.arange(NTILE)
    rc[:, RC_N:] = np.eye(P)
    rows = np.zeros((48, len(PARTS)))
    for i, (k0, k1) in enumerate(PARTS):
        kinds = np.tile(np.repeat(np.arange(k0, k1), 8), 2)
        rows[:len(kinds), i] = np.isin(kinds, SCALES)
    return {"dft": dft, "tables": tables, "mask": mask.reshape(P, -1), "route_consts": rc,
            "scale_rows": rows}


_INS = ["x_prompt", "x_sample", "cache_k", "cache_v", "c", "c_ctx", "ada_w", "ada_b", "norm1_g", "norm2_g", "na_w_in",
        "na_w_out", "q_gain", "k_gain", "rpb", "sg_w_in", "sg_w_out", "sg_v_gain", "sg_w_s", "sg_b_s", "router_w",
        "router_b", "moe_w_gate", "moe_w_up", "moe_w_down"]
_OUTS = [(1, P, D), (1, 512, D), (1, 1, P, HEADS, HD), (1, 1, P, HEADS, HD)]


def kernel(**inputs):
    import concourse.bacc as _bacc
    from concourse.bass_utils import run_bass_kernel_spmd as _run

    nc = _bacc.Bacc("TRN2", target_bir_lowering=False, num_devices=1)
    arrays, args = {}, []
    given = {name: np.ascontiguousarray(inputs[name]) for name in _INS}
    given["rpb"] = np.pad(given["rpb"][0, :, ::-1, ::-1], ((0, 0), (0, 0), (16, 17)))
    for name, a in shape_constants().items():
        given[name] = np.ascontiguousarray(a, dtype=np.float32)
    for name, a in given.items():
        arrays[f"in_{name}"] = a
        args.append(nc.dram_tensor(f"in_{name}", a.shape, F32, kind="ExternalInput").ap())
    for i, shape in enumerate(_OUTS):
        args.append(nc.dram_tensor(f"out_{i}", shape, F32, kind="ExternalOutput").ap())
    build(nc, *args)
    r = _run(nc, [arrays], core_ids=[0])
    return tuple(r.results[0][f"out_{i}"] for i in range(len(_OUTS)))
```
